# Optimizing a Trainium2 kernel written in Bass

```python
import math
import jax, jax.numpy as jnp
from jax import lax
import numpy as np
import jax
import jax.numpy as jnp

D_MODEL = 1024
BATCH = 1
SEQ = 256
DEPTH = 1

EPS = 1e-6
CHUNK = 128
SSD_INNER = D_MODEL
SSD_HEADDIM = 64
SSD_HEADS = SSD_INNER // SSD_HEADDIM
SSD_GROUPS = 2
SSD_STATE = 128
SSD_CONV = 4
SSD_CONV_DIM = SSD_INNER + 2 * SSD_GROUPS * SSD_STATE
LRU_WIDTH = D_MODEL
LRU_BLOCKS = 4
LRU_BLOCK = LRU_WIDTH // LRU_BLOCKS
LRU_CONV = 4
LRU_C = 8.0
RET_HEADS = 4
RET_QK_DIM = D_MODEL // (2 * RET_HEADS)
RET_V_DIM = D_MODEL // RET_HEADS
RET_WIDTH = RET_HEADS * RET_V_DIM
ROPE_BASE = 10000.0
FFN_DIM = 3 * D_MODEL
FFN_CONV = 3
N_BRANCHES = 3
IN_SPLITS = (SSD_INNER, SSD_CONV_DIM, SSD_HEADS, LRU_WIDTH, LRU_WIDTH,
             RET_HEADS * RET_QK_DIM, RET_HEADS * RET_QK_DIM, RET_WIDTH, RET_WIDTH,
             N_BRANCHES * D_MODEL)
IN_PROJ_DIM = sum(IN_SPLITS)


def rmsnorm(x, g):
    x32 = x.astype(jnp.float32)
    y = x32 * lax.rsqrt(jnp.mean(x32 * x32, axis=-1, keepdims=True) + EPS)
    return (y * g.astype(jnp.float32)).astype(x.dtype)

def causal_dwconv(x, w, b):
    k = w.shape[0]
    y = lax.conv_general_dilated(
        x, w[:, None, :].astype(x.dtype), window_strides=(1,), padding=[(k - 1, 0)],
        dimension_numbers=('NWC', 'WIO', 'NWC'), feature_group_count=x.shape[-1])
    return y + b

def ssd_chunked(xdt, a, bm, cm):
    b, s, h, p = xdt.shape
    g, n = bm.shape[-2:]
    r = h // g
    c, L = s // CHUNK, CHUNK
    xdt = xdt.reshape(b, c, L, g, r, p)
    a = a.reshape(b, c, L, g, r)
    bm = bm.reshape(b, c, L, g, n)
    cm = cm.reshape(b, c, L, g, n)
    a_cs = jnp.cumsum(a, axis=2)
    causal = jnp.tril(jnp.ones((L, L), dtype=bool))
    seg = a_cs[:, :, :, None] - a_cs[:, :, None]
    decay = jnp.exp(jnp.where(causal[:, :, None, None], seg, -jnp.inf))
    cb = jnp.einsum('bclgn,bcsgn->bclsg', cm, bm)
    y_diag = jnp.einsum('bclsgr,bcsgrp->bclgrp', cb[..., None] * decay, xdt)
    state_decay = jnp.exp(a_cs[:, :, -1:] - a_cs)
    chunk_states = jnp.einsum('bclgn,bclgr,bclgrp->bcgrpn', bm, state_decay, xdt)
    chunk_decay = jnp.exp(a_cs[:, :, -1])

    def step(state, inp):
        st, dec = inp
        return state * dec[..., None, None] + st, state

    init = jnp.zeros((b, g, r, p, n), dtype=jnp.float32)
    _, s_prev = lax.scan(step, init, (jnp.moveaxis(chunk_states, 1, 0), jnp.moveaxis(chunk_decay, 1, 0)))
    s_prev = jnp.moveaxis(s_prev, 0, 1)
    y_off = jnp.einsum('bclgn,bcgrpn,bclgr->bclgrp', cm, s_prev, jnp.exp(a_cs))
    return (y_diag + y_off).reshape(b, s, h, p)

def ssd_mixer(z, xbc, dt_raw, conv_w, conv_b, dt_bias, a_log, d_skip, norm_w):
    b, s, _ = z.shape
    xbc = jax.nn.silu(causal_dwconv(xbc, conv_w, conv_b))
    xs, bm, cm = jnp.split(xbc, [SSD_INNER, SSD_INNER + SSD_GROUPS * SSD_STATE], axis=-1)
    xs = xs.reshape(b, s, SSD_HEADS, SSD_HEADDIM).astype(jnp.float32)
    bm = bm.reshape(b, s, SSD_GROUPS, SSD_STATE).astype(jnp.float32)
    cm = cm.reshape(b, s, SSD_GROUPS, SSD_STATE).astype(jnp.float32)
    dt = jax.nn.softplus(dt_raw.astype(jnp.float32) + dt_bias.astype(jnp.float32))
    a = -jnp.exp(a_log.astype(jnp.float32))
    y = ssd_chunked(xs * dt[..., None], dt * a, bm, cm)
    y = y + xs * d_skip.astype(jnp.float32)[:, None]
    y = y.reshape(b, s, SSD_INNER) * jax.nn.silu(z.astype(jnp.float32))
    return rmsnorm(y, norm_w).astype(z.dtype)

def _lru_combine(left, right):
    a1, b1 = left
    a2, b2 = right
    return a1 * a2, a2 * b1 + b2

def rglru_mixer(y_gate, xb, conv_w, conv_b, w_a, b_a, w_i, b_i, lam):
    b, s, _ = xb.shape
    xb = causal_dwconv(xb, conv_w, conv_b).astype(jnp.float32)
    xblk = xb.reshape(b, s, LRU_BLOCKS, LRU_BLOCK)
    r = jax.nn.sigmoid(jnp.einsum('bski,kij->bskj', xblk, w_a).reshape(b, s, LRU_WIDTH) + b_a)
    i = jax.nn.sigmoid(jnp.einsum('bski,kij->bskj', xblk, w_i).reshape(b, s, LRU_WIDTH) + b_i)
    log_a = -LRU_C * r * jax.nn.softplus(-lam.astype(jnp.float32))
    a = jnp.exp(log_a)
    u = jnp.sqrt(-jnp.expm1(2.0 * log_a)) * (i * xb)
    _, h = lax.associative_scan(_lru_combine, (a, u), axis=1)
    return (h * jax.nn.gelu(y_gate.astype(jnp.float32))).astype(y_gate.dtype)

def rotary(x):
    s, d = x.shape[1], x.shape[-1]
    inv = 1.0 / (ROPE_BASE ** jnp.linspace(0.0, 1.0, d // 2, dtype=jnp.float32))
    ang = jnp.arange(s, dtype=jnp.float32)[:, None] * inv[None]
    cos = jnp.cos(ang)[None, :, None]
    sin = jnp.sin(ang)[None, :, None]
    x1 = x[..., 0::2]
    x2 = x[..., 1::2]
    return jnp.stack([x1 * cos - x2 * sin, x1 * sin + x2 * cos], axis=-1).reshape(x.shape)

def retention_chunked(q, k, v, log_gamma):
    b, s, h, dk = q.shape
    dv = v.shape[-1]
    c, L = s // CHUNK, CHUNK
    q = q.reshape(b, c, L, h, dk)
    k = k.reshape(b, c, L, h, dk)
    v = v.reshape(b, c, L, h, dv)
    idx = jnp.arange(L, dtype=jnp.float32)
    diff = idx[:, None] - idx[None, :]
    dmask = jnp.where(diff[None] >= 0, jnp.exp(jnp.maximum(diff, 0.0)[None] * log_gamma[:, None, None]), 0.0)
    scores = jnp.einsum('bclhd,bcshd->bchls', q, k) * dmask[None, None]
    inner = jnp.einsum('bchls,bcshe->bclhe', scores, v)
    k_decay = jnp.exp((L - 1.0 - idx)[:, None] * log_gamma[None])
    chunk_kv = jnp.einsum('bclhd,lh,bclhe->bchde', k, k_decay, v)
    chunk_decay = jnp.exp(L * log_gamma)

    def step(state, kv):
        return state * chunk_decay[:, None, None] + kv, state

    init = jnp.zeros((b, h, dk, dv), dtype=jnp.float32)
    _, s_prev = lax.scan(step, init, jnp.moveaxis(chunk_kv, 1, 0))
    s_prev = jnp.moveaxis(s_prev, 0, 1)
    q_decay = jnp.exp((idx + 1.0)[:, None] * log_gamma[None])
    cross = jnp.einsum('bclhd,lh,bchde->bclhe', q, q_decay, s_prev)
    return (inner + cross).reshape(b, s, h, dv)

def retention_mixer(q, k, v, g):
    b, s, _ = q.shape
    qh = rotary(q.reshape(b, s, RET_HEADS, RET_QK_DIM).astype(jnp.float32))
    kh = rotary(k.reshape(b, s, RET_HEADS, RET_QK_DIM).astype(jnp.float32)) * (RET_QK_DIM ** -0.5)
    vh = v.reshape(b, s, RET_HEADS, RET_V_DIM).astype(jnp.float32)
    log_gamma = jnp.log(1.0 - jnp.exp2(-5.0 - jnp.arange(RET_HEADS, dtype=jnp.float32)))
    y = retention_chunked(qh, kh, vh, log_gamma)
    y = y * lax.rsqrt(jnp.mean(y * y, axis=-1, keepdims=True) + EPS)
    y = y.reshape(b, s, RET_WIDTH) * jax.nn.silu(g.astype(jnp.float32))
    return y.astype(q.dtype)

def conv_ffn(h, w_in, conv_w, conv_b, w_out):
    a, u = jnp.split(h @ w_in, 2, axis=-1)
    a = causal_dwconv(a, conv_w, conv_b)
    return (jax.nn.gelu(a) * u) @ w_out

def first_inputs(seed: int = 0) -> dict:
    key = jax.random.key(seed)
    ks = jax.random.split(key, 24)
    f32 = jnp.float32
    nrm = lambda k, shape, scale: scale * jax.random.normal(k, shape, dtype=f32)
    x = jax.random.normal(ks[0], (BATCH, SEQ, D_MODEL), dtype=f32)
    norm_mix = 1.0 + nrm(ks[1], (DEPTH, D_MODEL), 0.02)
    w_in = nrm(ks[2], (DEPTH, D_MODEL, IN_PROJ_DIM), D_MODEL ** -0.5)
    ssd_conv_w = nrm(ks[3], (DEPTH, SSD_CONV, SSD_CONV_DIM), SSD_CONV ** -0.5)
    ssd_conv_b = nrm(ks[4], (DEPTH, SSD_CONV_DIM), 0.02)
    dt0 = jnp.exp(jax.random.uniform(ks[5], (DEPTH, SSD_HEADS), dtype=f32,
                                     minval=math.log(1e-3), maxval=math.log(1e-1)))
    ssd_dt_bias = dt0 + jnp.log(-jnp.expm1(-dt0))
    ssd_a_log = jnp.log(jax.random.uniform(ks[6], (DEPTH, SSD_HEADS), dtype=f32, minval=1.0, maxval=16.0))
    ssd_d = 1.0 + nrm(ks[7], (DEPTH, SSD_HEADS), 0.1)
    ssd_norm = 1.0 + nrm(ks[8], (DEPTH, SSD_INNER), 0.02)
    lru_conv_w = nrm(ks[9], (DEPTH, LRU_CONV, LRU_WIDTH), LRU_CONV ** -0.5)
    lru_conv_b = nrm(ks[10], (DEPTH, LRU_WIDTH), 0.02)
    lru_w_a = nrm(ks[11], (DEPTH, LRU_BLOCKS, LRU_BLOCK, LRU_BLOCK), LRU_BLOCK ** -0.5)
    lru_b_a = nrm(ks[12], (DEPTH, LRU_WIDTH), 0.02)
    lru_w_i = nrm(ks[13], (DEPTH, LRU_BLOCKS, LRU_BLOCK, LRU_BLOCK), LRU_BLOCK ** -0.5)
    lru_b_i = nrm(ks[14], (DEPTH, LRU_WIDTH), 0.02)
    a8 = jax.random.uniform(ks[15], (DEPTH, LRU_WIDTH), dtype=f32, minval=0.9, maxval=0.999)
    a0 = a8 ** (1.0 / LRU_C)
    lru_lambda = jnp.log(a0) - jnp.log1p(-a0)
    w_branch = nrm(ks[16], (DEPTH, N_BRANCHES, D_MODEL, D_MODEL), D_MODEL ** -0.5)
    w_o = nrm(ks[17], (DEPTH, D_MODEL, D_MODEL), D_MODEL ** -0.5)
    norm_ffn = 1.0 + nrm(ks[18], (DEPTH, D_MODEL), 0.02)
    ffn_w_in = nrm(ks[19], (DEPTH, D_MODEL, 2 * FFN_DIM), D_MODEL ** -0.5)
    ffn_conv_w = nrm(ks[20], (DEPTH, FFN_CONV, FFN_DIM), FFN_CONV ** -0.5)
    ffn_conv_b = nrm(ks[21], (DEPTH, FFN_DIM), 0.02)
    ffn_w_out = nrm(ks[22], (DEPTH, FFN_DIM, D_MODEL), FFN_DIM ** -0.5)
    norm_final = 1.0 + nrm(ks[23], (D_MODEL,), 0.02)
    return {'x': x, 'norm_mix': norm_mix, 'w_in': w_in,
            'ssd_conv_w': ssd_conv_w, 'ssd_conv_b': ssd_conv_b, 'ssd_dt_bias': ssd_dt_bias,
            'ssd_a_log': ssd_a_log, 'ssd_d': ssd_d, 'ssd_norm': ssd_norm,
            'lru_conv_w': lru_conv_w, 'lru_conv_b': lru_conv_b, 'lru_w_a': lru_w_a, 'lru_b_a': lru_b_a,
            'lru_w_i': lru_w_i, 'lru_b_i': lru_b_i, 'lru_lambda': lru_lambda,
            'w_branch': w_branch, 'w_o': w_o, 'norm_ffn': norm_ffn,
            'ffn_w_in': ffn_w_in, 'ffn_conv_w': ffn_conv_w, 'ffn_conv_b': ffn_conv_b,
            'ffn_w_out': ffn_w_out, 'norm_final': norm_final}

def first_block(x, norm_mix, w_in, ssd_conv_w, ssd_conv_b, ssd_dt_bias, ssd_a_log, ssd_d, ssd_norm,
              lru_conv_w, lru_conv_b, lru_w_a, lru_b_a, lru_w_i, lru_b_i, lru_lambda,
              w_branch, w_o, norm_ffn, ffn_w_in, ffn_conv_w, ffn_conv_b, ffn_w_out, norm_final):
    b, s, _ = x.shape
    offsets = np.cumsum(IN_SPLITS)[:-1].tolist()
    for l in range(DEPTH):
        h = rmsnorm(x, norm_mix[l])
        proj = h @ w_in[l]
        (z, xbc, dt_raw, lru_y, lru_x, q, k, v, ret_g, gate_pre) = jnp.split(proj, offsets, axis=-1)
        y_ssd = ssd_mixer(z, xbc, dt_raw, ssd_conv_w[l], ssd_conv_b[l], ssd_dt_bias[l],
                          ssd_a_log[l], ssd_d[l], ssd_norm[l])
        y_lru = rglru_mixer(lru_y, lru_x, lru_conv_w[l], lru_conv_b[l], lru_w_a[l], lru_b_a[l],
                            lru_w_i[l], lru_b_i[l], lru_lambda[l])
        y_ret = retention_mixer(q, k, v, ret_g)
        branches = jnp.stack([y_ssd, y_lru, y_ret], axis=2)
        branch_d = jnp.einsum('bskw,kwd->bskd', branches, w_branch[l])
        gates = jax.nn.sigmoid(gate_pre.reshape(b, s, N_BRANCHES, D_MODEL))
        merged = jnp.sum(gates * branch_d, axis=2)
        x = x + merged @ w_o[l]
        h = rmsnorm(x, norm_ffn[l])
        x = x + conv_ffn(h, ffn_w_in[l], ffn_conv_w[l], ffn_conv_b[l], ffn_w_out[l])
    return rmsnorm(x, norm_final)


DEPTH_2 = 2

CTX_LEN = 256
GRID_W = 64
CONV_W = D_MODEL // 4
CONV_K = 31
MLSTM_DH = 64
MLSTM_W = D_MODEL // 4
MLSTM_HEADS = MLSTM_W // MLSTM_DH
MLSTM_CHUNK = 64
DIFF_DH = 64
DIFF_DV = 2 * DIFF_DH
DIFF_W = D_MODEL // 2
DIFF_HEADS = DIFF_W // DIFF_DV
MIX_W = CONV_W + MLSTM_W + DIFF_W
Q_BLOCK = 128
AXIS_ROT = DIFF_DH // 2
IN_SIZES = (2 * CONV_W, MLSTM_W, MLSTM_W, MLSTM_W, MLSTM_W, 4 * MLSTM_HEADS, 2 * DIFF_HEADS * DIFF_DH, 2 * DIFF_HEADS * DIFF_DH, DIFF_W)
IN_W = sum(IN_SIZES)
PEER_HEADS = 8
PEER_DK = 128
N_KEYS = 128
N_EXPERTS = N_KEYS * N_KEYS
PEER_TOPK = 16
TOKEN_BLOCK = 128


def rmsnorm_2(x, g):
    xf = x.astype(jnp.float32)
    y = xf * lax.rsqrt(jnp.mean(xf * xf, axis=-1, keepdims=True) + EPS)
    return (y * g.astype(jnp.float32)).astype(x.dtype)

def layernorm(x, g, b):
    xf = x.astype(jnp.float32)
    mu = jnp.mean(xf, axis=-1, keepdims=True)
    var = jnp.mean(jnp.square(xf - mu), axis=-1, keepdims=True)
    y = (xf - mu) * lax.rsqrt(var + EPS) * g.astype(jnp.float32) + b.astype(jnp.float32)
    return y.astype(x.dtype)

def heads(t, n):
    b, l, w = t.shape
    return t.reshape(b, l, n, w // n).transpose(0, 2, 1, 3)

def merge_heads(t):
    b, n, l, d = t.shape
    return t.transpose(0, 2, 1, 3).reshape(b, l, n * d)

def pair_heads(t):
    b, l, _ = t.shape
    t = t.reshape(b, l, DIFF_HEADS, 2, DIFF_DH)
    return t[:, :, :, 0].transpose(0, 2, 1, 3), t[:, :, :, 1].transpose(0, 2, 1, 3)

def flip_seq(t, rev):
    return jnp.flip(t, axis=2) if rev else t

def axial_rope(n_tokens):
    rows = n_tokens // GRID_W
    row = jnp.repeat(jnp.arange(rows), GRID_W).astype(jnp.float32)
    col = jnp.tile(jnp.arange(GRID_W), rows).astype(jnp.float32)
    inv = ROPE_BASE ** (-jnp.arange(0, AXIS_ROT, 2, dtype=jnp.float32) / AXIS_ROT)
    ang = jnp.concatenate([row[:, None] * inv, col[:, None] * inv], axis=-1)
    return jnp.cos(ang), jnp.sin(ang)

def apply_rope(t, cos, sin):
    tp = t.reshape(t.shape[:-1] + (t.shape[-1] // 2, 2))
    t1, t2 = tp[..., 0], tp[..., 1]
    c = cos.astype(t.dtype)
    s = sin.astype(t.dtype)
    return jnp.stack([t1 * c - t2 * s, t1 * s + t2 * c], axis=-1).reshape(t.shape)

def conv_module(a, conv_w, conv_b, ln_g, ln_b):
    u = a[..., :CONV_W] * jax.nn.sigmoid(a[..., CONV_W:])
    y = lax.conv_general_dilated(u, conv_w.astype(u.dtype), window_strides=(1,),
                                 padding=[(CONV_K // 2, CONV_K // 2)],
                                 dimension_numbers=("NWC", "WIO", "NWC"),
                                 feature_group_count=CONV_W) + conv_b
    return jax.nn.silu(layernorm(y, ln_g, ln_b))

def mlstm_chunk_scan(q, k, v, ig, lf, state):
    bsz, nh, seq, dh = q.shape
    nc = seq // MLSTM_CHUNK

    def chunks(t):
        t = t.reshape(t.shape[:2] + (nc, MLSTM_CHUNK) + t.shape[3:])
        return jnp.moveaxis(t, 2, 0)

    xs = tuple(chunks(t) for t in (q, k, v, ig, lf))
    tril = jnp.tril(jnp.ones((MLSTM_CHUNK, MLSTM_CHUNK), dtype=bool))

    def step(carry, inp):
        C, n, m = carry
        qc, kc, vc, ic, fc = inp
        qf, kf, vf = qc.astype(jnp.float32), kc.astype(jnp.float32), vc.astype(jnp.float32)
        b = jnp.cumsum(fc, axis=-1)
        dlog = jnp.where(tril, b[..., :, None] - b[..., None, :] + ic[..., None, :], -jnp.inf)
        inter = b + m[..., None]
        mt = jnp.maximum(inter, jnp.max(dlog, axis=-1))
        dw = jnp.exp(dlog - mt[..., None])
        iw = jnp.exp(inter - mt)
        s = jnp.einsum("bhtd,bhsd->bhts", qf, kf) * dw
        num = jnp.einsum("bhts,bhse->bhte", s, vf) + iw[..., None] * jnp.einsum("bhed,bhtd->bhte", C, qf)
        den = jnp.sum(s, axis=-1) + iw * jnp.einsum("bhd,bhtd->bht", n, qf)
        h = num / jnp.maximum(jnp.abs(den), jnp.exp(-mt))[..., None]
        bl = b[..., -1]
        wlog = bl[..., None] - b + ic
        mn = jnp.maximum(bl + m, jnp.max(wlog, axis=-1))
        wk = jnp.exp(wlog - mn[..., None])
        decay = jnp.exp(bl + m - mn)
        C = decay[..., None, None] * C + jnp.einsum("bhs,bhse,bhsd->bhed", wk, vf, kf)
        n = decay[..., None] * n + jnp.einsum("bhs,bhsd->bhd", wk, kf)
        return (C, n, mn), h

    state, hs = lax.scan(step, state, xs)
    h = jnp.moveaxis(hs, 0, 2).reshape(bsz, nh, seq, dh)
    return h, state

def mlstm_mixer(lat, ctx, gate_b, norm_g, need_ctx):
    gb = gate_b.reshape(-1).astype(jnp.float32)

    def prep(q, k, v, g):
        b, l, _ = q.shape
        g = (g.astype(jnp.float32) + gb).reshape(b, l, 4, MLSTM_HEADS).transpose(2, 0, 3, 1)
        return heads(q, MLSTM_HEADS), heads(k, MLSTM_HEADS) * (MLSTM_DH ** -0.5), heads(v, MLSTM_HEADS), g

    ql, kl, vl, gl = prep(lat[0], lat[1], lat[2], lat[4])
    qc, kc, vc, gc = prep(ctx[0], ctx[1], ctx[2], ctx[4])
    bsz = ql.shape[0]
    outs_l, outs_c = [], []
    for d, rev in enumerate((False, True)):
        state = (jnp.zeros((bsz, MLSTM_HEADS, MLSTM_DH, MLSTM_DH), jnp.float32),
                 jnp.zeros((bsz, MLSTM_HEADS, MLSTM_DH), jnp.float32),
                 jnp.zeros((bsz, MLSTM_HEADS), jnp.float32))
        hc, state = mlstm_chunk_scan(*[flip_seq(t, rev) for t in (qc, kc, vc, gc[2 * d], jax.nn.log_sigmoid(gc[2 * d + 1]))], state)
        hl, _ = mlstm_chunk_scan(*[flip_seq(t, rev) for t in (ql, kl, vl, gl[2 * d], jax.nn.log_sigmoid(gl[2 * d + 1]))], state)
        outs_c.append(flip_seq(hc, rev))
        outs_l.append(flip_seq(hl, rev))

    def finish(h, o):
        h = merge_heads(rmsnorm_2(h, norm_g))
        return (h * jax.nn.sigmoid(o.astype(jnp.float32))).astype(o.dtype)

    y_lat = finish(outs_l[0] + outs_l[1], lat[3])
    y_ctx = finish(outs_c[0] + outs_c[1], ctx[3]) if need_ctx else None
    return y_lat, y_ctx

def diff_attention(q1, q2, k1, k2, v, lam):
    bsz, nh, lq, dh = q1.shape
    nb = lq // Q_BLOCK
    scale = dh ** -0.5

    def blocks(t):
        return jnp.moveaxis(t.reshape(bsz, nh, nb, Q_BLOCK, dh), 2, 0)

    def one(args):
        a1, a2 = args
        p1 = jax.nn.softmax(jnp.einsum("bhqd,bhkd->bhqk", a1, k1).astype(jnp.float32) * scale, axis=-1)
        p2 = jax.nn.softmax(jnp.einsum("bhqd,bhkd->bhqk", a2, k2).astype(jnp.float32) * scale, axis=-1)
        p = p1 - lam * p2
        return jnp.einsum("bhqk,bhkd->bhqd", p.astype(v.dtype), v)

    o = lax.map(one, (blocks(q1), blocks(q2)))
    return jnp.moveaxis(o, 0, 2).reshape(bsz, nh, lq, v.shape[-1])

def diff_mixer(lat, ctx, lam_params, lam_init, norm_g, cos, sin, need_ctx):
    dql, dkl, dvl = lat
    dqc, dkc, dvc = ctx
    lp = lam_params.astype(jnp.float32)
    lam = jnp.exp(jnp.sum(lp[0] * lp[1])) - jnp.exp(jnp.sum(lp[2] * lp[3])) + lam_init
    ql1, ql2 = (apply_rope(t, cos, sin) for t in pair_heads(dql))
    kl1, kl2 = (apply_rope(t, cos, sin) for t in pair_heads(dkl))
    qc1, qc2 = pair_heads(dqc)
    kc1, kc2 = pair_heads(dkc)
    vl = heads(dvl, DIFF_HEADS)
    vc = heads(dvc, DIFF_HEADS)
    k1 = jnp.concatenate([kc1, kl1], axis=2)
    k2 = jnp.concatenate([kc2, kl2], axis=2)
    v = jnp.concatenate([vc, vl], axis=2)

    def finish(o):
        return merge_heads(rmsnorm_2(o, norm_g) * (1.0 - lam_init))

    y_lat = finish(diff_attention(ql1, ql2, k1, k2, v, lam))
    y_ctx = finish(diff_attention(qc1, qc2, kc1, kc2, vc, lam)) if need_ctx else None
    return y_lat, y_ctx

def peer_ffn(h, wq, sub_keys, eu, ev):
    bsz, seq, dm = h.shape
    nb = (bsz * seq) // TOKEN_BLOCK
    hb = h.reshape(nb, TOKEN_BLOCK, dm)

    def one(t):
        q = (t @ wq).reshape(TOKEN_BLOCK, PEER_HEADS, 2, PEER_DK // 2)
        s = jnp.einsum("thpd,hpnd->thpn", q, sub_keys).astype(jnp.float32)
        st, it = lax.top_k(s, PEER_TOPK)
        cand = (st[:, :, 0, :, None] + st[:, :, 1, None, :]).reshape(TOKEN_BLOCK, PEER_HEADS, PEER_TOPK * PEER_TOPK)
        cidx = (it[:, :, 0, :, None] * N_KEYS + it[:, :, 1, None, :]).reshape(TOKEN_BLOCK, PEER_HEADS, PEER_TOPK * PEER_TOPK)
        best, pos = lax.top_k(cand, PEER_TOPK)
        e = jnp.take_along_axis(cidx, pos, axis=-1)
        g = jax.nn.softmax(best, axis=-1)
        u = jnp.take(eu, e, axis=0)
        act = jax.nn.gelu(jnp.einsum("thkd,td->thk", u, t).astype(jnp.float32), approximate=False)
        return jnp.einsum("thk,thkd->td", (g * act).astype(ev.dtype), jnp.take(ev, e, axis=0))

    return lax.map(one, hb).reshape(bsz, seq, dm)

def trunk_layer(x, xc, mod, modc, lam_init, cos, sin, need_ctx,
                norm1_g, norm2_g, w_in, conv_w, conv_b, conv_ln_g, conv_ln_b,
                mlstm_gate_b, mlstm_norm_g, diff_lambda, diff_norm_g, w_out,
                peer_wq, peer_keys, peer_u, peer_v):
    sh1, sc1, g1, sh2, sc2, g2 = [m[:, None, :] for m in jnp.split(mod, 6, axis=-1)]
    sh1c, sc1c, g1c, sh2c, sc2c, g2c = jnp.split(modc, 6, axis=-1)
    splits = np.cumsum(IN_SIZES)[:-1].tolist()
    h = rmsnorm_2(x, norm1_g) * (1.0 + sc1) + sh1
    hc = rmsnorm_2(xc, norm1_g) * (1.0 + sc1c) + sh1c
    a, mq, mk, mv, mo, mg, dq, dk, dv = jnp.split(h @ w_in, splits, axis=-1)
    ac, mqc, mkc, mvc, moc, mgc, dqc, dkc, dvc = jnp.split(hc @ w_in, splits, axis=-1)
    conv_l = conv_module(a, conv_w, conv_b, conv_ln_g, conv_ln_b)
    mlstm_l, mlstm_c = mlstm_mixer((mq, mk, mv, mo, mg), (mqc, mkc, mvc, moc, mgc), mlstm_gate_b, mlstm_norm_g, need_ctx)
    diff_l, diff_c = diff_mixer((dq, dk, dv), (dqc, dkc, dvc), diff_lambda, lam_init, diff_norm_g, cos, sin, need_ctx)
    mix = jnp.concatenate([conv_l.astype(x.dtype), mlstm_l.astype(x.dtype), diff_l.astype(x.dtype)], axis=-1)
    x = x + g1 * (mix @ w_out)
    h2 = rmsnorm_2(x, norm2_g) * (1.0 + sc2) + sh2
    x = x + g2 * peer_ffn(h2, peer_wq, peer_keys, peer_u, peer_v)
    if need_ctx:
        conv_c = conv_module(ac, conv_w, conv_b, conv_ln_g, conv_ln_b)
        mix_c = jnp.concatenate([conv_c.astype(xc.dtype), mlstm_c.astype(xc.dtype), diff_c.astype(xc.dtype)], axis=-1)
        xc = xc + g1c * (mix_c @ w_out)
        h2c = rmsnorm_2(xc, norm2_g) * (1.0 + sc2c) + sh2c
        xc = xc + g2c * peer_ffn(h2c, peer_wq, peer_keys, peer_u, peer_v)
    return x, xc

def second_inputs(seed: int = 0) -> dict:
    key = jax.random.key(seed)
    ks = jax.random.split(key, 24)
    f32 = jnp.float32

    def nrm(k, shape, scale):
        return jax.random.normal(k, shape, f32) * scale

    gate_offset = jnp.array([0.0, 3.0, 0.0, 3.0], f32)[None, :, None]
    return {
        "x": nrm(ks[0], (BATCH, SEQ, D_MODEL), 1.0),
        "c": nrm(ks[1], (BATCH, D_MODEL), 1.0),
        "ctx": nrm(ks[2], (BATCH, CTX_LEN, D_MODEL), 1.0),
        "c_ctx": nrm(ks[3], (D_MODEL,), 1.0),
        "ada_w": nrm(ks[4], (DEPTH_2, D_MODEL, 6 * D_MODEL), 0.5 * D_MODEL ** -0.5),
        "ada_b": nrm(ks[5], (DEPTH_2, 6 * D_MODEL), 0.02),
        "norm1_g": 1.0 + nrm(ks[6], (DEPTH_2, D_MODEL), 0.02),
        "norm2_g": 1.0 + nrm(ks[7], (DEPTH_2, D_MODEL), 0.02),
        "w_in": nrm(ks[8], (DEPTH_2, D_MODEL, IN_W), D_MODEL ** -0.5),
        "conv_w": nrm(ks[9], (DEPTH_2, CONV_K, 1, CONV_W), CONV_K ** -0.5),
        "conv_b": nrm(ks[10], (DEPTH_2, CONV_W), 0.02),
        "conv_ln_g": 1.0 + nrm(ks[11], (DEPTH_2, CONV_W), 0.02),
        "conv_ln_b": nrm(ks[12], (DEPTH_2, CONV_W), 0.02),
        "mlstm_gate_b": gate_offset + nrm(ks[13], (DEPTH_2, 4, MLSTM_HEADS), 0.5),
        "mlstm_norm_g": 1.0 + nrm(ks[14], (DEPTH_2, MLSTM_DH), 0.02),
        "diff_lambda": nrm(ks[15], (DEPTH_2, 4, DIFF_DH), 0.1),
        "diff_norm_g": 1.0 + nrm(ks[16], (DEPTH_2, DIFF_DV), 0.02),
        "w_out": nrm(ks[17], (DEPTH_2, MIX_W, D_MODEL), MIX_W ** -0.5),
        "peer_wq": nrm(ks[18], (DEPTH_2, D_MODEL, PEER_HEADS * PEER_DK), D_MODEL ** -0.5),
        "peer_keys": nrm(ks[19], (DEPTH_2, PEER_HEADS, 2, N_KEYS, PEER_DK // 2), (PEER_DK // 2) ** -0.5),
        "peer_u": nrm(ks[20], (DEPTH_2, N_EXPERTS, D_MODEL), D_MODEL ** -0.5),
        "peer_v": nrm(ks[21], (DEPTH_2, N_EXPERTS, D_MODEL), PEER_HEADS ** -0.5),
        "final_g": 1.0 + nrm(ks[22], (D_MODEL,), 0.02),
    }

def second_block(x, c, ctx, c_ctx, ada_w, ada_b, norm1_g, norm2_g, w_in, conv_w, conv_b,
              conv_ln_g, conv_ln_b, mlstm_gate_b, mlstm_norm_g, diff_lambda, diff_norm_g,
              w_out, peer_wq, peer_keys, peer_u, peer_v, final_g):
    cos, sin = axial_rope(x.shape[1])
    sc = jax.nn.silu(c)
    scc = jax.nn.silu(c_ctx)
    xc = ctx
    for l in range(DEPTH_2):
        mod = sc @ ada_w[l] + ada_b[l]
        modc = scc @ ada_w[l] + ada_b[l]
        lam_init = 0.8 - 0.6 * math.exp(-0.3 * l)
        x, xc = trunk_layer(x, xc, mod, modc, lam_init, cos, sin, l < DEPTH_2 - 1,
                            norm1_g[l], norm2_g[l], w_in[l], conv_w[l], conv_b[l],
                            conv_ln_g[l], conv_ln_b[l], mlstm_gate_b[l], mlstm_norm_g[l],
                            diff_lambda[l], diff_norm_g[l], w_out[l], peer_wq[l],
                            peer_keys[l], peer_u[l], peer_v[l])
    return rmsnorm_2(x, final_g)


def setup_inputs(seed=0):
    out = dict(first_inputs(seed))
    for name, value in second_inputs(seed + 1).items():
        if name != "x":
            out[name + "_2"] = value
    return out


def reference(
    x, norm_mix, w_in, ssd_conv_w, ssd_conv_b, ssd_dt_bias, ssd_a_log, ssd_d, ssd_norm,
    lru_conv_w, lru_conv_b, lru_w_a, lru_b_a, lru_w_i, lru_b_i, lru_lambda, w_branch, w_o,
    norm_ffn, ffn_w_in, ffn_conv_w, ffn_conv_b, ffn_w_out, norm_final, c_2, ctx_2, c_ctx_2,
    ada_w_2, ada_b_2, norm1_g_2, norm2_g_2, w_in_2, conv_w_2, conv_b_2, conv_ln_g_2,
    conv_ln_b_2, mlstm_gate_b_2, mlstm_norm_g_2, diff_lambda_2, diff_norm_g_2, w_out_2,
    peer_wq_2, peer_keys_2, peer_u_2, peer_v_2, final_g_2,
):
    x = first_block(
        x, norm_mix, w_in, ssd_conv_w, ssd_conv_b, ssd_dt_bias, ssd_a_log, ssd_d, ssd_norm,
        lru_conv_w, lru_conv_b, lru_w_a, lru_b_a, lru_w_i, lru_b_i, lru_lambda, w_branch, w_o,
        norm_ffn, ffn_w_in, ffn_conv_w, ffn_conv_b, ffn_w_out, norm_final,
    )
    return second_block(
        x, c_2, ctx_2, c_ctx_2, ada_w_2, ada_b_2, norm1_g_2, norm2_g_2, w_in_2, conv_w_2,
        conv_b_2, conv_ln_g_2, conv_ln_b_2, mlstm_gate_b_2, mlstm_norm_g_2, diff_lambda_2,
        diff_norm_g_2, w_out_2, peer_wq_2, peer_keys_2, peer_u_2, peer_v_2, final_g_2,
    )


_drawn_inputs = setup_inputs


def setup_inputs(seed=0):
    import zlib

    import numpy as np

    out = dict(_drawn_inputs(seed))
    spreads = {}
    factors = {'ssd_conv_b': 3.247,
     'ssd_norm': 4.365,
     'lru_b_a': 8.0,
     'lru_b_i': 8.0,
     'norm_ffn': 3.254,
     'ffn_conv_b': 4.229,
     'norm1_g_2': 5.349,
     'norm2_g_2': 4.538,
     'conv_b_2': 7.593,
     'conv_ln_g_2': 8.0,
     'conv_ln_b_2': 8.0,
     'mlstm_norm_g_2': 8.0,
     'diff_norm_g_2': 7.104,
     'final_g_2': 2.966}
    for name, (base, spread) in spreads.items():
        noise = np.random.default_rng([zlib.crc32(name.encode()), seed]).standard_normal(out[name].shape)
        drawn = base * np.exp(spread * noise) if base else spread * noise
        out[name] = jnp.asarray(drawn.astype(out[name].dtype))
    for name, factor in factors.items():
        out[name] = (out[name] * factor).astype(out[name].dtype)
    return out
```

```python
import math
from contextlib import ExitStack

import numpy as np

import concourse.bass as bass
from concourse import mybir

F32 = mybir.dt.float32
U32 = mybir.dt.uint32
ALU = mybir.AluOpType
ACT = mybir.ActivationFunctionType
AX = mybir.AxisListType

P = 128
D = 1024
KT = D // P
T = 256
TT = T // P
EPS = 1e-6
NS = 4
SLOT = D

FFN_T = 3 * D // P
SSD_H, SSD_P = 16, 64
RET_H = 4
LRU_O = 8
ML_H, ML_D = 4, 64
DF_H = 4
CONV_K = 31
PEER_H, TOPK, NK = 8, 16, 128
LAYERS = 2


def small_columns():
    cols = {}
    at = 0

    def add(name, n):
        nonlocal at
        cols[name] = (at, n)
        at += n

    for name, n in (("norm_mix", 8), ("ssd_conv_w", 48), ("ssd_conv_b", 12), ("ssd_norm", 8), ("ssd_d", 8),
                    ("lru_conv_w", 32), ("lru_conv_b", 8), ("lru_b_a", 8), ("lru_b_i", 8), ("lru_lambda", 8),
                    ("norm_ffn", 8), ("ffn_conv_w", 72), ("ffn_conv_b", 24), ("norm_final", 8), ("final_g", 8),
                    ("cond", 16), ("dt_bias", 1), ("a_log", 1), ("w_dt", 8 * SSD_H)):
        add(name, n)
    for l in range(LAYERS):
        for name, n in (("ada_b", 48), ("norm1", 8), ("norm2", 8), ("conv_w", 2 * CONV_K), ("conv_b", 2),
                        ("ln_g", 2), ("ln_b", 2), ("gate_b", 1), ("ml_norm", 1), ("df_norm", 1), ("lam", 256)):
            add(f"{name}{l}", n)
    return cols, at


SMALL, N_SMALL = small_columns()


def const_columns():
    cols = {}
    at = 0
    for name, n in (("ident", P), ("iota", P), ("rot", P), ("causal", 384), ("anti", P), ("selm", ML_H * P),
                    ("iota16", 16)):
        cols[name] = (at, n)
        at += n
    return cols, at


CONST, N_CONST = const_columns()
TABLE = {"sel": (0, SSD_H * P), "ret_cos": (2048, T), "ret_sin": (2304, T), "retk_cos": (2560, T),
         "retk_sin": (2816, T), "ret_mask": (3072, RET_H * 384)}
N_TABLE = 3072 + RET_H * 384


def shape_tables():
    f = np.float32
    c = np.zeros((P, N_CONST), f)
    t = np.zeros((P, N_TABLE), f)

    def put(a, cols, name, v):
        o, n = cols[name]
        a[:v.shape[0], o:o + n] = v.reshape(v.shape[0], n)

    i = np.arange(P)
    put(c, CONST, "ident", np.eye(P, dtype=f))
    put(c, CONST, "iota", np.tile(i.astype(f), (P, 1)))
    rot = np.zeros((P, P), f)
    rot[i[1::2], i[0::2]] = -1.0
    rot[i[0::2], i[1::2]] = 1.0
    put(c, CONST, "rot", rot)
    tri = (i[None, :] >= i[:, None]).astype(f)
    put(c, CONST, "causal", np.concatenate([tri, np.ones((P, P), f), tri], 1))
    put(c, CONST, "anti", (i[None, :] <= i[:, None]).astype(f))
    selm = np.zeros((36, ML_H, P), f)
    for r in range(ML_H):
        selm[r, r] = 1.0
        selm[32 + r, r] = 1.0
    put(c, CONST, "selm", selm)
    put(c, CONST, "iota16", np.tile(np.arange(16, dtype=f), (P, 1)))

    sel = np.zeros((SSD_H, SSD_H, P), f)
    for h in range(SSD_H):
        sel[h, h] = 1.0
    put(t, TABLE, "sel", sel)
    inv = (f(1.0) / (f(10000.0) ** np.linspace(0.0, 1.0, 64, dtype=f))).astype(f)
    ang = (np.arange(T, dtype=f)[:, None] * inv[None]).astype(f).T
    cos, sin = np.repeat(np.cos(ang), 2, 0), np.repeat(np.sin(ang), 2, 0)
    k_scale = f(P ** -0.5)
    put(t, TABLE, "ret_cos", cos)
    put(t, TABLE, "ret_sin", sin)
    put(t, TABLE, "retk_cos", cos * k_scale)
    put(t, TABLE, "retk_sin", sin * k_scale)
    gamma = np.log(1.0 - np.exp2(-5.0 - np.arange(RET_H)))
    s, l = i[:, None], np.arange(T)[None]
    full = np.stack([np.where(l >= s, np.exp(np.maximum(l - s, 0) * g), 0.0) for g in gamma], 1)
    put(t, TABLE, "ret_mask", np.concatenate([full, full[:, :, :P]], 2).astype(f))

    n = np.arange(T)
    inv = (10000.0 ** (-np.arange(0, 32, 2, dtype=f) / f(32))).astype(f)
    ang = np.concatenate([(n // 64).astype(f)[:, None] * inv, (n % 64).astype(f)[:, None] * inv], -1).T
    rope = np.stack([np.tile(np.repeat(np.cos(ang), 2, 0), (2, 1)), np.tile(np.repeat(np.sin(ang), 2, 0), (2, 1))], 1)
    return {"consts": c, "tables": t, "axial": rope.astype(f).reshape(P, 2 * T)}


class Space:

    def __init__(self, tensor, size):
        self.tensor, self.size, self.at = tensor, size, 0

    def take(self, *shape):
        n = int(np.prod(shape))
        assert self.at + n <= self.size, (self.at, n, self.size)
        ap = self.tensor[:, self.at:self.at + n]
        self.at += n
        if len(shape) == 2:
            return ap.rearrange("p (a b) -> p a b", b=shape[1])
        if len(shape) == 3:
            return ap.rearrange("p (a b c) -> p a b c", b=shape[1], c=shape[2])
        return ap


def linker(eng, sem):
    n = [0]

    def link(ins):
        n[0] += 1
        ins.then_inc(sem, 1)
        eng.wait_ge(sem, n[0])

    return link


def build(nc, x, smalls, consts, tables, axial, w_in1, w_lru, w_br, w_o1, w_f1, w_f2, ada, w_in2,
          w_out2, w_q2, keys2, uv, out):
    ctx = ExitStack()
    with ctx:
        def sb(name, shape):
            return ctx.enter_context(nc.sbuf_tensor(name, shape, F32))

        ring = sb("ring", [P, NS, SLOT])
        X = sb("X", [P, KT, 2, T])
        H = sb("H", [P, KT, 2, T])
        CS = sb("CS", [P, N_CONST])
        SM = sb("SM", [P, N_SMALL])
        ones = sb("ones", [P, P])
        n_arena = 38000
        arena = sb("arena", [P, n_arena])
        bank = [ctx.enter_context(nc.psum_tensor(f"bank{i}", [P, 512], F32)) for i in range(8)]
        w_ready = [ctx.enter_context(nc.semaphore(f"w_ready{i}")) for i in range(NS)]
        blocks_done = ctx.enter_context(nc.semaphore("blocks_done"))

        def cc(name):
            o, n = CONST[name]
            return CS[:, o:o + n]

        def sm(name):
            o, n = SMALL[name]
            return SM[:, o:o + n]

        ident = cc("ident")

        order = []
        order += [(w_in1, i) for i in range(84)]
        order += [(w_lru, i) for i in range(4)]
        order += [(w_br, i) for i in range(24)]
        order += [(w_o1, i) for i in range(8)]
        order += [(w_f1, i) for i in range(48)]
        order += [(w_f2, i) for i in range(24)]
        for l in range(LAYERS):
            order += [(ada[l], i) for i in range(48)]
            order += [(w_in2[l], i) for i in range(25)]
            order += [(w_out2[l], i) for i in range(8)]
            order += [(w_q2[l], i) for i in range(8)]
            for _ in range(2 if l == 0 else 1):
                order += [(uv[l], i) for i in range(2 * NK)]
        issued = [0]
        used = [0]

        def stream(sp, count):
            end = min(used[0] + count + NS, len(order))
            n = issued[0]
            while n < end:
                w, i = order[n]
                run = 1
                while n + run < end and order[n + run][0] is w and order[n + run][1] == i + run:
                    run += 1
                if n >= NS and run >= 4 * NS:
                    times = run // NS
                    with sp.Fori(0, times) as it:
                        for u in range(NS):
                            sp.wait_ge(blocks_done, it * NS + (n + u - NS + 1))
                            sp.dma_start(ring[:, (n + u) % NS, :], w[it * NS + (i + u)]).then_inc(w_ready[(n + u) % NS], 16)
                    n += times * NS
                else:
                    if n >= NS:
                        sp.wait_ge(blocks_done, n - NS + 1)
                    sp.dma_start(ring[:, n % NS, :], w[i]).then_inc(w_ready[n % NS], 16)
                    n += 1
            issued[0] = n

        def arrived(pe, n, it=None):
            value = 16 * (n // NS + 1)
            pe.wait_ge(w_ready[n % NS], value if it is None else it * 16 + value)

        def col(n, kt, width=P):
            return ring[:, n % NS, kt * width:(kt + 1) * width]

        def product(pe, n, out_ap, rhs, it=None):
            arrived(pe, n, it)
            for kt in range(KT):
                mm = pe.matmul(out_ap, col(n, kt), rhs(kt), start=(kt == 0), stop=(kt == KT - 1))
            mm.then_inc(blocks_done, 1)

        class Phase:

            def __init__(self, *names):
                self.names = names

            def __enter__(self):
                self.sems = [nc.alloc_semaphore(n) for n in self.names]
                self.block = nc.Block()
                return (self.block.__enter__(), *self.sems)

            def __exit__(self, *e):
                self.block.__exit__(*e)
                for s in self.sems:
                    nc.gpsimd.sem_clear(s)
                    nc.release_semaphore(s)

        def evac_wait(pe, sems, evac, b, lag):
            if b >= lag:
                who = evac[b - lag]
                pe.wait_ge(sems[who], evac[:b - lag + 1].count(who))

        def rms_phase(jobs, count=0):
            with Phase("squares", "sums", "inverse", "roots", "v_chain", "normed") as (
                    block, squares, sums, inverse, roots, v_chain, normed):
                mark = A.at
                sq = A.take(2, KT, T)
                rs = A.take(2, T)

                @block.sync
                def _(sp):
                    stream(sp, count)

                @block.scalar
                def _(act):
                    for j, (src, dst, gain, shift) in enumerate(jobs):
                        if j >= 2:
                            act.wait_ge(sums, j - 1)
                        for kt in range(KT):
                            act.activation(sq[:, j % 2, kt, :], src(kt), ACT.Square).then_inc(squares, 1)
                    for j in range(len(jobs)):
                        act.wait_ge(inverse, j + 1)
                        act.activation(rs[:, j % 2, :], rs[:, j % 2, :], ACT.Sqrt).then_inc(roots, 1)

                @block.tensor
                def _(pe):
                    for j in range(len(jobs)):
                        for kt in range(KT):
                            pe.wait_ge(squares, KT * j + kt + 1)
                            mm = pe.matmul(bank[j % 4][:, 0:T], ones[:, :], sq[:, j % 2, kt, :],
                                           start=(kt == 0), stop=(kt == KT - 1))
                        mm.then_inc(sums, 1)

                @block.vector
                def _(dve):
                    link = linker(dve, v_chain)
                    for j, (src, dst, gain, shift) in enumerate(jobs):
                        dve.wait_ge(sums, j + 1)
                        link(dve.tensor_scalar(rs[:, j % 2, :], bank[j % 4][:, 0:T], 1.0 / D, EPS, ALU.mult, ALU.add))
                        dve.reciprocal(rs[:, j % 2, :], rs[:, j % 2, :]).then_inc(inverse, 1)
                        dve.wait_ge(roots, j + 1)
                        for kt in range(KT):
                            dve.scalar_tensor_tensor(dst(kt), src(kt), gain(kt), rs[:, j % 2, :],
                                                     ALU.mult, ALU.mult).then_inc(normed, 1)
                        if shift is not None:
                            dve.wait_ge(normed, KT * (j + 1))
                            for kt in range(KT):
                                dve.tensor_scalar(dst(kt), dst(kt), shift(kt), None, ALU.add)
                A.at = mark

        A = Space(arena, n_arena)

        with Phase("loaded") as (block, loaded):
            @block.sync
            def _(sp):
                sp.dma_start(CS[:, :], consts).then_inc(loaded, 16)
                sp.dma_start(SM[:, :], smalls).then_inc(loaded, 16)
                sp.dma_start(X[:, :, :, :], x).then_inc(loaded, 16)
                stream(sp, 0)
                sp.wait_ge(loaded, 48)

            @block.vector
            def _(dve):
                dve.memset(ones[:, :], 1.0)

        def xl(kt):
            return X[:, kt, 1, :]

        def hl(kt):
            return H[:, kt, 1, :]

        def column(name, first=0):
            return lambda kt: sm(name)[:, first + kt:first + kt + 1]

        rms_phase([(xl, hl, column("norm_mix"), None)])

        TB = A.take(N_TABLE)

        def table(name):
            o, n = TABLE[name]
            return TB[:, o:o + n]

        xbc = A.take(12, T)
        xl_conv = A.take(8, T)
        q_ret = A.take(RET_H, T)
        k_ret = A.take(RET_H, T)
        v_ret = A.take(8, T)
        z_gate = A.take(8, T)
        y_gate = A.take(8, T)
        g_gate = A.take(8, T)
        gates = A.take(24, T)
        dtT = A.take(T)[0:SSD_H]
        acsT = A.take(T)[0:SSD_H]
        negA = A.take(1)[0:SSD_H]
        one_row = A.take(T)[0:SSD_H]
        mixer_mark = A.at

        kinds = [("conv", xbc, i) for i in range(12)] + [("conv", xl_conv, i) for i in range(8)]
        kinds += [(ACT.Copy, q_ret, i) for i in range(4)] + [(ACT.Copy, k_ret, i) for i in range(4)]
        kinds += [(ACT.Copy, v_ret, i) for i in range(8)] + [(ACT.Silu, z_gate, i) for i in range(8)]
        kinds += [(ACT.Silu, g_gate, i) for i in range(8)]
        kinds += [(ACT.Gelu_apprx_tanh, y_gate, i) for i in range(8)]
        kinds += [(ACT.Sigmoid, gates, i) for i in range(24)]
        evac = ["dve" if k[0] == "conv" else "act" for k in kinds]
        n0 = used[0]
        with Phase("tables_in", "by_act", "by_dve", "dt_sum", "a_chain", "v_chain", "dt_soft", "dt_read") as (
                block, tables_in, by_act, by_dve, dt_sum, a_chain, v_chain, dt_soft, dt_read):
            sems = {"act": by_act, "dve": by_dve}

            @block.sync
            def _(sp):
                sp.dma_start(TB, tables).then_inc(tables_in, 16)
                stream(sp, 84)
                sp.wait_ge(tables_in, 16)

            @block.tensor
            def _(pe):
                for kt in range(KT):
                    mm = pe.matmul(bank[4][0:SSD_H, 0:T], sm("w_dt")[:, kt * SSD_H:(kt + 1) * SSD_H], hl(kt),
                                   start=(kt == 0), stop=(kt == KT - 1))
                mm.then_inc(dt_sum, 1)
                for b in range(84):
                    evac_wait(pe, sems, evac, b, 4)
                    product(pe, n0 + b, bank[b % 4][:, 0:T], hl)

            @block.vector
            def _(dve):
                link = linker(dve, v_chain)
                link(dve.memset(one_row, 1.0))
                dve.wait_ge(dt_sum, 1)
                dve.tensor_scalar(dtT, bank[4][0:SSD_H, 0:T], sm("dt_bias")[0:SSD_H], None, ALU.add).then_inc(dt_read, 1)
                for b in range(20):
                    _, dst, i = kinds[b]
                    w, bias, nb = (("ssd_conv_w", "ssd_conv_b", 12) if dst is xbc else ("lru_conv_w", "lru_conv_b", 8))
                    y, ps = dst[:, i, :], bank[b % 4]
                    dve.wait_ge(blocks_done, n0 + b + 1)
                    link(dve.tensor_scalar(y, ps[:, 0:T], sm(w)[:, 3 * nb + i:3 * nb + i + 1],
                                           sm(bias)[:, i:i + 1], ALU.mult, ALU.add))
                    for j in range(1, 4):
                        tap = sm(w)[:, (3 - j) * nb + i:(3 - j) * nb + i + 1]
                        ins = dve.scalar_tensor_tensor(y[:, j:], ps[:, 0:T - j], tap, y[:, j:], ALU.mult, ALU.add)
                        if j < 3:
                            link(ins)
                    ins.then_inc(by_dve, 1)
                dve.wait_ge(dt_soft, 1)
                link(dve.scalar_tensor_tensor(dtT, dtT, 0.0, acsT, ALU.max, ALU.add))
                link(dve.tensor_scalar(acsT, dtT, negA, -1.0, ALU.mult, ALU.mult))
                dve.tensor_tensor_scan(acsT, one_row, acsT, 0.0, ALU.mult, ALU.add)

            @block.scalar
            def _(act):
                link = linker(act, a_chain)
                act.wait_ge(dt_read, 1)
                link(act.activation(acsT, dtT, ACT.Abs))
                link(act.activation(acsT, acsT, ACT.Exp, scale=-1.0))
                act.activation(negA, sm("a_log")[0:SSD_H], ACT.Exp)
                act.activation(acsT, acsT, ACT.Ln, bias=1.0).then_inc(dt_soft, 1)
                for b in range(20, 84):
                    f, dst, i = kinds[b]
                    if b == 36:
                        for c in range(12):
                            act.wait_ge(by_dve, c + 1)
                            act.activation(xbc[:, c, :], xbc[:, c, :], ACT.Silu)
                    act.wait_ge(blocks_done, n0 + b + 1)
                    act.activation(dst[:, i, :], bank[b % 4][:, 0:T], f).then_inc(by_act, 1)
        used[0] += 84

        A.at = mixer_mark
        xs_tok = A.take(TT, D)
        cb = A.take(2, 384)
        seg = A.take(2, 384)
        dt_tok = A.take(TT, SSD_H)
        nacs = A.take(TT, SSD_H)
        y_tok = A.take(TT, D)
        with Phase("small_t", "xs_t", "cb_ps", "bc_ps", "y_ps", "yt_ps", "v_small", "v_xs", "v_cb", "v_seg",
                   "a_exp", "v_m", "v_ytok", "v_y", "v_chain", "a_ytok") as (
                block, small_t, xs_t, cb_ps, bc_ps, y_ps, yt_ps, v_small, v_xs, v_cb, v_seg, a_exp, v_m, v_ytok, v_y,
                v_chain, a_ytok):
            @block.sync
            def _(sp):
                stream(sp, 0)

            @block.tensor
            def _(pe):
                for src, o in ((dtT, 0), (acsT, TT * SSD_H)):
                    for t in range(TT):
                        mm = pe.transpose(bank[4][:, o + t * SSD_H:o + (t + 1) * SSD_H], src[:, t * P:(t + 1) * P],
                                          ident[0:SSD_H, 0:SSD_H])
                mm.then_inc(small_t, 1)
                for t in range(TT):
                    for b in range(8):
                        mm = pe.transpose(bank[2 * t + b // 4][:, (b % 4) * P:(b % 4 + 1) * P],
                                          xbc[:, b, t * P:(t + 1) * P], ident)
                    mm.then_inc(xs_t, 1)
                for g in range(2):
                    pe.matmul(bank[5 + g][:, 0:T], xbc[:, 8 + g, 0:P], xbc[:, 10 + g, :], start=True, stop=True)
                    pe.matmul(bank[5 + g][:, T:384], xbc[:, 8 + g, P:T], xbc[:, 10 + g, P:T],
                              start=True, stop=True).then_inc(cb_ps, 1)
                pe.wait_ge(v_xs, 4)
                pe.wait_ge(v_small, 2)

                def broadcast(h):
                    if h >= 2:
                        pe.wait_ge(v_seg, h - 1)
                    pe.matmul(bank[4 + 3 * (h % 2)][:, 0:T], table("sel")[0:SSD_H, h * P:(h + 1) * P], acsT,
                              start=True, stop=True).then_inc(bc_ps, 1)

                broadcast(0)
                for h in range(SSD_H):
                    if h + 1 < SSD_H:
                        broadcast(h + 1)
                    pe.wait_ge(v_m, h + 1)
                    M = seg[:, h % 2, :]
                    c = slice((h % 8) * SSD_P, (h % 8 + 1) * SSD_P)
                    xh = slice(h * SSD_P, (h + 1) * SSD_P)
                    pe.matmul(bank[h // 8][:, c], M[:, 0:P], xs_tok[:, 0, xh], start=True, stop=True)
                    pe.matmul(bank[2 + h // 8][:, c], M[:, P:T], xs_tok[:, 0, xh], start=True, stop=False)
                    pe.matmul(bank[2 + h // 8][:, c], M[:, T:384], xs_tok[:, 1, xh], start=False,
                              stop=True).then_inc(y_ps, 1)
                for b in range(8):
                    if b >= 2:
                        pe.wait_ge(v_y, b - 1)
                    pe.wait_ge(a_ytok, 4)
                    for t in range(TT):
                        mm = pe.transpose(bank[4 + 3 * (b % 2)][:, t * P:(t + 1) * P],
                                          y_tok[:, t, b * P:(b + 1) * P], ident)
                    mm.then_inc(yt_ps, 1)

            @block.scalar
            def _(act):
                for h in range(SSD_H):
                    act.wait_ge(v_seg, h + 1)
                    act.activation(seg[:, h % 2, :], seg[:, h % 2, :], ACT.Exp).then_inc(a_exp, 1)
                act.wait_ge(y_ps, SSD_H)
                for t in range(TT):
                    for c in range(2):
                        act.activation(y_tok[:, t, c * 512:(c + 1) * 512], bank[2 * t + c][:, :],
                                       ACT.Copy).then_inc(a_ytok, 1)

            @block.vector
            def _(dve):
                link = linker(dve, v_chain)
                dve.wait_ge(small_t, 1)
                dve.tensor_copy(dt_tok.rearrange("p a b -> p (a b)"), bank[4][:, 0:32]).then_inc(v_small, 1)
                dve.tensor_scalar(nacs.rearrange("p a b -> p (a b)"), bank[4][:, 32:64], -1.0, None,
                                  ALU.mult).then_inc(v_small, 1)
                dve.wait_ge(v_small, 2)
                for t in range(TT):
                    dve.wait_ge(xs_t, t + 1)
                    for c in range(2):
                        dve.tensor_tensor(
                            xs_tok[:, t, c * 512:(c + 1) * 512].rearrange("p (h e) -> p h e", e=SSD_P),
                            bank[2 * t + c][:, :].rearrange("p (h e) -> p h e", e=SSD_P),
                            dt_tok[:, t, c * 8:(c + 1) * 8].unsqueeze(2).to_broadcast([P, 8, SSD_P]),
                            ALU.mult).then_inc(v_xs, 1)
                for g in range(2):
                    dve.wait_ge(cb_ps, g + 1)
                    dve.tensor_tensor(cb[:, g, :], bank[5 + g][:, 0:384], cc("causal"), ALU.mult).then_inc(v_cb, 1)
                dve.wait_ge(v_cb, 2)

                def segment(h):
                    dve.wait_ge(bc_ps, h + 1)
                    if h >= 2:
                        dve.wait_ge(y_ps, h - 1)
                    ps = bank[4 + 3 * (h % 2)]
                    dve.tensor_scalar(seg[:, h % 2, 0:T], ps[:, 0:T], nacs[:, 0, h:h + 1], 0.0, ALU.add, ALU.min)
                    dve.tensor_scalar(seg[:, h % 2, T:384], ps[:, P:T], nacs[:, 1, h:h + 1], 0.0, ALU.add,
                                      ALU.min).then_inc(v_seg, 1)

                segment(0)
                for h in range(SSD_H):
                    if h + 1 < SSD_H:
                        segment(h + 1)
                    dve.wait_ge(a_exp, h + 1)
                    dve.tensor_tensor(seg[:, h % 2, :], seg[:, h % 2, :], cb[:, h // 8, :], ALU.mult).then_inc(v_m, 1)
                for b in range(8):
                    dve.wait_ge(yt_ps, b + 1)
                    dve.scalar_tensor_tensor(xbc[:, b, :], xbc[:, b, :], sm("ssd_d")[:, b:b + 1],
                                             bank[4 + 3 * (b % 2)][:, 0:T], ALU.mult, ALU.add).then_inc(v_y, 1)
                dve.wait_ge(v_y, 8)
                dve.tensor_tensor(xbc[:, 0:8, :], xbc[:, 0:8, :], z_gate, ALU.mult)

        y_ssd = xbc
        A.at = mixer_mark
        rms_phase([(lambda kt: xbc[:, kt, :], lambda kt: xbc[:, kt, :], column("ssd_norm"), None)])

        A.at = mixer_mark
        r_g = A.take(8, T)
        i_g = A.take(8, T)
        sp_l = A.take(3, 8)
        n0 = used[0]
        with Phase("v_c", "a_lam", "v_r", "a_r", "a_sp", "v_sp", "gates_ps", "a_gates", "a_exp", "v_u2",
                   "a_sqrt", "v_u", "v_scan", "a_chain", "v_chain") as (
                block, v_c, a_lam, v_r, a_r, a_sp, v_sp, gates_ps, a_gates, a_exp, v_u2, a_sqrt, v_u, v_scan,
                a_chain, v_chain):
            u_t = A.take(8, T)

            @block.sync
            def _(sp):
                stream(sp, 4)

            @block.tensor
            def _(pe):
                for o in range(LRU_O):
                    if o % 4 == 0:
                        arrived(pe, n0 + o // 4 * 2)
                        arrived(pe, n0 + o // 4 * 2 + 1)
                    if o >= 4:
                        pe.wait_ge(a_gates, 2 * (o - 3))
                    for w in range(2):
                        for k in range(2):
                            c = ((o % 4) * 2 + k) * P
                            mm = pe.matmul(bank[o % 4][:, w * T:(w + 1) * T],
                                           ring[:, (n0 + o // 4 * 2 + w) % NS, c:c + P],
                                           xl_conv[:, o // 2 * 2 + k, :], start=(k == 0), stop=(k == 1))
                        if o % 4 == 3:
                            mm.then_inc(blocks_done, 1)
                    if o % 4 != 3:
                        mm.then_inc(gates_ps, 1)

            @block.scalar
            def _(act):
                link = linker(act, a_chain)
                lam = sm("lru_lambda")
                link(act.activation(sp_l[:, 0, :], lam, ACT.Abs))
                link(act.activation(sp_l[:, 0, :], sp_l[:, 0, :], ACT.Exp, scale=-1.0))
                act.activation(sp_l[:, 0, :], sp_l[:, 0, :], ACT.Ln, bias=1.0).then_inc(a_sp, 1)
                for o in range(LRU_O):
                    if o % 4 == 3:
                        act.wait_ge(blocks_done, n0 + o // 4 * 2 + 2)
                    else:
                        act.wait_ge(gates_ps, o + 1 - o // 4)
                    act.activation(r_g[:, o, :], bank[o % 4][:, 0:T], ACT.Sigmoid,
                                   bias=sm("lru_b_a")[:, o:o + 1]).then_inc(a_gates, 1)
                    act.activation(i_g[:, o, :], bank[o % 4][:, T:2 * T], ACT.Sigmoid,
                                   bias=sm("lru_b_i")[:, o:o + 1]).then_inc(a_gates, 1)
                act.wait_ge(v_sp, 1)
                act.wait_ge(a_gates, 16)
                for o in range(LRU_O):
                    act.activation(u_t[:, o, :], r_g[:, o, :], ACT.Tanh, scale=sp_l[:, 1, o:o + 1]).then_inc(a_r, 1)
                act.wait_ge(a_r, 8)
                for o in range(LRU_O):
                    act.activation(r_g[:, o, :], r_g[:, o, :], ACT.Exp, scale=sp_l[:, 2, o:o + 1]).then_inc(a_exp, 1)
                for o in range(LRU_O):
                    act.wait_ge(v_u2, o + 1)
                    act.activation(u_t[:, o, :], u_t[:, o, :], ACT.Sqrt).then_inc(a_sqrt, 1)

            @block.vector
            def _(dve):
                link = linker(dve, v_chain)
                dve.wait_ge(a_sp, 1)
                link(dve.tensor_scalar(sp_l[:, 1, :], sm("lru_lambda"), -1.0, 0.0, ALU.mult, ALU.max))
                link(dve.tensor_tensor(sp_l[:, 0, :], sp_l[:, 1, :], sp_l[:, 0, :], ALU.add))
                dve.tensor_scalar(sp_l[:, 1, :], sp_l[:, 0, :], 8.0, None, ALU.mult)
                dve.tensor_scalar(sp_l[:, 2, :], sp_l[:, 0, :], -8.0, None, ALU.mult).then_inc(v_sp, 1)
                dve.wait_ge(a_gates, 16)
                link(dve.tensor_tensor(i_g, i_g, xl_conv, ALU.mult))
                for o in range(LRU_O):
                    dve.wait_ge(a_exp, o + 1)
                    a, u, xo = r_g[:, o, :], u_t[:, o, :], xl_conv[:, o, :]
                    link(dve.tensor_tensor(xo, a, a, ALU.mult))
                    link(dve.scalar_tensor_tensor(u, xo, 1.0, u, ALU.add, ALU.mult))
                    dve.tensor_scalar(u, u, 1e-34, None, ALU.max).then_inc(v_u2, 1)
                for o in range(LRU_O):
                    dve.wait_ge(a_sqrt, o + 1)
                    a, u = r_g[:, o, :], u_t[:, o, :]
                    link(dve.tensor_tensor(u, u, i_g[:, o, :], ALU.mult))
                    link(dve.tensor_tensor_scan(u, a, u, 0.0, ALU.mult, ALU.add))
                    dve.tensor_tensor(xl_conv[:, o, :], u, y_gate[:, o, :], ALU.mult)
        used[0] += 4
        y_lru = xl_conv

        A.at = mixer_mark
        v_tok = A.take(TT, D)
        tmp = A.take(2, T)
        sc = A.take(2, 384)
        y_ret = A.take(8, T)
        ysq = A.take(2, 2, T)
        rs_r = A.take(RET_H, T)
        with Phase("rot_ps", "v_rot", "rotated", "vt_ps", "a_vt", "sc_ps", "v_sc", "y_ps", "a_y", "a_sq", "norm_ps",
                   "v_inv", "a_root", "v_chain") as (
                block, rot_ps, v_rot, rotated, vt_ps, a_vt, sc_ps, v_sc, y_ps, a_y, a_sq, norm_ps, v_inv, a_root,
                v_chain):
            qk = [(q_ret[:, h, :], "ret") for h in range(RET_H)] + [(k_ret[:, h, :], "retk") for h in range(RET_H)]

            @block.sync
            def _(sp):
                stream(sp, 0)

            @block.tensor
            def _(pe):
                for n, (q, _) in enumerate(qk):
                    if n >= 2:
                        pe.wait_ge(v_rot, n - 1)
                    pe.matmul(bank[n % 2][:, 0:T], cc("rot"), q, start=True, stop=True).then_inc(rot_ps, 1)
                for b in range(8):
                    if b >= 2:
                        pe.wait_ge(a_vt, b - 1)
                    for t in range(TT):
                        mm = pe.transpose(bank[2 + b % 2][:, t * P:(t + 1) * P], v_ret[:, b, t * P:(t + 1) * P], ident)
                    mm.then_inc(vt_ps, 1)
                pe.wait_ge(rotated, 8)
                pe.wait_ge(a_vt, 8)

                def scores(h):
                    if h >= 2:
                        pe.wait_ge(v_sc, h - 1)
                    ps = bank[4 + h % 2]
                    pe.matmul(ps[:, 0:T], k_ret[:, h, 0:P], q_ret[:, h, :], start=True, stop=True)
                    pe.matmul(ps[:, T:384], k_ret[:, h, P:T], q_ret[:, h, P:T], start=True,
                              stop=True).then_inc(sc_ps, 1)

                scores(0)
                for h in range(RET_H):
                    if h + 1 < RET_H:
                        scores(h + 1)
                    pe.wait_ge(v_sc, h + 1)
                    if h >= 2:
                        pe.wait_ge(a_y, h - 1)
                    for e in range(2):
                        v = slice((2 * h + e) * P, (2 * h + e + 1) * P)
                        o = bank[h % 2][:, e * T:(e + 1) * T]
                        pe.matmul(o, v_tok[:, 0, v], sc[:, h % 2, 0:T], start=True, stop=False)
                        mm = pe.matmul(o[:, P:T], v_tok[:, 1, v], sc[:, h % 2, T:384], start=False, stop=True)
                    mm.then_inc(y_ps, 1)
                for h in range(RET_H):
                    pe.wait_ge(a_sq, h + 1)
                    if h >= 2:
                        pe.wait_ge(v_inv, h - 1)
                    for e in range(2):
                        mm = pe.matmul(bank[6 + h % 2][:, 0:T], ones[:, :], ysq[:, h % 2, e, :], start=(e == 0),
                                       stop=(e == 1))
                    mm.then_inc(norm_ps, 1)

            @block.scalar
            def _(act):
                for b in range(8):
                    act.wait_ge(vt_ps, b + 1)
                    act.activation(v_tok[:, :, b * P:(b + 1) * P],
                                   bank[2 + b % 2][:, 0:T].rearrange("p (t c) -> p t c", t=TT), ACT.Copy).then_inc(a_vt, 1)
                for h in range(RET_H):
                    act.wait_ge(y_ps, h + 1)
                    act.activation(y_ret[:, 2 * h:2 * h + 2, :],
                                   bank[h % 2][:, :].rearrange("p (t c) -> p t c", t=2), ACT.Copy).then_inc(a_y, 1)
                    if h >= 2:
                        act.wait_ge(norm_ps, h - 1)
                    act.wait_ge(a_y, h + 1)
                    act.activation(ysq[:, h % 2, :, :], y_ret[:, 2 * h:2 * h + 2, :], ACT.Square).then_inc(a_sq, 1)
                for h in range(RET_H):
                    act.wait_ge(v_inv, h + 1)
                    act.activation(rs_r[:, h, :], rs_r[:, h, :], ACT.Sqrt).then_inc(a_root, 1)

            @block.vector
            def _(dve):
                link = linker(dve, v_chain)
                for n, (q, name) in enumerate(qk):
                    dve.wait_ge(rot_ps, n + 1)
                    dve.tensor_tensor(tmp[:, n % 2, :], bank[n % 2][:, 0:T], table(name + "_sin"), ALU.mult).then_inc(v_rot, 1)
                    link(dve.tensor_tensor(q, q, table(name + "_cos"), ALU.mult))
                    dve.wait_ge(v_rot, n + 1)
                    dve.tensor_tensor(q, q, tmp[:, n % 2, :], ALU.add).then_inc(rotated, 1)
                for h in range(RET_H):
                    dve.wait_ge(sc_ps, h + 1)
                    if h >= 2:
                        dve.wait_ge(y_ps, h - 1)
                    dve.tensor_tensor(sc[:, h % 2, :], bank[4 + h % 2][:, 0:384],
                                      table("ret_mask")[:, h * 384:(h + 1) * 384], ALU.mult).then_inc(v_sc, 1)
                for h in range(RET_H):
                    dve.wait_ge(norm_ps, h + 1)
                    link(dve.tensor_scalar(rs_r[:, h, :], bank[6 + h % 2][:, 0:T], 1.0 / T, EPS, ALU.mult, ALU.add))
                    dve.reciprocal(rs_r[:, h, :], rs_r[:, h, :]).then_inc(v_inv, 1)
                for h in range(RET_H):
                    dve.wait_ge(a_root, h + 1)
                    y = y_ret[:, 2 * h:2 * h + 2, :]
                    link(dve.tensor_tensor(y, y, rs_r[:, h, :].unsqueeze(1).to_broadcast([P, 2, T]), ALU.mult))
                    dve.tensor_tensor(y, y, g_gate[:, 2 * h:2 * h + 2, :], ALU.mult)

        merged = z_gate
        n0 = used[0]
        with Phase("by_dve", "v_chain") as (block, by_dve, v_chain):
            tm = A.take(T)
            branches = [y_ret, y_lru, y_ssd]

            @block.sync
            def _(sp):
                stream(sp, 24)

            @block.tensor
            def _(pe):
                for b in range(24):
                    evac_wait(pe, {"dve": by_dve}, ["dve"] * 24, b, 4)
                    product(pe, n0 + b, bank[b % 4][:, 0:T], lambda kt: branches[b // 8][:, kt, :])

            @block.vector
            def _(dve):
                link = linker(dve, v_chain)
                for b in range(24):
                    br, d = 2 - b // 8, b % 8
                    dve.wait_ge(blocks_done, n0 + b + 1)
                    if b < 8:
                        dve.tensor_tensor(merged[:, d, :], bank[b % 4][:, 0:T], gates[:, br * 8 + d, :],
                                          ALU.mult).then_inc(by_dve, 1)
                    else:
                        dve.tensor_tensor(tm, bank[b % 4][:, 0:T], gates[:, br * 8 + d, :], ALU.mult).then_inc(by_dve, 1)
                        dve.wait_ge(by_dve, b + 1)
                        link(dve.tensor_tensor(merged[:, d, :], merged[:, d, :], tm, ALU.add))
        used[0] += 24

        def residual(n, rhs, gain=None, streams=(1,), kgroups=1):
            n0 = used[0]
            both = len(streams) == 2
            width = 512 if both else T
            with Phase("by_dve") as (block, by_dve):
                @block.sync
                def _(sp):
                    stream(sp, n * kgroups)

                @block.tensor
                def _(pe):
                    for d in range(n):
                        if d >= 4:
                            pe.wait_ge(by_dve, (d - 3) * len(streams))
                        for g in range(kgroups):
                            arrived(pe, n0 + d * kgroups + g)
                            for kt in range(KT):
                                mm = pe.matmul(bank[d % 4][:, 0:width], col(n0 + d * kgroups + g, kt),
                                               rhs(g * KT + kt), start=(g == 0 and kt == 0),
                                               stop=(g == kgroups - 1 and kt == KT - 1))
                            mm.then_inc(blocks_done, 1)

                @block.vector
                def _(dve):
                    for d in range(n):
                        dve.wait_ge(blocks_done, n0 + (d + 1) * kgroups)
                        for j, s in enumerate(streams):
                            ps = bank[d % 4][:, j * T:(j + 1) * T]
                            if gain is None:
                                dve.tensor_tensor(X[:, d, s, :], X[:, d, s, :], ps, ALU.add).then_inc(by_dve, 1)
                            else:
                                dve.scalar_tensor_tensor(X[:, d, s, :], ps, gain(d, s), X[:, d, s, :], ALU.mult,
                                                         ALU.add).then_inc(by_dve, 1)
            used[0] += n * kgroups

        residual(8, lambda kt: merged[:, kt, :])

        A.at = 0
        rms_phase([(xl, hl, column("norm_ffn"), None)])
        f = A.take(FFN_T, T)
        n0 = used[0]
        with Phase("v_conv", "a_gelu", "by_dve", "v_chain") as (block, v_conv, a_gelu, by_dve, v_chain):
            @block.sync
            def _(sp):
                stream(sp, 48)

            @block.tensor
            def _(pe):
                for b in range(48):
                    if b >= 6:
                        pe.wait_ge(by_dve if b % 2 else v_conv, (b - 6) // 2 + 1)
                    product(pe, n0 + b, bank[b % 6][:, 0:T], hl)

            @block.scalar
            def _(act):
                for i in range(FFN_T):
                    act.wait_ge(v_conv, i + 1)
                    act.activation(f[:, i, :], f[:, i, :], ACT.Gelu_apprx_tanh).then_inc(a_gelu, 1)

            @block.vector
            def _(dve):
                link = linker(dve, v_chain)

                def up(i):
                    dve.wait_ge(a_gelu, i + 1)
                    dve.wait_ge(blocks_done, n0 + 2 * i + 2)
                    dve.tensor_tensor(f[:, i, :], f[:, i, :], bank[(2 * i + 1) % 6][:, 0:T], ALU.mult).then_inc(by_dve, 1)

                for i in range(FFN_T):
                    y, ps = f[:, i, :], bank[2 * i % 6]
                    w = sm("ffn_conv_w")
                    dve.wait_ge(blocks_done, n0 + 2 * i + 1)
                    link(dve.tensor_scalar(y, ps[:, 0:T], w[:, 48 + i:49 + i], sm("ffn_conv_b")[:, i:i + 1],
                                           ALU.mult, ALU.add))
                    link(dve.scalar_tensor_tensor(y[:, 1:], ps[:, 0:T - 1], w[:, 24 + i:25 + i], y[:, 1:],
                                                  ALU.mult, ALU.add))
                    dve.scalar_tensor_tensor(y[:, 2:], ps[:, 0:T - 2], w[:, i:i + 1], y[:, 2:],
                                             ALU.mult, ALU.add).then_inc(v_conv, 1)
                    if i:
                        up(i - 1)
                up(FFN_T - 1)
        used[0] += 48
        residual(8, lambda kt: f[:, kt, :], kgroups=3)
        A.at = 0
        rms_phase([(xl, xl, column("norm_final"), None)])

        for l in range(LAYERS):
            last = l == LAYERS - 1
            lam_init = 0.8 - 0.6 * math.exp(-0.3 * l)
            streams = (1,) if last else (0, 1)
            t0 = T if last else 0
            A.at = 0
            mod = A.take(48, 2)
            gain1 = A.take(8, 2)
            gain2 = A.take(8, 2)
            nlam = A.take(1)
            cond = A.take(8, 2)
            layer_mark = A.at

            n0 = used[0]
            with Phase("a_cond", "a_chain", "v_chain", "v_lam", "a_lam") as (block, a_cond, a_chain, v_chain, v_lam, a_lam):
                lam2 = A.take(2)
                prod = A.take(2, 64)

                @block.sync
                def _(sp):
                    stream(sp, 48)

                @block.scalar
                def _(act):
                    act.activation(cond.rearrange("p a b -> p (a b)"), sm("cond"), ACT.Silu).then_inc(a_cond, 1)
                    act.wait_ge(v_lam, 1)
                    act.activation(lam2, lam2, ACT.Exp).then_inc(a_lam, 1)

                @block.tensor
                def _(pe):
                    pe.wait_ge(a_cond, 1)
                    with pe.Fori(0, 48 // NS) as it:
                        for u in range(NS):
                            product(pe, n0 + u, bank[0][:, bass.ds(it * (2 * NS) + 2 * u, 2)], lambda kt: cond[:, kt, :], it)

                @block.vector
                def _(dve):
                    link = linker(dve, v_chain)
                    lp = sm(f"lam{l}").rearrange("p (a b c) -> p a b c", a=2, b=2)
                    link(dve.tensor_tensor(prod, lp[:, :, 0, :], lp[:, :, 1, :], ALU.mult))
                    dve.tensor_reduce(lam2, prod, AX.X, ALU.add).then_inc(v_lam, 1)
                    dve.wait_ge(a_lam, 1)
                    link(dve.tensor_tensor(nlam, lam2[:, 1:2], lam2[:, 0:1], ALU.subtract))
                    dve.tensor_scalar(nlam, nlam, -lam_init, None, ALU.add)
                    dve.wait_ge(blocks_done, n0 + 48)
                    link(dve.tensor_tensor(mod, bank[0][:, 0:96].rearrange("p (a b) -> p a b", b=2),
                                           sm(f"ada_b{l}").unsqueeze(2).to_broadcast([P, 48, 2]), ALU.add))
                    for g, first, name in ((gain1, 8, "norm1"), (gain2, 32, "norm2")):
                        dve.scalar_tensor_tensor(g, mod[:, first:first + 8, :], 1.0,
                                                 sm(f"{name}{l}").unsqueeze(2).to_broadcast([P, 8, 2]), ALU.add, ALU.mult)
            used[0] += 48
            A.at = layer_mark

            def norm_jobs(gain, first, ss):
                return [((lambda kt, s=s: X[:, kt, s, :]), (lambda kt, s=s: H[:, kt, s, :]),
                         (lambda kt, s=s: gain[:, kt, s:s + 1]), (lambda kt, s=s: mod[:, first + kt, s:s + 1])) for s in ss]

            rms_phase(norm_jobs(gain1, 0, (0, 1)))

            mix = A.take(8, 2 * T)
            mix_mark = A.at
            u_pad = A.take(2, 2, T + CONV_K - 1)
            u_sig = A.take(2, 2 * T)
            mq, mk, mv, mo = (A.take(2, 2 * T) for _ in range(4))
            dq, dk, dv = (A.take(4, 2 * T) for _ in range(3))
            ig = A.take(2 * T)[0:36]
            fg = A.take(2 * T)[0:36]
            kinds = [("gate", None, 0)] + [(ACT.Sigmoid, u_sig, i) for i in range(2)] + [("glu", u_pad, i) for i in range(2)]
            kinds += [(ACT.Sigmoid, mo, i) for i in range(2)]
            kinds += [(ACT.Copy, m, i) for m in (mq, mk, mv) for i in range(2)]
            kinds += [(ACT.Copy, m, i) for m in (dq, dk, dv) for i in range(4)]
            evac = ["dve" if isinstance(k[0], str) else "act" for k in kinds]
            n0 = used[0]
            with Phase("by_act", "by_dve", "padded", "v_gate") as (block, by_act, by_dve, padded, v_gate):
                @block.sync
                def _(sp):
                    stream(sp, 25)

                @block.gpsimd
                def _(pool):
                    pool.memset(u_pad, 0.0).then_inc(padded, 1)

                @block.tensor
                def _(pe):
                    for b in range(25):
                        evac_wait(pe, {"act": by_act, "dve": by_dve}, evac, b, 6)
                        product(pe, n0 + b, bank[b % 6][:, :], lambda kt: H[:, kt, :, :].rearrange("p s t -> p (s t)"))

                @block.scalar
                def _(act):
                    for b, (f, dst, i) in enumerate(kinds):
                        if evac[b] == "act":
                            act.wait_ge(blocks_done, n0 + b + 1)
                            act.activation(dst[:, i, :], bank[b % 6][:, :], f,
                                           scale=ML_D ** -0.5 if dst is mk else 1.0).then_inc(by_act, 1)

                @block.vector
                def _(dve):
                    gb = sm(f"gate_b{l}")
                    dve.wait_ge(blocks_done, n0 + 1)
                    dve.tensor_scalar(ig, bank[0][0:36, :], gb[0:36], None, ALU.add)
                    dve.tensor_scalar(fg, bank[0][64:100, :], gb[64:100], None, ALU.add).then_inc(by_dve, 1)
                    dve.wait_ge(padded, 1)
                    for i in range(2):
                        dve.wait_ge(by_act, i + 1)
                        dve.wait_ge(blocks_done, n0 + 4 + i)
                        dve.tensor_tensor(u_pad[:, i, :, CONV_K // 2:CONV_K // 2 + T],
                                          bank[3 + i][:, :].rearrange("p (s t) -> p s t", s=2),
                                          u_sig[:, i, :].rearrange("p (s t) -> p s t", s=2), ALU.mult).then_inc(by_dve, 1)
            used[0] += 25

            conv_mark = A.at
            acc = A.take(2, 2 * T)
            csq = A.take(2, 2 * T)
            crs = A.take(2 * T)
            with Phase("v_tap", "mean_ps", "v_cent", "a_csq", "var_ps", "v_inv", "a_root", "v_norm", "v_chain") as (
                    block, v_tap, mean_ps, v_cent, a_csq, var_ps, v_inv, a_root, v_norm, v_chain):
                @block.sync
                def _(sp):
                    stream(sp, 0)

                @block.vector
                def _(dve):
                    link = linker(dve, v_chain)
                    w = sm(f"conv_w{l}")
                    for k in range(CONV_K):
                        for i in range(2):
                            y = acc[:, i, :].rearrange("p (s t) -> p s t", s=2)
                            src = u_pad[:, i, :, k:k + T]
                            tap = w[:, 2 * k + i:2 * k + i + 1]
                            if k == 0:
                                dve.tensor_scalar(y, src, tap, sm(f"conv_b{l}")[:, i:i + 1], ALU.mult, ALU.add).then_inc(v_tap, 1)
                            else:
                                dve.wait_ge(v_tap, 2 * k + i - 1)
                                dve.scalar_tensor_tensor(y, src, tap, y, ALU.mult, ALU.add).then_inc(v_tap, 1)
                    dve.wait_ge(mean_ps, 1)
                    for i in range(2):
                        dve.scalar_tensor_tensor(acc[:, i, :], bank[0][:, :], -1.0 / T, acc[:, i, :],
                                                 ALU.mult, ALU.add).then_inc(v_cent, 1)
                    dve.wait_ge(var_ps, 1)
                    link(dve.tensor_scalar(crs, bank[1][:, :], 1.0 / T, EPS, ALU.mult, ALU.add))
                    dve.reciprocal(crs, crs).then_inc(v_inv, 1)
                    dve.wait_ge(a_root, 1)
                    for i in range(2):
                        dve.scalar_tensor_tensor(acc[:, i, :], acc[:, i, :], sm(f"ln_g{l}")[:, i:i + 1], crs,
                                                 ALU.mult, ALU.mult).then_inc(v_norm, 1)

                @block.tensor
                def _(pe):
                    pe.wait_ge(v_tap, 2 * CONV_K)
                    for i in range(2):
                        mm = pe.matmul(bank[0][:, :], ones[:, :], acc[:, i, :], start=(i == 0), stop=(i == 1))
                    mm.then_inc(mean_ps, 1)
                    for i in range(2):
                        pe.wait_ge(a_csq, i + 1)
                        mm = pe.matmul(bank[1][:, :], ones[:, :], csq[:, i, :], start=(i == 0), stop=(i == 1))
                    mm.then_inc(var_ps, 1)

                @block.scalar
                def _(act):
                    for i in range(2):
                        act.wait_ge(v_cent, i + 1)
                        act.activation(csq[:, i, :], acc[:, i, :], ACT.Square).then_inc(a_csq, 1)
                    act.wait_ge(v_inv, 1)
                    act.activation(crs, crs, ACT.Sqrt).then_inc(a_root, 1)
                    for i in range(2):
                        act.wait_ge(v_norm, i + 1)
                        act.activation(mix[:, i, :], acc[:, i, :], ACT.Silu, bias=sm(f"ln_b{l}")[:, i:i + 1])
            A.at = conv_mark

            rows = 36
            Bt, Mx, En, Lt, on = (A.take(2 * T)[0:rows] for _ in range(5))
            u_tok = A.take(4, rows)
            en_tok = A.take(4, rows)
            v_aug = A.take(4, ML_H, ML_D + 1)
            wb = A.take(2, 4, 2 * T)
            rec = A.take(2, 4)
            hs = A.take(4, ML_H, ML_D)
            htmp = A.take(4, ML_D)
            ms = A.take(16)
            tiles = list(range(t0 // P, 4))

            def spans(d, st):
                if d == 0:
                    r = [(max(st * P, t0), 2 * T)]
                elif st >= 2:
                    r = [(T, (st + 1) * P)]
                elif last:
                    r = [(T, 2 * T)]
                else:
                    r = [(0, 2 * T)] if st == 1 else [(0, P), (T, 2 * T)]
                return r

            def sources(d, tt):
                if d == 0:
                    return list(range(tt + 1))
                return list(range(tt, 2)) if tt < 2 else [0, 1] + list(range(tt, 4))

            with Phase("zeroed", "a_soft", "v_lf", "v_state", "a_en", "tok_ps", "v_tok", "vt_ps", "v_vt", "bc_ps",
                       "sc_ps", "v_z", "a_w", "v_w", "pv_ps", "v_h", "v_chain", "a_chain", "v_mean", "a_root",
                       "v_hn", "ht_ps", "scan") as (
                    block, zeroed, a_soft, v_lf, v_state, a_en, tok_ps, v_tok, vt_ps, v_vt, bc_ps, sc_ps, v_z, a_w,
                    v_w, pv_ps, v_h, v_chain, a_chain, v_mean, a_root, v_hn, ht_ps, scan):
                @block.sync
                def _(sp):
                    stream(sp, 0)

                @block.gpsimd
                def _(pool):
                    pool.memset(Bt, 0.0)
                    pool.memset(Mx, 0.0)
                    pool.memset(v_aug, 1.0)
                    pool.memset(on, 1.0).then_inc(zeroed, 1)

                @block.scalar
                def _(act):
                    link = linker(act, a_chain)
                    link(act.activation(Lt, fg, ACT.Abs))
                    link(act.activation(Lt, Lt, ACT.Exp, scale=-1.0))
                    act.activation(Lt, Lt, ACT.Ln, bias=1.0).then_inc(a_soft, 1)
                    act.wait_ge(v_state, 1)
                    act.activation(En, En, ACT.Exp, scale=-1.0).then_inc(a_en, 1)
                    n = 0
                    for h in range(ML_H):
                        for d in range(2):
                            for st in range(4):
                                n += 1
                                act.wait_ge(v_z, n)
                                for i, (lo, hi) in enumerate(spans(d, st)):
                                    w = act.activation(wb[:, d, st, lo:hi], wb[:, d, st, lo:hi], ACT.Exp, scale=-1.0)
                                w.then_inc(a_w, 1)
                    act.wait_ge(v_mean, 1)
                    act.activation(ms, ms, ACT.Sqrt).then_inc(a_root, 1)

                @block.tensor
                def _(pe):
                    for b in range(2):
                        for tt in range(4):
                            mm = pe.transpose(bank[b][:, tt * P:(tt + 1) * P], mv[:, b, tt * P:(tt + 1) * P], ident)
                        mm.then_inc(vt_ps, 1)
                    pe.wait_ge(v_state, 1)
                    for tt in range(4):
                        pe.transpose(bank[2][:, tt * rows:(tt + 1) * rows], ig[:, tt * P:(tt + 1) * P],
                                     ident[0:rows, 0:rows])
                    pe.wait_ge(a_en, 1)
                    for tt in range(4):
                        mm = pe.transpose(bank[2][:, (4 + tt) * rows:(5 + tt) * rows], En[:, tt * P:(tt + 1) * P],
                                          ident[0:rows, 0:rows])
                    mm.then_inc(tok_ps, 1)
                    pe.wait_ge(v_vt, 2)
                    pe.wait_ge(v_tok, 2)
                    for h in range(ML_H):
                        r = slice((h % 2) * 64, (h % 2) * 64 + 64)
                        if h:
                            pe.wait_ge(v_w, 8 * h)
                        for d in range(2):
                            pe.matmul(bank[d][:, t0:], cc("selm")[32 * d:32 * d + 4, h * P:(h + 1) * P],
                                      Mx[32 * d:32 * d + 4, t0:], start=True, stop=True).then_inc(bc_ps, 1)
                        for st in range(4):
                            pe.matmul(bank[2 + st][:, t0:], mk[r, h // 2, st * P:(st + 1) * P], mq[r, h // 2, t0:],
                                      start=True, stop=True).then_inc(sc_ps, 1)
                        for d in range(2):
                            if h:
                                pe.wait_ge(v_h, 2 * (h - 1) + d + 1)
                            pe.wait_ge(v_w, 8 * h + 4 * (d + 1))
                            for tt in tiles:
                                src = sources(d, tt)
                                for st in src:
                                    mm = pe.matmul(bank[6 + d][:, tt * 65:tt * 65 + 65], wb[:, d, st, tt * P:(tt + 1) * P],
                                                   v_aug[:, st, h, :], start=(st == src[0]), stop=(st == src[-1]))
                            mm.then_inc(pv_ps, 1)
                    pe.wait_ge(v_hn, 1)
                    for b in range(2):
                        for tt in tiles:
                            mm = pe.transpose(bank[b][:, tt * P:(tt + 1) * P],
                                              hs[:, tt, 2 * b:2 * b + 2, :].rearrange("p a b -> p (a b)"), ident)
                        mm.then_inc(ht_ps, 1)

                @block.vector
                def _(dve):
                    link = linker(dve, v_chain)
                    dve.wait_ge(a_soft, 1)
                    dve.wait_ge(zeroed, 1)
                    link(dve.scalar_tensor_tensor(Lt, fg, 0.0, Lt, ALU.min, ALU.subtract))

                    def scans(dst, op, data0, data1, initial):
                        f, r = slice(0, 4), slice(32, 36)
                        dve.tensor_tensor_scan(dst[f], data0[f], data1[f], initial, op[0], op[1])
                        link(dve.tensor_tensor_scan(dst[r, T - 1::-1], data0[r, T - 1::-1], data1[r, T - 1::-1],
                                                    initial, op[0], op[1]))
                        link(dve.tensor_tensor_scan(dst[r, 2 * T - 1:T - 1:-1], data0[r, 2 * T - 1:T - 1:-1],
                                                    data1[r, 2 * T - 1:T - 1:-1], dst[r, 0:1], op[0], op[1]))

                    scans(Bt, (ALU.mult, ALU.add), on, Lt, 0.0)
                    link(dve.tensor_tensor(ig, ig, Bt, ALU.subtract))
                    scans(Mx, (ALU.max, ALU.max), ig, ig, 0.0)
                    dve.tensor_tensor(En, Bt, Mx, ALU.add).then_inc(v_state, 1)
                    for b in range(2):
                        dve.wait_ge(vt_ps, b + 1)
                        dve.tensor_copy(v_aug[:, :, 2 * b:2 * b + 2, 0:ML_D],
                                        bank[b][:, :].rearrange("p (t h e) -> p t h e", t=4, h=2)).then_inc(v_vt, 1)
                    dve.wait_ge(tok_ps, 1)
                    dve.tensor_copy(u_tok.rearrange("p a b -> p (a b)"), bank[2][:, 0:4 * rows]).then_inc(v_tok, 1)
                    dve.tensor_copy(en_tok.rearrange("p a b -> p (a b)"), bank[2][:, 4 * rows:8 * rows]).then_inc(v_tok, 1)
                    dve.wait_ge(v_tok, 2)
                    n = 0
                    for h in range(ML_H):
                        for d in range(2):
                            c = 32 * d + h
                            dve.wait_ge(bc_ps, 2 * h + d + 1)
                            if h:
                                dve.wait_ge(pv_ps, 2 * (h - 1) + d + 1)
                            for st in range(4):
                                for lo, hi in spans(d, st):
                                    w = dve.tensor_scalar(wb[:, d, st, lo:hi], bank[d][:, lo:hi], u_tok[:, st, c:c + 1],
                                                          0.0, ALU.subtract, ALU.max)
                                w.then_inc(v_z, 1)
                        for d in range(2):
                            for st in range(4):
                                n += 1
                                dve.wait_ge(a_w, n)
                                dve.wait_ge(sc_ps, 4 * h + st + 1)
                                diag = st * P >= t0
                                for lo, hi in spans(d, st):
                                    w = dve.tensor_tensor(wb[:, d, st, lo:hi], wb[:, d, st, lo:hi],
                                                          bank[2 + st][:, lo:hi], ALU.mult)
                                if diag:
                                    link(w)
                                    w = dve.tensor_tensor(wb[:, d, st, st * P:(st + 1) * P], wb[:, d, st, st * P:(st + 1) * P],
                                                          cc("anti") if d else cc("causal")[:, 0:P], ALU.mult)
                                w.then_inc(v_w, 1)
                        for d in range(2):
                            c = 32 * d + h
                            a, nt = tiles[0], len(tiles)
                            dve.wait_ge(pv_ps, 2 * h + d + 1)
                            ps = bank[6 + d][:, 0:260].rearrange("p (t e) -> p t e", t=4)[:, a:4, :]
                            link(dve.scalar_tensor_tensor(rec[:, d, a:4], ps[:, :, ML_D], -1.0, en_tok[:, a:4, c],
                                                          ALU.mult, ALU.max))
                            link(dve.tensor_tensor(rec[:, d, a:4], ps[:, :, ML_D], rec[:, d, a:4], ALU.max))
                            link(dve.reciprocal(rec[:, d, a:4], rec[:, d, a:4]))
                            rb = rec[:, d, a:4].unsqueeze(2).to_broadcast([P, nt, ML_D])
                            if d == 0:
                                dve.tensor_tensor(hs[:, a:4, h, :], ps[:, :, 0:ML_D], rb, ALU.mult).then_inc(v_h, 1)
                            else:
                                dve.tensor_tensor(htmp[:, a:4, :], ps[:, :, 0:ML_D], rb, ALU.mult).then_inc(v_h, 1)
                                dve.wait_ge(v_h, 2 * h + 2)
                                link(dve.tensor_tensor(hs[:, a:4, h, :], hs[:, a:4, h, :], htmp[:, a:4, :], ALU.add))
                    a, nt = tiles[0], len(tiles)
                    hv = hs[:, a:4, :, :].rearrange("p t h e -> p (t h) e")
                    mv_ = ms[:, 4 * a:16]
                    for tt in range(a, 4):
                        link(dve.tensor_tensor(wb[:, 0, tt, 0:T], hs[:, tt, :, :].rearrange("p h e -> p (h e)"),
                                               hs[:, tt, :, :].rearrange("p h e -> p (h e)"), ALU.mult))
                        link(dve.tensor_reduce(ms[:, 4 * tt:4 * tt + 4],
                                               wb[:, 0, tt, 0:T].rearrange("p (h e) -> p h e", e=ML_D), AX.X, ALU.add))
                    if a:
                        link(dve.memset(ms[:, 0:4 * a], 1.0))
                    link(dve.tensor_scalar(ms, ms, 1.0 / ML_D, EPS, ALU.mult, ALU.add))
                    dve.reciprocal(ms, ms).then_inc(v_mean, 1)
                    dve.wait_ge(a_root, 1)
                    dve.tensor_tensor(hv, hv, mv_.unsqueeze(2).to_broadcast([P, 4 * nt, ML_D]), ALU.mult).then_inc(v_hn, 1)
                    for b in range(2):
                        dve.wait_ge(ht_ps, b + 1)
                        dve.scalar_tensor_tensor(mix[:, 2 + b, t0:], bank[b][:, t0:], sm(f"ml_norm{l}"), mo[:, b, t0:],
                                                 ALU.mult, ALU.mult)
            A.at = conv_mark

            dv_tok = A.take(4, 4 * P)
            tmp = A.take(2, T)
            E = A.take(2, 2, 2 * T)
            pT = A.take(2, 2 * T)
            stats = A.take(2, 8)
            yd = A.take(DF_H, 2 * T)
            drs = A.take(2, 2 * T)
            dg = A.take(1)
            items = [(h, qt) for h in range(DF_H) for qt in (range(2, 4) if last else range(4))]
            with Phase("rot_ps", "v_rot", "rotated", "vt_ps", "a_vt", "sc_ps", "v_max", "a_exp", "v_p", "pt_ps",
                       "a_pt", "o_ps", "v_o", "a_sq", "norm_ps", "v_inv", "a_root", "v_chain", "v_p_rot", "v_chain2") as (
                    block, rot_ps, v_rot, rotated, vt_ps, a_vt, sc_ps, v_max, a_exp, v_p, pt_ps, a_pt, o_ps, v_o,
                    a_sq, norm_ps, v_inv, a_root, v_chain, v_p_rot, v_chain2):
                ax_t = A.take(2, T)
                qk = [dq[:, h, T:] for h in range(DF_H)] + [dk[:, h, T:] for h in range(DF_H)]
                keys_of = lambda qt: T if qt < 2 else 2 * T

                @block.sync
                def _(sp):
                    sp.dma_start(ax_t.rearrange("p a b -> p (a b)"), axial).then_inc(rotated, 16)
                    stream(sp, 0)

                @block.tensor
                def _(pe):
                    for n, q in enumerate(qk):
                        if n >= 2:
                            pe.wait_ge(v_rot, n - 1)
                        pe.matmul(bank[n % 2][:, 0:T], cc("rot"), q, start=True, stop=True).then_inc(rot_ps, 1)
                    for b in range(4):
                        if b >= 2:
                            pe.wait_ge(a_vt, b - 1)
                        for tt in range(4):
                            mm = pe.transpose(bank[2 + b % 2][:, tt * P:(tt + 1) * P], dv[:, b, tt * P:(tt + 1) * P], ident)
                        mm.then_inc(vt_ps, 1)
                    pe.wait_ge(v_p_rot, 8)
                    pe.wait_ge(a_vt, 4)

                    def scores(n):
                        h, qt = items[n]
                        if n >= 2:
                            pe.wait_ge(a_exp, 2 * (n - 1))
                        nk = keys_of(qt)
                        for s in range(2):
                            r = slice(64 * s, 64 * s + 64)
                            mm = pe.matmul(bank[2 * (n % 2) + s][:, 0:nk], dq[r, h, qt * P:(qt + 1) * P], dk[r, h, 0:nk],
                                           start=True, stop=True)
                        mm.then_inc(sc_ps, 1)

                    scores(0)
                    for n, (h, qt) in enumerate(items):
                        if n + 1 < len(items):
                            scores(n + 1)
                        nk = keys_of(qt)
                        pe.wait_ge(v_p, n + 1)
                        if n >= 2:
                            pe.wait_ge(a_pt, n - 1)
                        for k in range(nk // P):
                            mm = pe.transpose(bank[4 + n % 2][:, k * P:(k + 1) * P], E[:, n % 2, 0, k * P:(k + 1) * P], ident)
                        mm.then_inc(pt_ps, 1)
                        pe.wait_ge(a_pt, n + 1)
                        if n >= 2:
                            pe.wait_ge(v_o, n - 1)
                        for k in range(nk // P):
                            mm = pe.matmul(bank[6 + n % 2][:, 0:P], dv_tok[:, k, h * P:(h + 1) * P],
                                           pT[:, n % 2, k * P:(k + 1) * P], start=(k == 0), stop=(k == nk // P - 1))
                        mm.then_inc(o_ps, 1)
                    for h in range(DF_H):
                        pe.wait_ge(a_sq, h + 1)
                        if h >= 2:
                            pe.wait_ge(v_inv, h - 1)
                        pe.matmul(bank[h % 2][:, t0:], ones[:, :], E[:, h % 2, 1, t0:], start=True,
                                  stop=True).then_inc(norm_ps, 1)

                @block.scalar
                def _(act):
                    for b in range(4):
                        act.wait_ge(vt_ps, b + 1)
                        act.activation(dv_tok[:, :, b * P:(b + 1) * P],
                                       bank[2 + b % 2][:, :].rearrange("p (t c) -> p t c", t=4), ACT.Copy).then_inc(a_vt, 1)

                    def softmax(n):
                        nk = keys_of(items[n][1])
                        act.wait_ge(v_max, n + 1)
                        for s in range(2):
                            act.activation(E[:, n % 2, s, 0:nk], bank[2 * (n % 2) + s][:, 0:nk], ACT.Exp,
                                           bias=stats[:, n % 2, s:s + 1], scale=0.125,
                                           accum_out=stats[:, n % 2, 2 + s:3 + s]).then_inc(a_exp, 1)

                    softmax(0)
                    for n, (h, qt) in enumerate(items):
                        if n + 1 < len(items):
                            softmax(n + 1)
                        nk = keys_of(qt)
                        act.wait_ge(pt_ps, n + 1)
                        act.activation(pT[:, n % 2, 0:nk], bank[4 + n % 2][:, 0:nk], ACT.Copy).then_inc(a_pt, 1)
                    act.wait_ge(v_o, len(items))
                    for h in range(DF_H):
                        if h >= 2:
                            act.wait_ge(norm_ps, h - 1)
                        act.activation(E[:, h % 2, 1, t0:], yd[:, h, t0:], ACT.Square).then_inc(a_sq, 1)
                    for h in range(DF_H):
                        act.wait_ge(v_inv, h + 1)
                        act.activation(drs[:, h % 2, t0:], drs[:, h % 2, t0:], ACT.Sqrt).then_inc(a_root, 1)

                @block.vector
                def _(dve):
                    link = linker(dve, v_chain)
                    dve.wait_ge(rotated, 16)
                    for n, q in enumerate(qk):
                        dve.wait_ge(rot_ps, n + 1)
                        dve.tensor_tensor(tmp[:, n % 2, :], bank[n % 2][:, 0:T], ax_t[:, 1, :], ALU.mult).then_inc(v_rot, 1)
                        link(dve.tensor_tensor(q, q, ax_t[:, 0, :], ALU.mult))
                        dve.wait_ge(v_rot, n + 1)
                        dve.tensor_tensor(q, q, tmp[:, n % 2, :], ALU.add).then_inc(v_p_rot, 1)
                    dve.tensor_scalar(dg, sm(f"df_norm{l}"), 1.0 - lam_init, None, ALU.mult)

                    def maxima(n):
                        nk = keys_of(items[n][1])
                        st = stats[:, n % 2, :]
                        dve.wait_ge(sc_ps, n + 1)
                        for s in range(2):
                            w = dve.tensor_reduce(st[:, 4 + s:5 + s], bank[2 * (n % 2) + s][:, 0:nk], AX.X, ALU.max)
                        link(w)
                        dve.tensor_scalar(st[:, 0:2], st[:, 4:6], -0.125, None, ALU.mult).then_inc(v_max, 1)

                    def keep(n):
                        h, qt = items[n]
                        dve.wait_ge(o_ps, n + 1)
                        dve.tensor_copy(yd[:, h, qt * P:(qt + 1) * P], bank[6 + n % 2][:, 0:P]).then_inc(v_o, 1)

                    maxima(0)
                    for n, (h, qt) in enumerate(items):
                        nk = keys_of(qt)
                        st = stats[:, n % 2, :]
                        dve.wait_ge(a_exp, 2 * (n + 1))
                        link(dve.reciprocal(st[:, 6:8], st[:, 2:4]))
                        dve.tensor_tensor(st[:, 7:8], st[:, 7:8], nlam, ALU.mult).then_inc(v_chain2, 1)
                        link(dve.tensor_scalar(E[:, n % 2, 0, 0:nk], E[:, n % 2, 0, 0:nk], st[:, 6:7], None, ALU.mult))
                        dve.wait_ge(v_chain2, n + 1)
                        dve.scalar_tensor_tensor(E[:, n % 2, 0, 0:nk], E[:, n % 2, 1, 0:nk], st[:, 7:8],
                                                 E[:, n % 2, 0, 0:nk], ALU.mult, ALU.add).then_inc(v_p, 1)
                        if n + 1 < len(items):
                            maxima(n + 1)
                        if n:
                            keep(n - 1)
                    keep(len(items) - 1)
                    for h in range(DF_H):
                        dve.wait_ge(norm_ps, h + 1)
                        link(dve.tensor_scalar(drs[:, h % 2, t0:], bank[h % 2][:, t0:], 1.0 / P, EPS, ALU.mult, ALU.add))
                        dve.reciprocal(drs[:, h % 2, t0:], drs[:, h % 2, t0:]).then_inc(v_inv, 1)
                        dve.wait_ge(a_root, h + 1)
                        dve.scalar_tensor_tensor(mix[:, 4 + h, t0:], yd[:, h, t0:], dg, drs[:, h % 2, t0:],
                                                 ALU.mult, ALU.mult)
            A.at = mix_mark
            residual(8, lambda kt: mix[:, kt, t0:], gain=lambda d, s: mod[:, 16 + d, s:s + 1], streams=streams)
            A.at = layer_mark
            rms_phase(norm_jobs(gain2, 24, streams))

            R = [A.take(3, T) for _ in streams]
            peer_mark = A.at
            qT = A.take(PEER_H, 2 * T)
            KK = A.take(PEER_H, NK)
            n0 = used[0]
            with Phase("by_act", "keys_in") as (block, by_act, keys_in):
                @block.sync
                def _(sp):
                    sp.dma_start(KK.rearrange("p a b -> p (a b)"), keys2[l]).then_inc(keys_in, 16)
                    stream(sp, 8)
                    sp.wait_ge(keys_in, 16)

                @block.tensor
                def _(pe):
                    for b in range(8):
                        if b >= 4:
                            pe.wait_ge(by_act, b - 3)
                        product(pe, n0 + b, bank[b % 4][:, t0:],
                                lambda kt: H[:, kt, t0 // T:, :].rearrange("p s t -> p (s t)"))

                @block.scalar
                def _(act):
                    for b in range(8):
                        act.wait_ge(blocks_done, n0 + b + 1)
                        act.activation(qT[:, b, t0:], bank[b % 4][:, t0:], ACT.Copy).then_inc(by_act, 1)
            used[0] += 8

            S = A.take(16, NK)
            S2 = A.take(16, NK)
            best = A.take(16, TOPK)
            bidx = A.take(16, TOPK)
            bidx_u = A.take(16, TOPK).bitcast(U32)
            cand = A.take(PEER_H, 256)
            cand2 = A.take(PEER_H, 256)
            top = A.take(PEER_H, TOPK)
            pos_u = A.take(PEER_H, TOPK).bitcast(U32)
            half_u = A.take(2, PEER_H, TOPK).bitcast(U32)
            half = A.take(2, PEER_H, TOPK)
            found = A.take(3, PEER_H * TOPK)
            zsum = A.take(2, PEER_H)
            route = tiles
            with Phase("s_ps", "a_s", "v_read", "v_diff", "a_e", "v_found", "t_ps", "a_t", "v_chain") as (
                    block, s_ps, a_s, v_read, v_diff, a_e, v_found, t_ps, a_t, v_chain):
                @block.sync
                def _(sp):
                    stream(sp, 0)

                @block.tensor
                def _(pe):
                    def scores(n):
                        tt = route[n]
                        if n:
                            pe.wait_ge(a_s, 4 * n)
                        for h in range(PEER_H):
                            for s in range(2):
                                r = slice(64 * s, 64 * s + 64)
                                c = h % 4 * P
                                mm = pe.matmul(bank[2 * s + h // 4][:, c:c + P], qT[r, h, tt * P:(tt + 1) * P],
                                               KK[r, h, :], start=True, stop=True)
                            if h % 4 == 3:
                                mm.then_inc(s_ps, 1)

                    scores(0)
                    for n, tt in enumerate(route):
                        if n + 1 < len(route):
                            scores(n + 1)
                        pe.wait_ge(v_found, n + 1)
                        if n:
                            pe.wait_ge(a_t, n)
                        for i in range(3):
                            mm = pe.transpose(bank[4][:, i * P:(i + 1) * P], found[:, i, :], ident)
                        mm.then_inc(t_ps, 1)

                @block.scalar
                def _(act):
                    for n, tt in enumerate(route):
                        if n:
                            act.wait_ge(v_read, n)
                        for b in range(4):
                            act.wait_ge(s_ps, 2 * n + b % 2 + 1)
                            act.activation(S[:, 8 * (b % 2) + b // 2:8 * (b % 2) + 8:2, :],
                                           bank[b][:, :].rearrange("p (h n) -> p h n", h=4), ACT.Copy).then_inc(a_s, 1)
                        act.wait_ge(v_diff, n + 1)
                        act.activation(top, top, ACT.Exp).then_inc(a_e, 1)
                        act.wait_ge(t_ps, n + 1)
                        dst = R[tt // 2 if not last else 0]
                        act.activation(dst[:, :, (tt % 2) * P:(tt % 2 + 1) * P],
                                       bank[4][:, 0:384].rearrange("p (a b) -> p a b", a=3), ACT.Copy).then_inc(a_t, 1)

                @block.vector
                def _(dve):
                    link = linker(dve, v_chain)

                    def top16(n, src, scratch, val, idx):
                        for i in range(n):
                            w = dve.max(val(i)[:, 0:8], src(i))
                        link(w)
                        for i in range(n):
                            dve.max_index(idx(i)[:, 0:8], val(i)[:, 0:8], src(i))
                            w = dve.match_replace(scratch(i), val(i)[:, 0:8], src(i), -3.0e38)
                        link(w)
                        for i in range(n):
                            w = dve.max(val(i)[:, 8:16], scratch(i))
                        link(w)
                        for i in range(n):
                            w = dve.max_index(idx(i)[:, 8:16], val(i)[:, 8:16], scratch(i))
                        return w

                    for n, tt in enumerate(route):
                        dve.wait_ge(a_s, 4 * (n + 1))
                        top16(16, lambda i: S[:, i, :], lambda i: S2[:, i, :], lambda i: best[:, i, :],
                              lambda i: bidx_u[:, i, :]).then_inc(v_read, 1)
                        dve.wait_ge(v_read, n + 1)
                        dve.tensor_copy(bidx, bidx_u)
                        bh = best.rearrange("p (h s) k -> p h s k", s=2)
                        wide = [P, PEER_H, TOPK, TOPK]
                        c4 = cand.rearrange("p h (a b) -> p h a b", a=TOPK)
                        c24 = cand2.rearrange("p h (a b) -> p h a b", a=TOPK)
                        link(dve.tensor_tensor(c4, bh[:, :, 0, :].unsqueeze(3).to_broadcast(wide),
                                               bh[:, :, 1, :].unsqueeze(2).to_broadcast(wide), ALU.add))
                        link(top16(PEER_H, lambda i: cand[:, i, :], lambda i: cand2[:, i, :], lambda i: top[:, i, :],
                                   lambda i: pos_u[:, i, :]))
                        dve.tensor_scalar(half_u[:, 0, :, :], pos_u, 4, None, ALU.logical_shift_right)
                        link(dve.tensor_scalar(half_u[:, 1, :, :], pos_u, 15, None, ALU.bitwise_and))
                        link(dve.tensor_copy(half, half_u))
                        if n:
                            dve.wait_ge(t_ps, n)
                        ih = bidx.rearrange("p (h s) k -> p h s k", s=2)
                        for s in range(2):
                            link(dve.tensor_tensor(c4, half[:, s, :, :].unsqueeze(3).to_broadcast(wide),
                                                   cc("iota16").unsqueeze(1).unsqueeze(1).to_broadcast(wide), ALU.is_equal))
                            link(dve.tensor_tensor(c24, c4, ih[:, :, s, :].unsqueeze(2).to_broadcast(wide), ALU.mult))
                            link(dve.tensor_reduce(found[:, s, :].rearrange("p (h k) -> p h k", k=TOPK), c24, AX.X, ALU.add))
                        link(dve.tensor_copy(zsum[:, 1, :], top[:, :, 0]))
                        dve.tensor_tensor(top, top, zsum[:, 1, :].unsqueeze(2).to_broadcast([P, PEER_H, TOPK]),
                                          ALU.subtract).then_inc(v_diff, 1)
                        dve.wait_ge(a_e, n + 1)
                        link(dve.tensor_reduce(zsum[:, 0, :], top, AX.X, ALU.add))
                        link(dve.reciprocal(zsum[:, 0, :], zsum[:, 0, :]))
                        dve.tensor_tensor(found[:, 2, :].rearrange("p (h k) -> p h k", k=TOPK), top,
                                          zsum[:, 0, :].unsqueeze(2).to_broadcast([P, PEER_H, TOPK]),
                                          ALU.mult).then_inc(v_found, 1)

            for j, s in enumerate(streams):
                A.at = peer_mark
                G = A.take(NK, T)
                hotA = A.take(4, P)
                hotB = A.take(4, P)
                rows_, cols_, wts = (R[j][:, i, :] for i in range(3))
                with Phase("v_hot", "g_ps", "a_g") as (block, v_hot, g_ps, a_g):
                    @block.sync
                    def _(sp):
                        stream(sp, 0)

                    @block.vector
                    def _(dve):
                        def one_hots(t, u):
                            dve.tensor_scalar(hotA[:, u, :], cc("iota"), rows_[:, bass.ds(t, 1)], wts[:, bass.ds(t, 1)],
                                              ALU.is_equal, ALU.mult)
                            dve.tensor_scalar(hotB[:, u, :], cc("iota"), cols_[:, bass.ds(t, 1)], None,
                                              ALU.is_equal).then_inc(v_hot, 1)

                        for u in range(4):
                            one_hots(u, u)
                        with dve.Fori(1, T // 4) as it:
                            for u in range(4):
                                dve.wait_ge(g_ps, it * 4 + (u - 3))
                                one_hots(it * 4 + u, u)

                    @block.tensor
                    def _(pe):
                        def products(t, b, first=False):
                            for u in range(4):
                                pe.wait_ge(v_hot, t + (u + 1))
                                if u == 0 and not first:
                                    pe.wait_ge(a_g, group(t) - 3)
                                pe.matmul(bank[b][:, u * P:(u + 1) * P], hotA[:, u, :], hotB[:, u, :], start=True,
                                          stop=True).then_inc(g_ps, 1)

                        for g in range(4):
                            group = None
                            products(4 * g, g, first=True)
                        with pe.Fori(1, T // 16) as it:
                            for g in range(4):
                                group = lambda t, g=g: it * 4 + g
                                products(it * 16 + 4 * g, g)

                    @block.scalar
                    def _(act):
                        with act.Fori(0, T // 16) as it:
                            for g in range(4):
                                act.wait_ge(g_ps, it * 16 + (4 * g + 4))
                                act.activation(G[:, :, bass.ds(it * 16 + 4 * g, 4)].rearrange("p j t -> p t j"),
                                               bank[g][:, :].rearrange("p (t j) -> p t j", t=4), ACT.Copy).then_inc(a_g, 1)

                A.at = peer_mark + NK * T
                act_w = A.take(4, T)
                n0 = used[0]
                with Phase("a_gelu", "v_w") as (block, a_gelu, v_w):
                    @block.sync
                    def _(sp):
                        stream(sp, 2 * NK)

                    @block.tensor
                    def _(pe):
                        def up(n, b, it=None):
                            product(pe, n, bank[4 + b][:, 0:T], lambda kt: H[:, kt, s, :], it)

                        def down(n, b, it=None, start=False, stop=False):
                            arrived(pe, n, it)
                            for t in range(TT):
                                for c in range(2):
                                    mm = pe.matmul(bank[2 * t + c][:, :], act_w[:, b, t * P:(t + 1) * P],
                                                   ring[:, n % NS, c * 512:(c + 1) * 512], start=start, stop=stop)
                            mm.then_inc(blocks_done, 1)

                        up(n0, 0)
                        for c in range(3):
                            up(n0 + 1 + 2 * c, c + 1)
                            pe.wait_ge(v_w, c + 1)
                            down(n0 + 2 + 2 * c, c, start=(c == 0))
                        with pe.Fori(0, (NK - 4) // 4) as i4:
                            for u in range(4):
                                pe.wait_ge(a_gelu, i4 * 4 + (u + 1))
                                n = n0 + 7 + 2 * u
                                up(n, (4 + u) % 4, i4 * 2)
                                pe.wait_ge(v_w, i4 * 4 + (u + 4))
                                down(n + 1, (3 + u) % 4, i4 * 2)
                        pe.wait_ge(v_w, NK)
                        down(n0 + 2 * NK - 1, 3, stop=True)

                    @block.scalar
                    def _(act):
                        def gelu(b, done):
                            act.wait_ge(blocks_done, done)
                            act.activation(act_w[:, b, :], bank[4 + b][:, 0:T], ACT.Gelu).then_inc(a_gelu, 1)

                        gelu(0, n0 + 1)
                        for c in range(1, 4):
                            gelu(c, n0 + 2 * c)
                        with act.Fori(1, NK // 4) as i4:
                            for u in range(4):
                                gelu(u, i4 * 8 + (n0 + 2 * u))

                    @block.vector
                    def _(dve):
                        with dve.Fori(0, NK // 4) as i4:
                            for u in range(4):
                                dve.wait_ge(a_gelu, i4 * 4 + (u + 1))
                                dve.tensor_tensor(act_w[:, u, :], act_w[:, u, :],
                                                  G[:, bass.ds(i4 * 4 + u, 1), :].rearrange("p a t -> p (a t)"),
                                                  ALU.mult).then_inc(v_w, 1)
                used[0] += 2 * NK
                A.at = peer_mark
                y_tok = A.take(TT, D)
                with Phase("a_y", "t_ps", "v_x") as (block, a_y, t_ps, v_x):
                    @block.sync
                    def _(sp):
                        stream(sp, 0)

                    @block.scalar
                    def _(act):
                        for c in range(2):
                            for t in range(TT):
                                act.activation(y_tok[:, t, c * 512:(c + 1) * 512], bank[2 * t + c][:, :],
                                               ACT.Copy).then_inc(a_y, 1)

                    @block.tensor
                    def _(pe):
                        for b in range(8):
                            pe.wait_ge(a_y, 2 * (b // 4) + 2)
                            if b >= 4:
                                pe.wait_ge(v_x, b - 3)
                            for t in range(TT):
                                mm = pe.transpose(bank[4 + b % 4][:, t * P:(t + 1) * P], y_tok[:, t, b * P:(b + 1) * P], ident)
                            mm.then_inc(t_ps, 1)

                    @block.vector
                    def _(dve):
                        for b in range(8):
                            dve.wait_ge(t_ps, b + 1)
                            dve.scalar_tensor_tensor(X[:, b, s, :], bank[4 + b % 4][:, 0:T], mod[:, 40 + b, s:s + 1],
                                                     X[:, b, s, :], ALU.mult, ALU.add).then_inc(v_x, 1)

        A.at = 0
        rms_phase([(xl, hl, column("final_g"), None)])
        with Phase("stored") as (block, stored):
            @block.sync
            def _(sp):
                sp.dma_start(out, H[:, :, 1, :]).then_inc(stored, 16)
                sp.wait_ge(stored, 16)


def blocks(w):
    g, n = w.shape[0] // D, w.shape[1] // P
    return np.ascontiguousarray(w.reshape(g, KT, P, n, P).transpose(3, 0, 2, 1, 4).reshape(n * g, P, D))


def feature_columns(a):
    return a.reshape(-1, P).T


def streams_layout(ctx, x):
    return np.ascontiguousarray(np.stack([ctx, x]).reshape(2, T, KT, P).transpose(3, 2, 0, 1))


def lay_out(i):
    z = np.zeros
    sm = z((P, N_SMALL), np.float32)

    def put(name, a):
        o, n = SMALL[name]
        sm[:a.shape[0], o:o + n] = a.reshape(a.shape[0], n)

    fc = feature_columns
    put("norm_mix", fc(i["norm_mix"]))
    put("ssd_conv_w", fc(i["ssd_conv_w"]))
    put("ssd_conv_b", fc(i["ssd_conv_b"]))
    put("ssd_norm", fc(i["ssd_norm"]))
    put("ssd_d", fc(np.repeat(i["ssd_d"][0], SSD_P)))
    put("lru_conv_w", fc(i["lru_conv_w"]))
    put("lru_conv_b", fc(i["lru_conv_b"]))
    put("lru_b_a", fc(i["lru_b_a"]))
    put("lru_b_i", fc(i["lru_b_i"]))
    put("lru_lambda", fc(i["lru_lambda"]))
    put("norm_ffn", fc(i["norm_ffn"]))
    put("ffn_conv_w", fc(i["ffn_conv_w"]))
    put("ffn_conv_b", fc(i["ffn_conv_b"]))
    put("norm_final", fc(i["norm_final"]))
    put("final_g", fc(i["final_g_2"]))
    put("cond", np.stack([fc(i["c_ctx_2"]), fc(i["c_2"])], 2))
    put("dt_bias", i["ssd_dt_bias"].T)
    put("a_log", i["ssd_a_log"].T)
    w = i["w_in"][0]
    o = np.cumsum([0, D, D + 512, SSD_H, D, D, 512, 512, D, D, 3 * D])
    part = [w[:, a:b] for a, b in zip(o[:-1], o[1:])]
    put("w_dt", part[2].reshape(KT, P, SSD_H).transpose(1, 0, 2))
    d = {"x": streams_layout(i["ctx_2"][0], i["x"][0])}
    d["w_in1"] = blocks(np.concatenate([part[k] for k in (1, 4, 5, 6, 7, 0, 8, 3, 9)], 1))
    lru = [i[n][0].reshape(4, 2, P, 2, P).transpose(2, 0, 3, 1, 4).reshape(P, 2, D).transpose(1, 0, 2)
           for n in ("lru_w_a", "lru_w_i")]
    d["w_lru"] = np.ascontiguousarray(np.stack(lru, 1).reshape(4, P, D))
    d["w_br"] = np.concatenate([blocks(i["w_branch"][0, k]) for k in (2, 1, 0)])
    d["w_o1"] = blocks(i["w_o"][0])
    a, u = blocks(i["ffn_w_in"][0][:, :3 * D]), blocks(i["ffn_w_in"][0][:, 3 * D:])
    d["w_f1"] = np.ascontiguousarray(np.stack([a, u], 1).reshape(48, P, D))
    d["w_f2"] = blocks(i["ffn_w_out"][0])
    for l in range(LAYERS):
        put(f"ada_b{l}", fc(i["ada_b_2"][l]))
        put(f"norm1{l}", fc(i["norm1_g_2"][l]))
        put(f"norm2{l}", fc(i["norm2_g_2"][l]))
        put(f"conv_w{l}", fc(i["conv_w_2"][l]))
        put(f"conv_b{l}", fc(i["conv_b_2"][l]))
        put(f"ln_g{l}", fc(i["conv_ln_g_2"][l]))
        put(f"ln_b{l}", fc(i["conv_ln_b_2"][l]))
        gb = z((P, 1), np.float32)
        g = i["mlstm_gate_b_2"][l]
        gw = z((D, P), np.float32)
        mg = i["w_in_2"][l][:, 1536:1552]
        for row, k in ((0, 0), (64, 1), (32, 2), (96, 3)):
            gb[row:row + 4, 0] = g[k]
            gw[:, row:row + 4] = mg[:, 4 * k:4 * k + 4]
        put(f"gate_b{l}", gb)
        put(f"ml_norm{l}", fc(np.tile(i["mlstm_norm_g_2"][l], 2)))
        put(f"df_norm{l}", fc(i["diff_norm_g_2"][l]))
        put(f"lam{l}", np.broadcast_to(i["diff_lambda_2"][l].reshape(1, 256), (P, 256)))
        d[f"ada{l}"] = blocks(i["ada_w_2"][l])
        w = i["w_in_2"][l]
        order = [w[:, 256:512], w[:, 0:256], w[:, 1280:1536], w[:, 512:1280], w[:, 1552:3088]]
        d[f"w_in2_{l}"] = blocks(np.concatenate([gw] + order, 1))
        d[f"w_out2_{l}"] = blocks(i["w_out_2"][l])
        d[f"w_q2_{l}"] = blocks(i["peer_wq_2"][l])
        d[f"keys2_{l}"] = np.ascontiguousarray(i["peer_keys_2"][l].transpose(1, 3, 0, 2).reshape(P, PEER_H * NK))
        U = i["peer_u_2"][l].reshape(NK, NK, KT, P).transpose(1, 3, 2, 0).reshape(NK, P, D)
        V = i["peer_v_2"][l].reshape(NK, NK, D).transpose(1, 0, 2)
        uv = np.empty((2 * NK, P, D), np.float32)
        uv[0] = U[0]
        uv[1:-1:2] = U[1:]
        uv[2::2] = V[:-1]
        uv[-1] = V[-1]
        d[f"uv{l}"] = uv
    d["smalls"] = sm
    d.update(shape_tables())
    return d


def kernel(**inputs):
    import concourse.bacc as bacc
    from concourse.bass_utils import run_bass_kernel_spmd

    nc = bacc.Bacc("TRN2", target_bir_lowering=False, num_devices=1)
    arrays = lay_out({n: np.asarray(a) for n, a in inputs.items()})
    ap = {name: nc.dram_tensor("in_" + name, a.shape, mybir.dt.from_np(a.dtype), kind="ExternalInput").ap()
          for name, a in arrays.items()}
    out = nc.dram_tensor("out_0", (P, KT, T), F32, kind="ExternalOutput").ap()
    pair = lambda n: [ap[f"{n}{l}"] for l in range(LAYERS)]
    build(nc, ap["x"], ap["smalls"], ap["consts"], ap["tables"], ap["axial"], ap["w_in1"], ap["w_lru"], ap["w_br"],
          ap["w_o1"], ap["w_f1"], ap["w_f2"], pair("ada"), pair("w_in2_"), pair("w_out2_"), pair("w_q2_"),
          pair("keys2_"), pair("uv"), out)
    r = run_bass_kernel_spmd(nc, [{"in_" + n: a for n, a in arrays.items()}], core_ids=[0])
    return r.results[0]["out_0"].transpose(2, 1, 0).reshape(1, T, D)
```

```python
import math
from contextlib import ExitStack

import numpy as np

import concourse.bass as bass
from concourse import mybir

F32 = mybir.dt.float32
F32R = mybir.dt.float32r
U32 = mybir.dt.uint32
ALU = mybir.AluOpType
ACT = mybir.ActivationFunctionType
AX = mybir.AxisListType

P = 128
D = 1024
KT = D // P
T = 256
TT = T // P
EPS = 1e-6
NS = 4
NH = 3
SLOT = D

FFN_T = 3 * D // P
SSD_H, SSD_P = 16, 64
RET_H = 4
LRU_O = 8
ML_H, ML_D = 4, 64
DF_H = 4
CONV_K = 31
PEER_H, TOPK, NK = 8, 16, 128
LAYERS = 2


def small_columns():
    cols = {}
    at = 0

    def add(name, n):
        nonlocal at
        cols[name] = (at, n)
        at += n

    for name, n in (("norm_mix", 8), ("ssd_conv_w", 48), ("ssd_conv_b", 12), ("ssd_norm", 8), ("ssd_d", 8),
                    ("lru_conv_w", 32), ("lru_conv_b", 8), ("lru_b_a", 8), ("lru_b_i", 8), ("lru_lambda", 8),
                    ("norm_ffn", 8), ("ffn_conv_w", 72), ("ffn_conv_b", 24), ("norm_final", 8), ("final_g", 8),
                    ("cond", 16), ("dt_bias", 1), ("a_log", 1)):
        add(name, n)
    for l in range(LAYERS):
        for name, n in (("ada_b", 48), ("norm1", 8), ("norm2", 8), ("conv_w", 2 * CONV_K), ("conv_b", 2),
                        ("ln_g", 2), ("ln_b", 2), ("gate_b", 1), ("ml_norm", 1), ("df_norm", 1), ("lam", 256)):
            add(f"{name}{l}", n)
    return cols, at


SMALL, N_SMALL = small_columns()


def const_columns():
    cols = {}
    at = 0
    for name, n in (("ident", P), ("iota", P), ("iota16", 16)):
        cols[name] = (at, n)
        at += n
    return cols, at


CONST, N_CONST = const_columns()
MIX = {"rot": (0, P), "causal": (P, 384), "anti": (512, P), "selm": (640, ML_H * P)}
N_MIX = 640 + ML_H * P
TABLE = {"sel": (0, SSD_H * P), "ret_cos": (2048, T), "ret_sin": (2304, T), "retk_cos": (2560, T),
         "retk_sin": (2816, T), "ret_mask": (3072, RET_H * 384)}
N_TABLE = 3072 + RET_H * 384


def shape_tables():
    f = np.float32
    c = np.zeros((P, N_CONST), f)
    t = np.zeros((P, N_TABLE), f)
    m = np.zeros((P, N_MIX), f)

    def put(a, cols, name, v):
        o, n = cols[name]
        a[:v.shape[0], o:o + n] = v.reshape(v.shape[0], n)

    i = np.arange(P)
    put(c, CONST, "ident", np.eye(P, dtype=f))
    put(c, CONST, "iota", np.tile(i.astype(f), (P, 1)))
    rot = np.zeros((P, P), f)
    rot[i[1::2], i[0::2]] = -1.0
    rot[i[0::2], i[1::2]] = 1.0
    put(m, MIX, "rot", rot)
    tri = (i[None, :] >= i[:, None]).astype(f)
    put(m, MIX, "causal", np.concatenate([tri, np.ones((P, P), f), tri], 1))
    put(m, MIX, "anti", (i[None, :] <= i[:, None]).astype(f))
    selm = np.zeros((36, ML_H, P), f)
    for r in range(ML_H):
        selm[r, r] = 1.0
        selm[32 + r, r] = 1.0
    put(m, MIX, "selm", selm)
    put(c, CONST, "iota16", np.tile(np.arange(16, dtype=f), (P, 1)))

    sel = np.zeros((SSD_H, SSD_H, P), f)
    for h in range(SSD_H):
        sel[h, h] = 1.0
    put(t, TABLE, "sel", sel)
    inv = (f(1.0) / (f(10000.0) ** np.linspace(0.0, 1.0, 64, dtype=f))).astype(f)
    ang = (np.arange(T, dtype=f)[:, None] * inv[None]).astype(f).T
    cos, sin = np.repeat(np.cos(ang), 2, 0), np.repeat(np.sin(ang), 2, 0)
    k_scale = f(P ** -0.5)
    put(t, TABLE, "ret_cos", cos)
    put(t, TABLE, "ret_sin", sin)
    put(t, TABLE, "retk_cos", cos * k_scale)
    put(t, TABLE, "retk_sin", sin * k_scale)
    gamma = np.log(1.0 - np.exp2(-5.0 - np.arange(RET_H)))
    s, l = i[:, None], np.arange(T)[None]
    full = np.stack([np.where(l >= s, np.exp(np.maximum(l - s, 0) * g), 0.0) for g in gamma], 1)
    put(t, TABLE, "ret_mask", np.concatenate([full, full[:, :, :P]], 2).astype(f))

    n = np.arange(T)
    inv = (10000.0 ** (-np.arange(0, 32, 2, dtype=f) / f(32))).astype(f)
    ang = np.concatenate([(n // 64).astype(f)[:, None] * inv, (n % 64).astype(f)[:, None] * inv], -1).T
    rope = np.stack([np.tile(np.repeat(np.cos(ang), 2, 0), (2, 1)), np.tile(np.repeat(np.sin(ang), 2, 0), (2, 1))], 1)
    return {"consts": c, "mix_tables": m, "tables": t, "axial": rope.astype(f).reshape(P, 2 * T)}


class Space:

    def __init__(self, tensor, size):
        self.tensor, self.size, self.at = tensor, size, 0

    def take(self, *shape):
        n = int(np.prod(shape))
        assert self.at + n <= self.size, (self.at, n, self.size)
        ap = self.tensor[:, self.at:self.at + n]
        self.at += n
        if len(shape) == 2:
            return ap.rearrange("p (a b) -> p a b", b=shape[1])
        if len(shape) == 3:
            return ap.rearrange("p (a b c) -> p a b c", b=shape[1], c=shape[2])
        return ap


def linker(eng, sem):
    n = [0]

    def link(ins):
        n[0] += 1
        ins.then_inc(sem, 1)
        eng.wait_ge(sem, n[0])

    return link


def build(nc, x, smalls, consts, mix_tables, tables, axial, w_in1, w_lru, w_br, w_o1, w_f1, w_f2, ada, w_in2,
          w_out2, w_q2, keys2, uv, out):
    ctx = ExitStack()
    with ctx:
        def sb(name, shape):
            return ctx.enter_context(nc.sbuf_tensor(name, shape, F32))

        def pair_of(name, shape):
            at = (nc.sbuf_base + 31) // 32 * 32
            return sb(name, shape), nc.alloc_sbuf_tensor_at(name + "_r", shape, F32R, offset=at)

        ring, ring_lo = pair_of("ring", [P, NS, SLOT])
        ring_hi = ctx.enter_context(nc.sbuf_tensor("ring_hi", [P, NH, SLOT], F32R))
        X = sb("X", [P, KT, 2, T])
        H, H_r = pair_of("H", [P, KT, 2, T])
        spill = nc.dram_tensor("spill", (P, KT, T), F32, kind="Internal").ap()
        CS = sb("CS", [P, N_CONST])
        SM = sb("SM", [P, N_SMALL])
        ones = sb("ones", [P, P])
        n_arena = 36100
        MODS = sb("MODS", [P, LAYERS, 48, 2])
        cond = sb("cond", [P, KT, 2])
        arena_at = (nc.sbuf_base + 31) // 32 * 32
        arena = sb("arena", [P, n_arena])
        bank = [ctx.enter_context(nc.psum_tensor(f"bank{i}", [P, 512], F32)) for i in range(8)]
        w_ready = [ctx.enter_context(nc.semaphore(f"w_ready{i}")) for i in range(NS)]
        blocks_done = ctx.enter_context(nc.semaphore("blocks_done"))

        def cc(name):
            o, n = CONST[name]
            return CS[:, o:o + n]

        def sm(name):
            o, n = SMALL[name]
            return SM[:, o:o + n]

        def mx(name):
            o, n = MIX[name]
            return MT[:, o:o + n]

        ident = cc("ident")

        order = []
        order += [(w_in1, i) for i in range(85)]
        order += [(ada[0], i) for i in range(48)]
        order += [(w_lru, i) for i in (0, 1)] + [(ada[1], i) for i in range(12)]
        order += [(w_lru, i) for i in (2, 3)] + [(ada[1], i) for i in range(12, 24)]
        order += [(ada[1], i) for i in range(24, 48)]
        order += [(w_br, i) for i in range(24)]
        order += [(w_o1, i) for i in range(8)]
        order += [(w_f1, i) for i in range(48)]
        order += [(w_f2, i) for i in range(24)]
        for l in range(LAYERS):
            order += [(w_in2[l], i) for i in range(25)]
            order += [(w_out2[l], i) for i in range(8)]
            order += [(w_q2[l], i) for i in range(8)]
            for _ in range(2 if l == 0 else 1):
                order += [(uv[l], i) for i in range(2 * NK)]
        issued = [0]
        used = [0]

        def stream(sp, count):
            end = min(used[0] + count + NS, len(order))
            n = issued[0]
            while n < end:
                w, i = order[n]
                run = 1
                while n + run < end and order[n + run][0] is w and order[n + run][1] == i + run:
                    run += 1
                if n >= NS and run >= 4 * NS:
                    times = run // NS
                    with sp.Fori(0, times) as it:
                        for u in range(NS):
                            sp.wait_ge(blocks_done, it * NS + (n + u - NS + 1))
                            sp.dma_start(ring[:, (n + u) % NS, :], w[it * NS + (i + u)]).then_inc(w_ready[(n + u) % NS], 16)
                    n += times * NS
                else:
                    if n >= NS:
                        sp.wait_ge(blocks_done, n - NS + 1)
                    sp.dma_start(ring[:, n % NS, :], w[i]).then_inc(w_ready[n % NS], 16)
                    n += 1
            issued[0] = n

        def arrived(pe, n, it=None):
            value = 16 * (n // NS + 1)
            pe.wait_ge(w_ready[n % NS], value if it is None else it * 16 + value)

        def col(n, kt, width=P):
            return ring[:, n % NS, kt * width:(kt + 1) * width]

        def product(pe, n, out_ap, rhs, it=None):
            arrived(pe, n, it)
            for kt in range(KT):
                mm = pe.matmul(out_ap, col(n, kt), rhs(kt), start=(kt == 0), stop=(kt == KT - 1))
            mm.then_inc(blocks_done, 1)

        def high(act, n0, m, a_hi):
            arrived(act, n0 + m)
            if m >= NH:
                act.wait_ge(blocks_done, n0 + m - NH + 1)
            act.activation(ring_hi[:, m % NH, :], ring[:, (n0 + m) % NS, :], ACT.Copy).then_inc(a_hi, 1)

        def low(eng, n0, m, a_hi, lows):
            slot = (n0 + m) % NS
            eng.wait_ge(a_hi, m + 1)
            eng.tensor_tensor(ring_lo[:, slot, :], ring[:, slot, :], ring_hi[:, m % NH, :].bitcast(F32),
                              ALU.subtract).then_inc(lows, 1)

        def product3(pe, n0, m, lows, o, x_hi, x_lo):
            pe.wait_ge(lows, m + 1)
            hi, lo = ring_hi[:, m % NH, :], ring_lo[:, (n0 + m) % NS, :]
            for kt in range(KT):
                k = slice(kt * P, (kt + 1) * P)
                pe.matmul(o, hi[:, k], x_hi(kt), start=(kt == 0), stop=False)
                pe.matmul(o, hi[:, k], x_lo(kt), start=False, stop=False)
                mm = pe.matmul(o, lo[:, k], x_hi(kt), start=False, stop=(kt == KT - 1))
            mm.then_inc(blocks_done, 1)

        def turn(pe, k, rows_, o, kept, turned):
            pe.wait_ge(kept, k + 1)
            for j in range(4):
                mm = pe.transpose(o[:, 8 * k + 2 * j:8 * k + 2 * j + 2], rows_[0:2, k % 2, j * P:(j + 1) * P], ident[0:2, 0:2])
            mm.then_inc(turned, 1)

        def modulate(pe, n, k, acc, rows_, o, kept, turned):
            if k >= len(acc):
                pe.wait_ge(kept, k - len(acc) + 1)
            for g in range(4):
                arrived(pe, n + g)
                for e in range(2):
                    mm = pe.matmul(acc[k % len(acc)][0:2, :], cond[:, 2 * g + e, :], ring[:, (n + g) % NS, e * 512:(e + 1) * 512],
                                   start=(g == e == 0), stop=(g == 3 and e == 1))
                mm.then_inc(blocks_done, 1)
            if k:
                turn(pe, k - 1, rows_, o, kept, turned)

        def keep_row(eng, n, k, acc, rows_, kept, turned):
            eng.wait_ge(blocks_done, n + 4)
            if k >= 2:
                eng.wait_ge(turned, k - 1)
            dst, src = rows_[0:2, k % 2, :], acc[k % len(acc)][0:2, :]
            copy = eng.activation(dst, src, ACT.Copy) if eng is nc.scalar else eng.tensor_copy(dst, src)
            copy.then_inc(kept, 1)

        def keep_modulation(dve, l, o, first, count):
            dve.tensor_tensor(MODS[:, l, first:first + count, :], o[:, 0:2 * count].rearrange("p (a b) -> p a b", b=2),
                              sm(f"ada_b{l}")[:, first:first + count].unsqueeze(2).to_broadcast([P, count, 2]), ALU.add)

        class Phase:

            def __init__(self, *names):
                self.names = names

            def __enter__(self):
                self.sems = [nc.alloc_semaphore(n) for n in self.names]
                self.block = nc.Block()
                return (self.block.__enter__(), *self.sems)

            def __exit__(self, *e):
                self.block.__exit__(*e)
                for s in self.sems:
                    nc.gpsimd.sem_clear(s)
                    nc.release_semaphore(s)

        def evac_wait(pe, sems, evac, b, lag):
            if b >= lag:
                who = evac[b - lag]
                pe.wait_ge(sems[who], evac[:b - lag + 1].count(who))

        def rms_phase(jobs, parts=None):
            with Phase("squares", "sums", "inverse", "roots", "v_chain", "normed", "shifted", "highs") as (
                    block, squares, sums, inverse, roots, v_chain, normed, shifted, highs):
                mark = A.at
                sq = A.take(2, KT, T)
                rs = A.take(2, T)

                @block.sync
                def _(sp):
                    stream(sp, 0)

                @block.scalar
                def _(act):
                    for j, (src, dst, gain, shift) in enumerate(jobs):
                        if j >= 2:
                            act.wait_ge(sums, j - 1)
                        for kt in range(KT):
                            act.activation(sq[:, j % 2, kt, :], src(kt), ACT.Square).then_inc(squares, 1)
                    for j in range(len(jobs)):
                        act.wait_ge(inverse, j + 1)
                        act.activation(rs[:, j % 2, :], rs[:, j % 2, :], ACT.Sqrt).then_inc(roots, 1)
                        if parts is not None:
                            for kt in range(KT):
                                act.wait_ge(normed if jobs[j][3] is None else shifted, KT * j + kt + 1)
                                act.activation(parts(j, kt)[0], jobs[j][1](kt), ACT.Copy).then_inc(highs, 1)

                @block.tensor
                def _(pe):
                    for j in range(len(jobs)):
                        for kt in range(KT):
                            pe.wait_ge(squares, KT * j + kt + 1)
                            mm = pe.matmul(bank[j % 4][:, 0:T], ones[:, :], sq[:, j % 2, kt, :],
                                           start=(kt == 0), stop=(kt == KT - 1))
                        mm.then_inc(sums, 1)

                @block.vector
                def _(dve):
                    link = linker(dve, v_chain)
                    for j, (src, dst, gain, shift) in enumerate(jobs):
                        dve.wait_ge(sums, j + 1)
                        link(dve.tensor_scalar(rs[:, j % 2, :], bank[j % 4][:, 0:T], 1.0 / D, EPS, ALU.mult, ALU.add))
                        dve.reciprocal(rs[:, j % 2, :], rs[:, j % 2, :]).then_inc(inverse, 1)
                        dve.wait_ge(roots, j + 1)
                        for kt in range(KT):
                            dve.scalar_tensor_tensor(dst(kt), src(kt), gain(kt), rs[:, j % 2, :],
                                                     ALU.mult, ALU.mult).then_inc(normed, 1)
                        if shift is not None:
                            dve.wait_ge(normed, KT * (j + 1))
                            for kt in range(KT):
                                dve.tensor_scalar(dst(kt), dst(kt), shift(kt), None, ALU.add).then_inc(shifted, 1)
                        if parts is not None:
                            for kt in range(KT):
                                dve.wait_ge(highs, KT * j + kt + 1)
                                hi, lo = parts(j, kt)
                                dve.tensor_tensor(lo, dst(kt), hi.bitcast(F32), ALU.subtract)
                A.at = mark

        A = Space(arena, n_arena)

        with Phase("loaded") as (block, loaded):
            @block.sync
            def _(sp):
                sp.dma_start(CS[:, :], consts).then_inc(loaded, 16)
                sp.dma_start(SM[:, :], smalls).then_inc(loaded, 16)
                sp.dma_start(X[:, :, :, :], x).then_inc(loaded, 16)
                stream(sp, 0)
                sp.wait_ge(loaded, 48)

            @block.vector
            def _(dve):
                dve.memset(ones[:, :], 1.0)

        def xl(kt):
            return X[:, kt, 1, :]

        def hl(kt):
            return H[:, kt, 1, :]

        def column(name, first=0):
            return lambda kt: sm(name)[:, first + kt:first + kt + 1]

        def h_hi(kt):
            return H_r[:, kt, 0, :]

        def h_lo(kt):
            return H_r[:, kt, 1, :]

        rms_phase([(xl, hl, column("norm_mix"), None)], lambda j, kt: (h_hi(kt), h_lo(kt)))

        MT = A.take(N_MIX)
        TB = A.take(N_TABLE)

        def table(name):
            o, n = TABLE[name]
            return TB[:, o:o + n]

        xbc = A.take(12, T)
        xl_conv = A.take(8, T)
        q_ret = A.take(RET_H, T)
        k_ret = A.take(RET_H, T)
        v_ret = A.take(8, T)
        z_gate = A.take(8, T)
        y_gate = A.take(8, T)
        g_gate = A.take(8, T)
        gates = A.take(24, T)
        dtT = A.take(T)[0:SSD_H]
        acsT = A.take(T)[0:SSD_H]
        negA = A.take(1)[0:SSD_H]
        one_row = A.take(T)[0:SSD_H]
        mixer_mark = A.at

        kinds = [("dt", None, 0)] + [("conv", xbc, i) for i in range(12)] + [("conv", xl_conv, i) for i in range(8)]
        kinds += [(ACT.Copy, q_ret, i) for i in range(4)] + [(ACT.Copy, k_ret, i) for i in range(4)]
        kinds += [(ACT.Copy, v_ret, i) for i in range(8)] + [(ACT.Silu, z_gate, i) for i in range(8)]
        kinds += [(ACT.Silu, g_gate, i) for i in range(8)]
        kinds += [(ACT.Gelu_apprx_tanh, y_gate, i) for i in range(8)]
        kinds += [(ACT.Sigmoid, gates, i) for i in range(24)]
        evac = ["dve" if isinstance(k[0], str) else "act" for k in kinds]
        n0 = used[0]
        with Phase("tables_in", "by_act", "by_dve", "a_chain", "v_chain", "dt_soft", "a_hi", "p_lo") as (
                block, tables_in, by_act, by_dve, a_chain, v_chain, dt_soft, a_hi, p_lo):
            sems = {"act": by_act, "dve": by_dve}

            @block.sync
            def _(sp):
                sp.dma_start(TB, tables).then_inc(tables_in, 16)
                sp.dma_start(MT, mix_tables).then_inc(tables_in, 16)
                stream(sp, 85)
                sp.wait_ge(tables_in, 32)

            @block.tensor
            def _(pe):
                for b in range(85):
                    evac_wait(pe, sems, evac, b, 4)
                    product3(pe, n0, b, p_lo, bank[b % 4][:, 0:T], h_hi, h_lo)

            @block.gpsimd
            def _(pool):
                for b in range(85):
                    low(pool, n0, b, a_hi, p_lo)

            @block.vector
            def _(dve):
                link = linker(dve, v_chain)
                link(dve.memset(one_row, 1.0))
                dve.wait_ge(blocks_done, n0 + 1)
                dve.tensor_scalar(dtT, bank[0][0:SSD_H, 0:T], sm("dt_bias")[0:SSD_H], None, ALU.add).then_inc(by_dve, 1)
                for b in range(1, 21):
                    _, dst, i = kinds[b]
                    w, bias, nb = (("ssd_conv_w", "ssd_conv_b", 12) if dst is xbc else ("lru_conv_w", "lru_conv_b", 8))
                    y, ps = dst[:, i, :], bank[b % 4]
                    dve.wait_ge(blocks_done, n0 + b + 1)
                    link(dve.tensor_scalar(y, ps[:, 0:T], sm(w)[:, 3 * nb + i:3 * nb + i + 1],
                                           sm(bias)[:, i:i + 1], ALU.mult, ALU.add))
                    for j in range(1, 4):
                        tap = sm(w)[:, (3 - j) * nb + i:(3 - j) * nb + i + 1]
                        ins = dve.scalar_tensor_tensor(y[:, j:], ps[:, 0:T - j], tap, y[:, j:], ALU.mult, ALU.add)
                        if j < 3:
                            link(ins)
                    ins.then_inc(by_dve, 1)
                dve.wait_ge(dt_soft, 1)
                link(dve.scalar_tensor_tensor(dtT, dtT, 0.0, acsT, ALU.max, ALU.add))
                link(dve.tensor_scalar(acsT, dtT, negA, -1.0, ALU.mult, ALU.mult))
                dve.tensor_tensor_scan(acsT, one_row, acsT, 0.0, ALU.mult, ALU.add)

            @block.scalar
            def _(act):
                link = linker(act, a_chain)
                for m in range(NH):
                    high(act, n0, m, a_hi)
                act.wait_ge(by_dve, 1)
                link(act.activation(acsT, dtT, ACT.Abs))
                link(act.activation(acsT, acsT, ACT.Exp, scale=-1.0))
                act.activation(negA, sm("a_log")[0:SSD_H], ACT.Exp)
                act.activation(acsT, acsT, ACT.Ln, bias=1.0).then_inc(dt_soft, 1)
                for b in range(85):
                    f, dst, i = kinds[b]
                    if b == 37:
                        act.activation(cond[:, :, :].rearrange("p a b -> p (a b)"), sm("cond"), ACT.Silu)
                        for c in range(12):
                            act.wait_ge(by_dve, c + 2)
                            act.activation(xbc[:, c, :], xbc[:, c, :], ACT.Silu)
                    if evac[b] == "act":
                        act.wait_ge(blocks_done, n0 + b + 1)
                        act.activation(dst[:, i, :], bank[b % 4][:, 0:T], f).then_inc(by_act, 1)
                    if b + NH < 85:
                        high(act, n0, b + NH, a_hi)
        used[0] += 85

        A.at = mixer_mark
        xs_tok = A.take(TT, D)
        cb = A.take(2, 384)
        seg = A.take(2, 384)
        dt_tok = A.take(TT, SSD_H)
        nacs = A.take(TT, SSD_H)
        y_tok = A.take(TT, D)
        ada_rows = H[:, 0:2, :, :].rearrange("p k s t -> p k (s t)")
        n0 = used[0]
        with Phase("small_t", "xs_t", "cb_ps", "bc_ps", "y_ps", "yt_ps", "v_small", "v_xs", "v_cb", "v_seg",
                   "a_exp", "v_m", "v_ytok", "v_y", "v_chain", "a_ytok", "kept", "turned") as (
                block, small_t, xs_t, cb_ps, bc_ps, y_ps, yt_ps, v_small, v_xs, v_cb, v_seg, a_exp, v_m, v_ytok, v_y,
                v_chain, a_ytok, kept, turned):
            @block.sync
            def _(sp):
                stream(sp, 48)

            @block.tensor
            def _(pe):
                for src, o in ((dtT, 0), (acsT, TT * SSD_H)):
                    for t in range(TT):
                        mm = pe.transpose(bank[4][:, o + t * SSD_H:o + (t + 1) * SSD_H], src[:, t * P:(t + 1) * P],
                                          ident[0:SSD_H, 0:SSD_H])
                mm.then_inc(small_t, 1)
                for t in range(TT):
                    for b in range(8):
                        mm = pe.transpose(bank[2 * t + b // 4][:, (b % 4) * P:(b % 4 + 1) * P],
                                          xbc[:, b, t * P:(t + 1) * P], ident)
                    mm.then_inc(xs_t, 1)
                for g in range(2):
                    pe.matmul(bank[5 + g][:, 0:T], xbc[:, 8 + g, 0:P], xbc[:, 10 + g, :], start=True, stop=True)
                    pe.matmul(bank[5 + g][:, T:384], xbc[:, 8 + g, P:T], xbc[:, 10 + g, P:T],
                              start=True, stop=True).then_inc(cb_ps, 1)
                pe.wait_ge(v_xs, 4)
                pe.wait_ge(v_small, 2)

                def broadcast(h):
                    if h >= 2:
                        pe.wait_ge(v_seg, h - 1)
                    pe.matmul(bank[4 + 3 * (h % 2)][:, 0:T], table("sel")[0:SSD_H, h * P:(h + 1) * P], acsT,
                              start=True, stop=True).then_inc(bc_ps, 1)

                broadcast(0)
                for h in range(SSD_H):
                    if h + 1 < SSD_H:
                        broadcast(h + 1)
                    if h == 0:
                        pe.wait_ge(v_cb, 2)
                    if h < 12:
                        modulate(pe, n0 + 4 * h, h, [bank[5]], ada_rows, bank[6], kept, turned)
                    elif h == 12:
                        turn(pe, 11, ada_rows, bank[6], kept, turned)
                    pe.wait_ge(v_m, h + 1)
                    M = seg[:, h % 2, :]
                    c = slice((h % 8) * SSD_P, (h % 8 + 1) * SSD_P)
                    xh = slice(h * SSD_P, (h + 1) * SSD_P)
                    pe.matmul(bank[h // 8][:, c], M[:, 0:P], xs_tok[:, 0, xh], start=True, stop=True)
                    pe.matmul(bank[2 + h // 8][:, c], M[:, P:T], xs_tok[:, 0, xh], start=True, stop=False)
                    pe.matmul(bank[2 + h // 8][:, c], M[:, T:384], xs_tok[:, 1, xh], start=False,
                              stop=True).then_inc(y_ps, 1)
                for b in range(8):
                    if b >= 2:
                        pe.wait_ge(v_y, b - 1)
                    pe.wait_ge(a_ytok, 4)
                    for t in range(TT):
                        mm = pe.transpose(bank[4 + 3 * (b % 2)][:, t * P:(t + 1) * P],
                                          y_tok[:, t, b * P:(b + 1) * P], ident)
                    mm.then_inc(yt_ps, 1)

            @block.scalar
            def _(act):
                for h in range(SSD_H):
                    if 2 <= h < 14:
                        keep_row(act, n0 + 4 * (h - 2), h - 2, [bank[5]], ada_rows, kept, turned)
                    act.wait_ge(v_seg, h + 1)
                    act.activation(seg[:, h % 2, :], seg[:, h % 2, :], ACT.Exp).then_inc(a_exp, 1)
                act.wait_ge(y_ps, SSD_H)
                for t in range(TT):
                    for c in range(2):
                        act.activation(y_tok[:, t, c * 512:(c + 1) * 512], bank[2 * t + c][:, :],
                                       ACT.Copy).then_inc(a_ytok, 1)

            @block.vector
            def _(dve):
                link = linker(dve, v_chain)
                dve.wait_ge(small_t, 1)
                dve.tensor_copy(dt_tok.rearrange("p a b -> p (a b)"), bank[4][:, 0:32]).then_inc(v_small, 1)
                dve.tensor_scalar(nacs.rearrange("p a b -> p (a b)"), bank[4][:, 32:64], -1.0, None,
                                  ALU.mult).then_inc(v_small, 1)
                dve.wait_ge(v_small, 2)
                for t in range(TT):
                    dve.wait_ge(xs_t, t + 1)
                    for c in range(2):
                        dve.tensor_tensor(
                            xs_tok[:, t, c * 512:(c + 1) * 512].rearrange("p (h e) -> p h e", e=SSD_P),
                            bank[2 * t + c][:, :].rearrange("p (h e) -> p h e", e=SSD_P),
                            dt_tok[:, t, c * 8:(c + 1) * 8].unsqueeze(2).to_broadcast([P, 8, SSD_P]),
                            ALU.mult).then_inc(v_xs, 1)
                for g in range(2):
                    dve.wait_ge(cb_ps, g + 1)
                    dve.tensor_tensor(cb[:, g, :], bank[5 + g][:, 0:384], mx("causal"), ALU.mult).then_inc(v_cb, 1)
                dve.wait_ge(v_cb, 2)

                def segment(h):
                    dve.wait_ge(bc_ps, h + 1)
                    if h >= 2:
                        dve.wait_ge(y_ps, h - 1)
                    ps = bank[4 + 3 * (h % 2)]
                    dve.tensor_scalar(seg[:, h % 2, 0:T], ps[:, 0:T], nacs[:, 0, h:h + 1], 0.0, ALU.add, ALU.min)
                    dve.tensor_scalar(seg[:, h % 2, T:384], ps[:, P:T], nacs[:, 1, h:h + 1], 0.0, ALU.add,
                                      ALU.min).then_inc(v_seg, 1)

                segment(0)
                for h in range(SSD_H):
                    if h + 1 < SSD_H:
                        segment(h + 1)
                    dve.wait_ge(a_exp, h + 1)
                    dve.tensor_tensor(seg[:, h % 2, :], seg[:, h % 2, :], cb[:, h // 8, :], ALU.mult).then_inc(v_m, 1)
                for b in range(8):
                    dve.wait_ge(yt_ps, b + 1)
                    dve.scalar_tensor_tensor(xbc[:, b, :], xbc[:, b, :], sm("ssd_d")[:, b:b + 1],
                                             bank[4 + 3 * (b % 2)][:, 0:T], ALU.mult, ALU.add).then_inc(v_y, 1)
                dve.wait_ge(turned, 12)
                keep_modulation(dve, 0, bank[6], 0, 48)
                dve.wait_ge(v_y, 8)
                dve.tensor_tensor(xbc[:, 0:8, :], xbc[:, 0:8, :], z_gate, ALU.mult)
        used[0] += 48

        y_ssd = xbc
        A.at = mixer_mark
        rms_phase([(lambda kt: xbc[:, kt, :], lambda kt: xbc[:, kt, :], column("ssd_norm"), None)])

        A.at = mixer_mark
        r_g = A.take(8, T)
        i_g = A.take(8, T)
        sp_l = A.take(3, 8)
        n0 = used[0]
        with Phase("v_c", "a_lam", "v_r", "a_r", "a_sp", "v_sp", "gates_ps", "a_gates", "a_exp", "v_u2",
                   "a_sqrt", "v_u", "v_scan", "a_chain", "v_chain", "kept", "turned") as (
                block, v_c, a_lam, v_r, a_r, a_sp, v_sp, gates_ps, a_gates, a_exp, v_u2, a_sqrt, v_u, v_scan,
                a_chain, v_chain, kept, turned):
            u_t = A.take(8, T)
            ada_rows = H[:, 0:2, :, :].rearrange("p k s t -> p k (s t)")

            @block.sync
            def _(sp):
                stream(sp, 28)

            @block.tensor
            def _(pe):
                for o in range(LRU_O):
                    first = n0 + o // 4 * 14
                    if o % 4 == 0:
                        arrived(pe, first)
                        arrived(pe, first + 1)
                    if o >= 4:
                        pe.wait_ge(a_gates, 2 * (o - 3))
                    for w in range(2):
                        for k in range(2):
                            c = ((o % 4) * 2 + k) * P
                            mm = pe.matmul(bank[o % 4][:, w * T:(w + 1) * T], ring[:, (first + w) % NS, c:c + P],
                                           xl_conv[:, o // 2 * 2 + k, :], start=(k == 0), stop=(k == 1))
                        if o % 4 == 3:
                            mm.then_inc(blocks_done, 1)
                    if o % 4 != 3:
                        mm.then_inc(gates_ps, 1)
                    else:
                        for k in range(3):
                            modulate(pe, first + 2 + 4 * k, o // 4 * 3 + k, [bank[5], bank[7]], ada_rows, bank[6], kept, turned)
                turn(pe, 5, ada_rows, bank[6], kept, turned)

            @block.scalar
            def _(act):
                link = linker(act, a_chain)
                lam = sm("lru_lambda")
                link(act.activation(sp_l[:, 0, :], lam, ACT.Abs))
                link(act.activation(sp_l[:, 0, :], sp_l[:, 0, :], ACT.Exp, scale=-1.0))
                act.activation(sp_l[:, 0, :], sp_l[:, 0, :], ACT.Ln, bias=1.0).then_inc(a_sp, 1)
                for o in range(LRU_O):
                    if o % 4 == 3:
                        act.wait_ge(blocks_done, n0 + o // 4 * 14 + 2)
                    else:
                        act.wait_ge(gates_ps, o + 1 - o // 4)
                    act.activation(r_g[:, o, :], bank[o % 4][:, 0:T], ACT.Sigmoid,
                                   bias=sm("lru_b_a")[:, o:o + 1]).then_inc(a_gates, 1)
                    act.activation(i_g[:, o, :], bank[o % 4][:, T:2 * T], ACT.Sigmoid,
                                   bias=sm("lru_b_i")[:, o:o + 1]).then_inc(a_gates, 1)
                act.wait_ge(v_sp, 1)
                act.wait_ge(a_gates, 16)
                for o in range(LRU_O):
                    act.activation(u_t[:, o, :], r_g[:, o, :], ACT.Tanh, scale=sp_l[:, 1, o:o + 1]).then_inc(a_r, 1)
                act.wait_ge(a_r, 8)
                for o in range(LRU_O):
                    act.activation(r_g[:, o, :], r_g[:, o, :], ACT.Exp, scale=sp_l[:, 2, o:o + 1]).then_inc(a_exp, 1)
                for o in range(LRU_O):
                    act.wait_ge(v_u2, o + 1)
                    act.activation(u_t[:, o, :], u_t[:, o, :], ACT.Sqrt).then_inc(a_sqrt, 1)

            @block.vector
            def _(dve):
                link = linker(dve, v_chain)
                dve.wait_ge(a_sp, 1)
                link(dve.tensor_scalar(sp_l[:, 1, :], sm("lru_lambda"), -1.0, 0.0, ALU.mult, ALU.max))
                link(dve.tensor_tensor(sp_l[:, 0, :], sp_l[:, 1, :], sp_l[:, 0, :], ALU.add))
                dve.tensor_scalar(sp_l[:, 1, :], sp_l[:, 0, :], 8.0, None, ALU.mult)
                dve.tensor_scalar(sp_l[:, 2, :], sp_l[:, 0, :], -8.0, None, ALU.mult).then_inc(v_sp, 1)

                def keep(k):
                    keep_row(dve, n0 + k // 3 * 14 + 2 + k % 3 * 4, k, [bank[5], bank[7]], ada_rows, kept, turned)

                for k in range(3):
                    keep(k)
                dve.wait_ge(a_gates, 16)
                link(dve.tensor_tensor(i_g, i_g, xl_conv, ALU.mult))
                keep(3)
                for o in range(LRU_O):
                    dve.wait_ge(a_exp, o + 1)
                    a, u, xo = r_g[:, o, :], u_t[:, o, :], xl_conv[:, o, :]
                    link(dve.tensor_tensor(xo, a, a, ALU.mult))
                    link(dve.scalar_tensor_tensor(u, xo, 1.0, u, ALU.add, ALU.mult))
                    dve.tensor_scalar(u, u, 1e-34, None, ALU.max).then_inc(v_u2, 1)
                keep(4)
                for o in range(LRU_O):
                    dve.wait_ge(a_sqrt, o + 1)
                    a, u = r_g[:, o, :], u_t[:, o, :]
                    link(dve.tensor_tensor(u, u, i_g[:, o, :], ALU.mult))
                    link(dve.tensor_tensor_scan(u, a, u, 0.0, ALU.mult, ALU.add))
                    dve.tensor_tensor(xl_conv[:, o, :], u, y_gate[:, o, :], ALU.mult)
                keep(5)
                dve.wait_ge(turned, 6)
                keep_modulation(dve, 1, bank[6], 0, 24)
        used[0] += 28
        y_lru = xl_conv

        A.at = mixer_mark
        v_tok = A.take(TT, D)
        tmp = A.take(2, T)
        sc = A.take(2, 384)
        y_ret = A.take(8, T)
        ysq = A.take(2, 2, T)
        rs_r = A.take(RET_H, T)
        ada_rows = H[:, 0:2, :, :].rearrange("p k s t -> p k (s t)")
        n0 = used[0]
        with Phase("rot_ps", "v_rot", "rotated", "vt_ps", "a_vt", "sc_ps", "v_sc", "y_ps", "a_y", "a_sq", "norm_ps",
                   "v_inv", "a_root", "v_chain", "kept", "turned") as (
                block, rot_ps, v_rot, rotated, vt_ps, a_vt, sc_ps, v_sc, y_ps, a_y, a_sq, norm_ps, v_inv, a_root,
                v_chain, kept, turned):
            taken = [2, 2, 1, 1]

            qk = [(q_ret[:, h, :], "ret") for h in range(RET_H)] + [(k_ret[:, h, :], "retk") for h in range(RET_H)]

            @block.sync
            def _(sp):
                stream(sp, 24)

            @block.tensor
            def _(pe):
                for n, (q, _) in enumerate(qk):
                    if n >= 2:
                        pe.wait_ge(v_rot, n - 1)
                    pe.matmul(bank[n % 2][:, 0:T], mx("rot"), q, start=True, stop=True).then_inc(rot_ps, 1)
                for b in range(8):
                    if b >= 2:
                        pe.wait_ge(a_vt, b - 1)
                    for t in range(TT):
                        mm = pe.transpose(bank[2 + b % 2][:, t * P:(t + 1) * P], v_ret[:, b, t * P:(t + 1) * P], ident)
                    mm.then_inc(vt_ps, 1)
                pe.wait_ge(rotated, 8)
                pe.wait_ge(a_vt, 8)

                def scores(h):
                    if h >= 2:
                        pe.wait_ge(v_sc, h - 1)
                    ps = bank[4 + h % 2]
                    pe.matmul(ps[:, 0:T], k_ret[:, h, 0:P], q_ret[:, h, :], start=True, stop=True)
                    pe.matmul(ps[:, T:384], k_ret[:, h, P:T], q_ret[:, h, P:T], start=True,
                              stop=True).then_inc(sc_ps, 1)

                scores(0)
                for h in range(RET_H):
                    if h + 1 < RET_H:
                        scores(h + 1)
                    pe.wait_ge(v_sc, h + 1)
                    if h >= 2:
                        pe.wait_ge(a_y, h - 1)
                    for e in range(2):
                        v = slice((2 * h + e) * P, (2 * h + e + 1) * P)
                        o = bank[h % 2][:, e * T:(e + 1) * T]
                        pe.matmul(o, v_tok[:, 0, v], sc[:, h % 2, 0:T], start=True, stop=False)
                        mm = pe.matmul(o[:, P:T], v_tok[:, 1, v], sc[:, h % 2, T:384], start=False, stop=True)
                    mm.then_inc(y_ps, 1)
                    for k in range(sum(taken[:h]), sum(taken[:h + 1])):
                        modulate(pe, n0 + 4 * k, k, [bank[2], bank[3]], ada_rows, bank[7], kept, turned)
                turn(pe, 5, ada_rows, bank[7], kept, turned)
                for h in range(RET_H):
                    pe.wait_ge(a_sq, h + 1)
                    if h >= 2:
                        pe.wait_ge(v_inv, h - 1)
                    for e in range(2):
                        mm = pe.matmul(bank[4 + h % 2][:, 0:T], ones[:, :], ysq[:, h % 2, e, :], start=(e == 0),
                                       stop=(e == 1))
                    mm.then_inc(norm_ps, 1)

            @block.scalar
            def _(act):
                for b in range(8):
                    act.wait_ge(vt_ps, b + 1)
                    act.activation(v_tok[:, :, b * P:(b + 1) * P],
                                   bank[2 + b % 2][:, 0:T].rearrange("p (t c) -> p t c", t=TT), ACT.Copy).then_inc(a_vt, 1)
                for h in range(RET_H):
                    act.wait_ge(y_ps, h + 1)
                    act.activation(y_ret[:, 2 * h:2 * h + 2, :],
                                   bank[h % 2][:, :].rearrange("p (t c) -> p t c", t=2), ACT.Copy).then_inc(a_y, 1)
                    if h >= 2:
                        act.wait_ge(norm_ps, h - 1)
                    act.wait_ge(a_y, h + 1)
                    act.activation(ysq[:, h % 2, :, :], y_ret[:, 2 * h:2 * h + 2, :], ACT.Square).then_inc(a_sq, 1)
                for h in range(RET_H):
                    act.wait_ge(v_inv, h + 1)
                    act.activation(rs_r[:, h, :], rs_r[:, h, :], ACT.Sqrt).then_inc(a_root, 1)

            @block.vector
            def _(dve):
                link = linker(dve, v_chain)
                for n, (q, name) in enumerate(qk):
                    dve.wait_ge(rot_ps, n + 1)
                    dve.tensor_tensor(tmp[:, n % 2, :], bank[n % 2][:, 0:T], table(name + "_sin"), ALU.mult).then_inc(v_rot, 1)
                    link(dve.tensor_tensor(q, q, table(name + "_cos"), ALU.mult))
                    dve.wait_ge(v_rot, n + 1)
                    dve.tensor_tensor(q, q, tmp[:, n % 2, :], ALU.add).then_inc(rotated, 1)

                def keep(h):
                    for k in range(sum(taken[:h]), sum(taken[:h + 1])):
                        keep_row(dve, n0 + 4 * k, k, [bank[2], bank[3]], ada_rows, kept, turned)

                for h in range(RET_H):
                    dve.wait_ge(sc_ps, h + 1)
                    if h >= 2:
                        dve.wait_ge(y_ps, h - 1)
                    dve.tensor_tensor(sc[:, h % 2, :], bank[4 + h % 2][:, 0:384],
                                      table("ret_mask")[:, h * 384:(h + 1) * 384], ALU.mult).then_inc(v_sc, 1)
                    if h:
                        keep(h - 1)
                keep(RET_H - 1)
                for h in range(RET_H):
                    dve.wait_ge(norm_ps, h + 1)
                    link(dve.tensor_scalar(rs_r[:, h, :], bank[4 + h % 2][:, 0:T], 1.0 / T, EPS, ALU.mult, ALU.add))
                    dve.reciprocal(rs_r[:, h, :], rs_r[:, h, :]).then_inc(v_inv, 1)
                for h in range(RET_H):
                    dve.wait_ge(a_root, h + 1)
                    y = y_ret[:, 2 * h:2 * h + 2, :]
                    link(dve.tensor_tensor(y, y, rs_r[:, h, :].unsqueeze(1).to_broadcast([P, 2, T]), ALU.mult))
                    dve.tensor_tensor(y, y, g_gate[:, 2 * h:2 * h + 2, :], ALU.mult)
                dve.wait_ge(turned, 6)
                keep_modulation(dve, 1, bank[7], 24, 24)
        used[0] += 24

        merged = z_gate
        n0 = used[0]
        with Phase("by_dve", "v_chain") as (block, by_dve, v_chain):
            tm = A.take(T)
            branches = [y_ret, y_lru, y_ssd]

            @block.sync
            def _(sp):
                stream(sp, 24)

            @block.tensor
            def _(pe):
                for b in range(24):
                    evac_wait(pe, {"dve": by_dve}, ["dve"] * 24, b, 4)
                    product(pe, n0 + b, bank[b % 4][:, 0:T], lambda kt: branches[b // 8][:, kt, :])

            @block.vector
            def _(dve):
                link = linker(dve, v_chain)
                for b in range(24):
                    br, d = 2 - b // 8, b % 8
                    dve.wait_ge(blocks_done, n0 + b + 1)
                    if b < 8:
                        dve.tensor_tensor(merged[:, d, :], bank[b % 4][:, 0:T], gates[:, br * 8 + d, :],
                                          ALU.mult).then_inc(by_dve, 1)
                    else:
                        dve.tensor_tensor(tm, bank[b % 4][:, 0:T], gates[:, br * 8 + d, :], ALU.mult).then_inc(by_dve, 1)
                        dve.wait_ge(by_dve, b + 1)
                        link(dve.tensor_tensor(merged[:, d, :], merged[:, d, :], tm, ALU.add))
        used[0] += 24

        def residual(n, rhs, gain=None, streams=(1,), kgroups=1):
            n0 = used[0]
            both = len(streams) == 2
            width = 512 if both else T
            with Phase("by_dve") as (block, by_dve):
                @block.sync
                def _(sp):
                    stream(sp, n * kgroups)

                @block.tensor
                def _(pe):
                    for d in range(n):
                        if d >= 4:
                            pe.wait_ge(by_dve, (d - 3) * len(streams))
                        for g in range(kgroups):
                            arrived(pe, n0 + d * kgroups + g)
                            for kt in range(KT):
                                mm = pe.matmul(bank[d % 4][:, 0:width], col(n0 + d * kgroups + g, kt),
                                               rhs(g * KT + kt), start=(g == 0 and kt == 0),
                                               stop=(g == kgroups - 1 and kt == KT - 1))
                            mm.then_inc(blocks_done, 1)

                @block.vector
                def _(dve):
                    for d in range(n):
                        dve.wait_ge(blocks_done, n0 + (d + 1) * kgroups)
                        for j, s in enumerate(streams):
                            ps = bank[d % 4][:, j * T:(j + 1) * T]
                            if gain is None:
                                dve.tensor_tensor(X[:, d, s, :], X[:, d, s, :], ps, ALU.add).then_inc(by_dve, 1)
                            else:
                                dve.scalar_tensor_tensor(X[:, d, s, :], ps, gain(d, s), X[:, d, s, :], ALU.mult,
                                                         ALU.add).then_inc(by_dve, 1)
            used[0] += n * kgroups

        residual(8, lambda kt: merged[:, kt, :])

        A.at = 0
        rms_phase([(xl, hl, column("norm_ffn"), None)], lambda j, kt: (h_hi(kt), h_lo(kt)))
        f = A.take(FFN_T, T)
        n0 = used[0]
        with Phase("v_conv", "a_gelu", "by_dve", "v_chain", "a_hi", "p_lo") as (
                block, v_conv, a_gelu, by_dve, v_chain, a_hi, p_lo):
            @block.sync
            def _(sp):
                stream(sp, 48)

            @block.tensor
            def _(pe):
                for b in range(48):
                    if b >= 6:
                        pe.wait_ge(by_dve if b % 2 else v_conv, (b - 6) // 2 + 1)
                    product3(pe, n0, b, p_lo, bank[b % 6][:, 0:T], h_hi, h_lo)

            @block.gpsimd
            def _(pool):
                for b in range(48):
                    low(pool, n0, b, a_hi, p_lo)

            @block.scalar
            def _(act):
                for m in range(NH):
                    high(act, n0, m, a_hi)
                for i in range(FFN_T):
                    if 2 * i + 3 < 48:
                        high(act, n0, 2 * i + 3, a_hi)
                    act.wait_ge(v_conv, i + 1)
                    act.activation(f[:, i, :], f[:, i, :], ACT.Gelu_apprx_tanh).then_inc(a_gelu, 1)
                    if 2 * i + 4 < 48:
                        high(act, n0, 2 * i + 4, a_hi)

            @block.vector
            def _(dve):
                link = linker(dve, v_chain)

                def up(i):
                    dve.wait_ge(a_gelu, i + 1)
                    dve.wait_ge(blocks_done, n0 + 2 * i + 2)
                    dve.tensor_tensor(f[:, i, :], f[:, i, :], bank[(2 * i + 1) % 6][:, 0:T], ALU.mult).then_inc(by_dve, 1)

                for i in range(FFN_T):
                    y, ps = f[:, i, :], bank[2 * i % 6]
                    w = sm("ffn_conv_w")
                    dve.wait_ge(blocks_done, n0 + 2 * i + 1)
                    link(dve.tensor_scalar(y, ps[:, 0:T], w[:, 48 + i:49 + i], sm("ffn_conv_b")[:, i:i + 1],
                                           ALU.mult, ALU.add))
                    link(dve.scalar_tensor_tensor(y[:, 1:], ps[:, 0:T - 1], w[:, 24 + i:25 + i], y[:, 1:],
                                                  ALU.mult, ALU.add))
                    dve.scalar_tensor_tensor(y[:, 2:], ps[:, 0:T - 2], w[:, i:i + 1], y[:, 2:],
                                             ALU.mult, ALU.add).then_inc(v_conv, 1)
                    if i:
                        up(i - 1)
                up(FFN_T - 1)
        used[0] += 48
        residual(8, lambda kt: f[:, kt, :], kgroups=3)
        A.at = 0
        rms_phase([(xl, xl, column("norm_final"), None)])

        for l in range(LAYERS):
            last = l == LAYERS - 1
            lam_init = 0.8 - 0.6 * math.exp(-0.3 * l)
            streams = (1,) if last else (0, 1)
            t0 = T if last else 0
            A.at = 0
            mod = MODS[:, l, :, :]
            gain1 = A.take(8, 2)
            gain2 = A.take(8, 2)
            nlam = A.take(1)
            layer_mark = A.at

            with Phase("v_chain", "v_lam", "a_lam") as (block, v_chain, v_lam, a_lam):
                lam2 = A.take(2)
                prod = A.take(2, 64)

                @block.sync
                def _(sp):
                    stream(sp, 0)

                @block.scalar
                def _(act):
                    act.wait_ge(v_lam, 1)
                    act.activation(lam2, lam2, ACT.Exp).then_inc(a_lam, 1)

                @block.vector
                def _(dve):
                    link = linker(dve, v_chain)
                    lp = sm(f"lam{l}").rearrange("p (a b c) -> p a b c", a=2, b=2)
                    link(dve.tensor_tensor(prod, lp[:, :, 0, :], lp[:, :, 1, :], ALU.mult))
                    dve.tensor_reduce(lam2, prod, AX.X, ALU.add).then_inc(v_lam, 1)
                    for g, first, name in ((gain1, 8, "norm1"), (gain2, 32, "norm2")):
                        dve.scalar_tensor_tensor(g, mod[:, first:first + 8, :], 1.0,
                                                 sm(f"{name}{l}").unsqueeze(2).to_broadcast([P, 8, 2]), ALU.add, ALU.mult)
                    dve.wait_ge(a_lam, 1)
                    link(dve.tensor_tensor(nlam, lam2[:, 1:2], lam2[:, 0:1], ALU.subtract))
                    dve.tensor_scalar(nlam, nlam, -lam_init, None, ALU.add)
            A.at = layer_mark

            def norm_jobs(gain, first, ss):
                return [((lambda kt, s=s: X[:, kt, s, :]), (lambda kt, s=s: H[:, kt, s, :]),
                         (lambda kt, s=s: gain[:, kt, s:s + 1]), (lambda kt, s=s: mod[:, first + kt, s:s + 1])) for s in ss]

            A.at = (A.at + 7) // 8 * 8
            XH = nc.alloc_sbuf_tensor_at(f"h_high{l}", [P, KT, 2, T], F32R, offset=arena_at + 4 * A.at)
            A.take(KT * 2 * T)
            rms_phase(norm_jobs(gain1, 0, (0, 1)), lambda j, kt: (XH[:, kt, j, :], H_r[:, kt, j, :]))

            MT = A.take(N_MIX)
            mix = A.take(8, 2 * T)
            mix_mark = A.at
            u_pad = A.take(2, 2, T + CONV_K - 1)
            u_sig = A.take(2, 2 * T)
            mq, mk, mv, mo = (A.take(2, 2 * T) for _ in range(4))
            dq, dk, dv = (A.take(4, 2 * T) for _ in range(3))
            ig = A.take(2 * T)[0:36]
            fg = A.take(2 * T)[0:36]
            acc = A.take(2, 2 * T)
            kinds = [("gate", None, 0)] + [(ACT.Sigmoid, u_sig, i) for i in range(2)] + [("glu", u_pad, i) for i in range(2)]
            kinds += [(ACT.Sigmoid, mo, i) for i in range(2)]
            kinds += [(ACT.Copy, m, i) for m in (mq, mk, mv) for i in range(2)]
            kinds += [(ACT.Copy, m, i) for m in (dq, dk, dv) for i in range(4)]
            evac = ["dve" if isinstance(k[0], str) else "act" for k in kinds]
            n0 = used[0]
            with Phase("by_act", "by_dve", "padded", "tables_in", "v_tap", "a_hi", "p_lo") as (
                    block, by_act, by_dve, padded, tables_in, v_tap, a_hi, p_lo):
                @block.sync
                def _(sp):
                    sp.dma_start(MT, mix_tables).then_inc(tables_in, 16)
                    stream(sp, 25)
                    sp.wait_ge(tables_in, 16)

                @block.gpsimd
                def _(pool):
                    pool.memset(u_pad, 0.0).then_inc(padded, 1)
                    for b in range(25):
                        low(pool, n0, b, a_hi, p_lo)

                @block.tensor
                def _(pe):
                    for b in range(25):
                        evac_wait(pe, {"act": by_act, "dve": by_dve}, evac, b, 6)
                        product3(pe, n0, b, p_lo, bank[b % 6][:, :], lambda kt: XH[:, kt, :, :].rearrange("p s t -> p (s t)"),
                                 lambda kt: H_r[:, kt, :, :].rearrange("p s t -> p (s t)"))

                @block.scalar
                def _(act):
                    for m in range(NH):
                        high(act, n0, m, a_hi)
                    for b, (f, dst, i) in enumerate(kinds):
                        if evac[b] == "act":
                            act.wait_ge(blocks_done, n0 + b + 1)
                            act.activation(dst[:, i, :], bank[b % 6][:, :], f,
                                           scale=ML_D ** -0.5 if dst is mk else 1.0).then_inc(by_act, 1)
                        if b + NH < 25:
                            high(act, n0, b + NH, a_hi)

                @block.vector
                def _(dve):
                    gb = sm(f"gate_b{l}")
                    dve.wait_ge(blocks_done, n0 + 1)
                    dve.tensor_scalar(ig, bank[0][0:36, :], gb[0:36], None, ALU.add)
                    dve.tensor_scalar(fg, bank[0][64:100, :], gb[64:100], None, ALU.add).then_inc(by_dve, 1)
                    dve.wait_ge(padded, 1)
                    for i in range(2):
                        dve.wait_ge(by_act, i + 1)
                        dve.wait_ge(blocks_done, n0 + 4 + i)
                        dve.tensor_tensor(u_pad[:, i, :, CONV_K // 2:CONV_K // 2 + T],
                                          bank[3 + i][:, :].rearrange("p (s t) -> p s t", s=2),
                                          u_sig[:, i, :].rearrange("p (s t) -> p s t", s=2), ALU.mult).then_inc(by_dve, 1)
                    dve.wait_ge(by_dve, 3)
                    w = sm(f"conv_w{l}")
                    for k in range(CONV_K):
                        for i in range(2):
                            y = acc[:, i, :].rearrange("p (s t) -> p s t", s=2)
                            src = u_pad[:, i, :, k:k + T]
                            tap = w[:, 2 * k + i:2 * k + i + 1]
                            if k == 0:
                                dve.tensor_scalar(y, src, tap, sm(f"conv_b{l}")[:, i:i + 1], ALU.mult, ALU.add).then_inc(v_tap, 1)
                            else:
                                dve.wait_ge(v_tap, 2 * k + i - 1)
                                dve.scalar_tensor_tensor(y, src, tap, y, ALU.mult, ALU.add).then_inc(v_tap, 1)
            used[0] += 25

            conv_mark = A.at
            csq = A.take(2, 2 * T)
            crs = A.take(2 * T)
            with Phase("mean_ps", "v_cent", "a_csq", "var_ps", "v_inv", "a_root", "v_norm", "v_chain") as (
                    block, mean_ps, v_cent, a_csq, var_ps, v_inv, a_root, v_norm, v_chain):
                @block.sync
                def _(sp):
                    stream(sp, 0)

                @block.vector
                def _(dve):
                    link = linker(dve, v_chain)
                    dve.wait_ge(mean_ps, 1)
                    for i in range(2):
                        dve.scalar_tensor_tensor(acc[:, i, :], bank[0][:, :], -1.0 / T, acc[:, i, :],
                                                 ALU.mult, ALU.add).then_inc(v_cent, 1)
                    dve.wait_ge(var_ps, 1)
                    link(dve.tensor_scalar(crs, bank[1][:, :], 1.0 / T, EPS, ALU.mult, ALU.add))
                    dve.reciprocal(crs, crs).then_inc(v_inv, 1)
                    dve.wait_ge(a_root, 1)
                    for i in range(2):
                        dve.scalar_tensor_tensor(acc[:, i, :], acc[:, i, :], sm(f"ln_g{l}")[:, i:i + 1], crs,
                                                 ALU.mult, ALU.mult).then_inc(v_norm, 1)

                @block.tensor
                def _(pe):
                    for i in range(2):
                        mm = pe.matmul(bank[0][:, :], ones[:, :], acc[:, i, :], start=(i == 0), stop=(i == 1))
                    mm.then_inc(mean_ps, 1)
                    for i in range(2):
                        pe.wait_ge(a_csq, i + 1)
                        mm = pe.matmul(bank[1][:, :], ones[:, :], csq[:, i, :], start=(i == 0), stop=(i == 1))
                    mm.then_inc(var_ps, 1)

                @block.scalar
                def _(act):
                    for i in range(2):
                        act.wait_ge(v_cent, i + 1)
                        act.activation(csq[:, i, :], acc[:, i, :], ACT.Square).then_inc(a_csq, 1)
                    act.wait_ge(v_inv, 1)
                    act.activation(crs, crs, ACT.Sqrt).then_inc(a_root, 1)
                    for i in range(2):
                        act.wait_ge(v_norm, i + 1)
                        act.activation(mix[:, i, :], acc[:, i, :], ACT.Silu, bias=sm(f"ln_b{l}")[:, i:i + 1])
            A.at = conv_mark

            rows = 36
            Bt, Mx, En, Lt, on = (A.take(2 * T)[0:rows] for _ in range(5))
            u_tok = A.take(4, rows)
            en_tok = A.take(4, rows)
            v_aug = A.take(4, ML_H, ML_D + 1)
            wb = A.take(2, 4, 2 * T)
            rec = A.take(2, 4)
            hs = A.take(4, ML_H, ML_D)
            htmp = A.take(4, ML_D)
            ms = A.take(16)
            tiles = list(range(t0 // P, 4))

            def spans(d, st):
                if d == 0:
                    r = [(max(st * P, t0), 2 * T)]
                elif st >= 2:
                    r = [(T, (st + 1) * P)]
                elif last:
                    r = [(T, 2 * T)]
                else:
                    r = [(0, 2 * T)] if st == 1 else [(0, P), (T, 2 * T)]
                return r

            def sources(d, tt):
                if d == 0:
                    return list(range(tt + 1))
                return list(range(tt, 2)) if tt < 2 else [0, 1] + list(range(tt, 4))

            with Phase("zeroed", "a_soft", "v_lf", "v_state", "a_en", "tok_ps", "v_tok", "vt_ps", "v_vt", "bc_ps",
                       "sc_ps", "v_z", "a_w", "v_w", "pv_ps", "v_h", "v_chain", "a_chain", "v_mean", "a_root",
                       "v_hn", "ht_ps", "scan") as (
                    block, zeroed, a_soft, v_lf, v_state, a_en, tok_ps, v_tok, vt_ps, v_vt, bc_ps, sc_ps, v_z, a_w,
                    v_w, pv_ps, v_h, v_chain, a_chain, v_mean, a_root, v_hn, ht_ps, scan):
                @block.sync
                def _(sp):
                    stream(sp, 0)

                @block.gpsimd
                def _(pool):
                    pool.memset(Bt, 0.0)
                    pool.memset(Mx, 0.0)
                    pool.memset(v_aug, 1.0)
                    pool.memset(on, 1.0).then_inc(zeroed, 1)

                @block.scalar
                def _(act):
                    link = linker(act, a_chain)
                    link(act.activation(Lt, fg, ACT.Abs))
                    link(act.activation(Lt, Lt, ACT.Exp, scale=-1.0))
                    act.activation(Lt, Lt, ACT.Ln, bias=1.0).then_inc(a_soft, 1)
                    act.wait_ge(v_state, 1)
                    act.activation(En, En, ACT.Exp, scale=-1.0).then_inc(a_en, 1)
                    n = 0
                    for h in range(ML_H):
                        for d in range(2):
                            for st in range(4):
                                n += 1
                                act.wait_ge(v_z, n)
                                for i, (lo, hi) in enumerate(spans(d, st)):
                                    w = act.activation(wb[:, d, st, lo:hi], wb[:, d, st, lo:hi], ACT.Exp, scale=-1.0)
                                w.then_inc(a_w, 1)
                    act.wait_ge(v_mean, 1)
                    act.activation(ms, ms, ACT.Sqrt).then_inc(a_root, 1)

                @block.tensor
                def _(pe):
                    for b in range(2):
                        for tt in range(4):
                            mm = pe.transpose(bank[b][:, tt * P:(tt + 1) * P], mv[:, b, tt * P:(tt + 1) * P], ident)
                        mm.then_inc(vt_ps, 1)
                    pe.wait_ge(v_state, 1)
                    for tt in range(4):
                        pe.transpose(bank[2][:, tt * rows:(tt + 1) * rows], ig[:, tt * P:(tt + 1) * P],
                                     ident[0:rows, 0:rows])
                    pe.wait_ge(a_en, 1)
                    for tt in range(4):
                        mm = pe.transpose(bank[2][:, (4 + tt) * rows:(5 + tt) * rows], En[:, tt * P:(tt + 1) * P],
                                          ident[0:rows, 0:rows])
                    mm.then_inc(tok_ps, 1)
                    pe.wait_ge(v_vt, 2)
                    pe.wait_ge(v_tok, 2)
                    for h in range(ML_H):
                        r = slice((h % 2) * 64, (h % 2) * 64 + 64)
                        if h:
                            pe.wait_ge(v_w, 8 * h)
                        for d in range(2):
                            pe.matmul(bank[d][:, t0:], mx("selm")[32 * d:32 * d + 4, h * P:(h + 1) * P],
                                      Mx[32 * d:32 * d + 4, t0:], start=True, stop=True).then_inc(bc_ps, 1)
                        for st in range(4):
                            pe.matmul(bank[2 + st][:, t0:], mk[r, h // 2, st * P:(st + 1) * P], mq[r, h // 2, t0:],
                                      start=True, stop=True).then_inc(sc_ps, 1)
                        for d in range(2):
                            if h:
                                pe.wait_ge(v_h, 2 * (h - 1) + d + 1)
                            pe.wait_ge(v_w, 8 * h + 4 * (d + 1))
                            for tt in tiles:
                                src = sources(d, tt)
                                for st in src:
                                    mm = pe.matmul(bank[6 + d][:, tt * 65:tt * 65 + 65], wb[:, d, st, tt * P:(tt + 1) * P],
                                                   v_aug[:, st, h, :], start=(st == src[0]), stop=(st == src[-1]))
                            mm.then_inc(pv_ps, 1)
                    pe.wait_ge(v_hn, 1)
                    for b in range(2):
                        for tt in tiles:
                            mm = pe.transpose(bank[b][:, tt * P:(tt + 1) * P],
                                              hs[:, tt, 2 * b:2 * b + 2, :].rearrange("p a b -> p (a b)"), ident)
                        mm.then_inc(ht_ps, 1)

                @block.vector
                def _(dve):
                    link = linker(dve, v_chain)
                    dve.wait_ge(a_soft, 1)
                    dve.wait_ge(zeroed, 1)
                    link(dve.scalar_tensor_tensor(Lt, fg, 0.0, Lt, ALU.min, ALU.subtract))

                    def scans(dst, op, data0, data1, initial):
                        f, r = slice(0, 4), slice(32, 36)
                        dve.tensor_tensor_scan(dst[f], data0[f], data1[f], initial, op[0], op[1])
                        link(dve.tensor_tensor_scan(dst[r, T - 1::-1], data0[r, T - 1::-1], data1[r, T - 1::-1],
                                                    initial, op[0], op[1]))
                        link(dve.tensor_tensor_scan(dst[r, 2 * T - 1:T - 1:-1], data0[r, 2 * T - 1:T - 1:-1],
                                                    data1[r, 2 * T - 1:T - 1:-1], dst[r, 0:1], op[0], op[1]))

                    scans(Bt, (ALU.mult, ALU.add), on, Lt, 0.0)
                    link(dve.tensor_tensor(ig, ig, Bt, ALU.subtract))
                    scans(Mx, (ALU.max, ALU.max), ig, ig, 0.0)
                    dve.tensor_tensor(En, Bt, Mx, ALU.add).then_inc(v_state, 1)
                    for b in range(2):
                        dve.wait_ge(vt_ps, b + 1)
                        dve.tensor_copy(v_aug[:, :, 2 * b:2 * b + 2, 0:ML_D],
                                        bank[b][:, :].rearrange("p (t h e) -> p t h e", t=4, h=2)).then_inc(v_vt, 1)
                    dve.wait_ge(tok_ps, 1)
                    dve.tensor_copy(u_tok.rearrange("p a b -> p (a b)"), bank[2][:, 0:4 * rows]).then_inc(v_tok, 1)
                    dve.tensor_copy(en_tok.rearrange("p a b -> p (a b)"), bank[2][:, 4 * rows:8 * rows]).then_inc(v_tok, 1)
                    dve.wait_ge(v_tok, 2)
                    n = 0
                    for h in range(ML_H):
                        for d in range(2):
                            c = 32 * d + h
                            dve.wait_ge(bc_ps, 2 * h + d + 1)
                            if h:
                                dve.wait_ge(pv_ps, 2 * (h - 1) + d + 1)
                            for st in range(4):
                                for lo, hi in spans(d, st):
                                    w = dve.tensor_scalar(wb[:, d, st, lo:hi], bank[d][:, lo:hi], u_tok[:, st, c:c + 1],
                                                          0.0, ALU.subtract, ALU.max)
                                w.then_inc(v_z, 1)
                        for d in range(2):
                            for st in range(4):
                                n += 1
                                dve.wait_ge(a_w, n)
                                dve.wait_ge(sc_ps, 4 * h + st + 1)
                                diag = st * P >= t0
                                for lo, hi in spans(d, st):
                                    w = dve.tensor_tensor(wb[:, d, st, lo:hi], wb[:, d, st, lo:hi],
                                                          bank[2 + st][:, lo:hi], ALU.mult)
                                if diag:
                                    link(w)
                                    w = dve.tensor_tensor(wb[:, d, st, st * P:(st + 1) * P], wb[:, d, st, st * P:(st + 1) * P],
                                                          mx("anti") if d else mx("causal")[:, 0:P], ALU.mult)
                                w.then_inc(v_w, 1)
                        for d in range(2):
                            c = 32 * d + h
                            a, nt = tiles[0], len(tiles)
                            dve.wait_ge(pv_ps, 2 * h + d + 1)
                            ps = bank[6 + d][:, 0:260].rearrange("p (t e) -> p t e", t=4)[:, a:4, :]
                            link(dve.scalar_tensor_tensor(rec[:, d, a:4], ps[:, :, ML_D], -1.0, en_tok[:, a:4, c],
                                                          ALU.mult, ALU.max))
                            link(dve.tensor_tensor(rec[:, d, a:4], ps[:, :, ML_D], rec[:, d, a:4], ALU.max))
                            link(dve.reciprocal(rec[:, d, a:4], rec[:, d, a:4]))
                            rb = rec[:, d, a:4].unsqueeze(2).to_broadcast([P, nt, ML_D])
                            if d == 0:
                                dve.tensor_tensor(hs[:, a:4, h, :], ps[:, :, 0:ML_D], rb, ALU.mult).then_inc(v_h, 1)
                            else:
                                dve.tensor_tensor(htmp[:, a:4, :], ps[:, :, 0:ML_D], rb, ALU.mult).then_inc(v_h, 1)
                                dve.wait_ge(v_h, 2 * h + 2)
                                link(dve.tensor_tensor(hs[:, a:4, h, :], hs[:, a:4, h, :], htmp[:, a:4, :], ALU.add))
                    a, nt = tiles[0], len(tiles)
                    hv = hs[:, a:4, :, :].rearrange("p t h e -> p (t h) e")
                    mv_ = ms[:, 4 * a:16]
                    for tt in range(a, 4):
                        link(dve.tensor_tensor(wb[:, 0, tt, 0:T], hs[:, tt, :, :].rearrange("p h e -> p (h e)"),
                                               hs[:, tt, :, :].rearrange("p h e -> p (h e)"), ALU.mult))
                        link(dve.tensor_reduce(ms[:, 4 * tt:4 * tt + 4],
                                               wb[:, 0, tt, 0:T].rearrange("p (h e) -> p h e", e=ML_D), AX.X, ALU.add))
                    if a:
                        link(dve.memset(ms[:, 0:4 * a], 1.0))
                    link(dve.tensor_scalar(ms, ms, 1.0 / ML_D, EPS, ALU.mult, ALU.add))
                    dve.reciprocal(ms, ms).then_inc(v_mean, 1)
                    dve.wait_ge(a_root, 1)
                    dve.tensor_tensor(hv, hv, mv_.unsqueeze(2).to_broadcast([P, 4 * nt, ML_D]), ALU.mult).then_inc(v_hn, 1)
                    for b in range(2):
                        dve.wait_ge(ht_ps, b + 1)
                        dve.scalar_tensor_tensor(mix[:, 2 + b, t0:], bank[b][:, t0:], sm(f"ml_norm{l}"), mo[:, b, t0:],
                                                 ALU.mult, ALU.mult)
            A.at = conv_mark

            dv_tok = A.take(4, 4 * P)
            tmp = A.take(2, T)
            E = A.take(2, 2, 2 * T)
            pT = A.take(2, 2 * T)
            stats = A.take(2, 8)
            yd = A.take(DF_H, 2 * T)
            drs = A.take(2, 2 * T)
            dg = A.take(1)
            items = [(h, qt) for h in range(DF_H) for qt in (range(2, 4) if last else range(4))]
            with Phase("rot_ps", "v_rot", "rotated", "vt_ps", "a_vt", "sc_ps", "v_max", "a_exp", "v_p", "pt_ps",
                       "a_pt", "o_ps", "v_o", "a_sq", "norm_ps", "v_inv", "a_root", "v_chain", "v_p_rot", "v_chain2") as (
                    block, rot_ps, v_rot, rotated, vt_ps, a_vt, sc_ps, v_max, a_exp, v_p, pt_ps, a_pt, o_ps, v_o,
                    a_sq, norm_ps, v_inv, a_root, v_chain, v_p_rot, v_chain2):
                ax_t = A.take(2, T)
                qk = [dq[:, h, T:] for h in range(DF_H)] + [dk[:, h, T:] for h in range(DF_H)]
                keys_of = lambda qt: T if qt < 2 else 2 * T

                @block.sync
                def _(sp):
                    sp.dma_start(ax_t.rearrange("p a b -> p (a b)"), axial).then_inc(rotated, 16)
                    stream(sp, 0)

                @block.tensor
                def _(pe):
                    for n, q in enumerate(qk):
                        if n >= 2:
                            pe.wait_ge(v_rot, n - 1)
                        pe.matmul(bank[n % 2][:, 0:T], mx("rot"), q, start=True, stop=True).then_inc(rot_ps, 1)
                    for b in range(4):
                        if b >= 2:
                            pe.wait_ge(a_vt, b - 1)
                        for tt in range(4):
                            mm = pe.transpose(bank[2 + b % 2][:, tt * P:(tt + 1) * P], dv[:, b, tt * P:(tt + 1) * P], ident)
                        mm.then_inc(vt_ps, 1)
                    pe.wait_ge(v_p_rot, 8)
                    pe.wait_ge(a_vt, 4)

                    def scores(n):
                        h, qt = items[n]
                        if n >= 2:
                            pe.wait_ge(a_exp, 2 * (n - 1))
                        nk = keys_of(qt)
                        for s in range(2):
                            r = slice(64 * s, 64 * s + 64)
                            mm = pe.matmul(bank[2 * (n % 2) + s][:, 0:nk], dq[r, h, qt * P:(qt + 1) * P], dk[r, h, 0:nk],
                                           start=True, stop=True)
                        mm.then_inc(sc_ps, 1)

                    scores(0)
                    for n, (h, qt) in enumerate(items):
                        if n + 1 < len(items):
                            scores(n + 1)
                        nk = keys_of(qt)
                        pe.wait_ge(v_p, n + 1)
                        if n >= 2:
                            pe.wait_ge(a_pt, n - 1)
                        for k in range(nk // P):
                            mm = pe.transpose(bank[4 + n % 2][:, k * P:(k + 1) * P], E[:, n % 2, 0, k * P:(k + 1) * P], ident)
                        mm.then_inc(pt_ps, 1)
                        pe.wait_ge(a_pt, n + 1)
                        if n >= 2:
                            pe.wait_ge(v_o, n - 1)
                        for k in range(nk // P):
                            mm = pe.matmul(bank[6 + n % 2][:, 0:P], dv_tok[:, k, h * P:(h + 1) * P],
                                           pT[:, n % 2, k * P:(k + 1) * P], start=(k == 0), stop=(k == nk // P - 1))
                        mm.then_inc(o_ps, 1)
                    for h in range(DF_H):
                        pe.wait_ge(a_sq, h + 1)
                        if h >= 2:
                            pe.wait_ge(v_inv, h - 1)
                        pe.matmul(bank[h % 2][:, t0:], ones[:, :], E[:, h % 2, 1, t0:], start=True,
                                  stop=True).then_inc(norm_ps, 1)

                @block.scalar
                def _(act):
                    for b in range(4):
                        act.wait_ge(vt_ps, b + 1)
                        act.activation(dv_tok[:, :, b * P:(b + 1) * P],
                                       bank[2 + b % 2][:, :].rearrange("p (t c) -> p t c", t=4), ACT.Copy).then_inc(a_vt, 1)

                    def softmax(n):
                        nk = keys_of(items[n][1])
                        act.wait_ge(v_max, n + 1)
                        for s in range(2):
                            act.activation(E[:, n % 2, s, 0:nk], bank[2 * (n % 2) + s][:, 0:nk], ACT.Exp,
                                           bias=stats[:, n % 2, s:s + 1], scale=0.125,
                                           accum_out=stats[:, n % 2, 2 + s:3 + s]).then_inc(a_exp, 1)

                    softmax(0)
                    for n, (h, qt) in enumerate(items):
                        if n + 1 < len(items):
                            softmax(n + 1)
                        nk = keys_of(qt)
                        act.wait_ge(pt_ps, n + 1)
                        act.activation(pT[:, n % 2, 0:nk], bank[4 + n % 2][:, 0:nk], ACT.Copy).then_inc(a_pt, 1)
                    act.wait_ge(v_o, len(items))
                    for h in range(DF_H):
                        if h >= 2:
                            act.wait_ge(norm_ps, h - 1)
                        act.activation(E[:, h % 2, 1, t0:], yd[:, h, t0:], ACT.Square).then_inc(a_sq, 1)
                    for h in range(DF_H):
                        act.wait_ge(v_inv, h + 1)
                        act.activation(drs[:, h % 2, t0:], drs[:, h % 2, t0:], ACT.Sqrt).then_inc(a_root, 1)

                @block.vector
                def _(dve):
                    link = linker(dve, v_chain)
                    dve.wait_ge(rotated, 16)
                    for n, q in enumerate(qk):
                        dve.wait_ge(rot_ps, n + 1)
                        dve.tensor_tensor(tmp[:, n % 2, :], bank[n % 2][:, 0:T], ax_t[:, 1, :], ALU.mult).then_inc(v_rot, 1)
                        link(dve.tensor_tensor(q, q, ax_t[:, 0, :], ALU.mult))
                        dve.wait_ge(v_rot, n + 1)
                        dve.tensor_tensor(q, q, tmp[:, n % 2, :], ALU.add).then_inc(v_p_rot, 1)
                    dve.tensor_scalar(dg, sm(f"df_norm{l}"), 1.0 - lam_init, None, ALU.mult)

                    def maxima(n):
                        nk = keys_of(items[n][1])
                        st = stats[:, n % 2, :]
                        dve.wait_ge(sc_ps, n + 1)
                        for s in range(2):
                            w = dve.tensor_reduce(st[:, 4 + s:5 + s], bank[2 * (n % 2) + s][:, 0:nk], AX.X, ALU.max)
                        link(w)
                        dve.tensor_scalar(st[:, 0:2], st[:, 4:6], -0.125, None, ALU.mult).then_inc(v_max, 1)

                    def keep(n):
                        h, qt = items[n]
                        dve.wait_ge(o_ps, n + 1)
                        dve.tensor_copy(yd[:, h, qt * P:(qt + 1) * P], bank[6 + n % 2][:, 0:P]).then_inc(v_o, 1)

                    maxima(0)
                    for n, (h, qt) in enumerate(items):
                        nk = keys_of(qt)
                        st = stats[:, n % 2, :]
                        dve.wait_ge(a_exp, 2 * (n + 1))
                        link(dve.reciprocal(st[:, 6:8], st[:, 2:4]))
                        dve.tensor_tensor(st[:, 7:8], st[:, 7:8], nlam, ALU.mult).then_inc(v_chain2, 1)
                        link(dve.tensor_scalar(E[:, n % 2, 0, 0:nk], E[:, n % 2, 0, 0:nk], st[:, 6:7], None, ALU.mult))
                        dve.wait_ge(v_chain2, n + 1)
                        dve.scalar_tensor_tensor(E[:, n % 2, 0, 0:nk], E[:, n % 2, 1, 0:nk], st[:, 7:8],
                                                 E[:, n % 2, 0, 0:nk], ALU.mult, ALU.add).then_inc(v_p, 1)
                        if n + 1 < len(items):
                            maxima(n + 1)
                        if n:
                            keep(n - 1)
                    keep(len(items) - 1)
                    for h in range(DF_H):
                        dve.wait_ge(norm_ps, h + 1)
                        link(dve.tensor_scalar(drs[:, h % 2, t0:], bank[h % 2][:, t0:], 1.0 / P, EPS, ALU.mult, ALU.add))
                        dve.reciprocal(drs[:, h % 2, t0:], drs[:, h % 2, t0:]).then_inc(v_inv, 1)
                        dve.wait_ge(a_root, h + 1)
                        dve.scalar_tensor_tensor(mix[:, 4 + h, t0:], yd[:, h, t0:], dg, drs[:, h % 2, t0:],
                                                 ALU.mult, ALU.mult)
            A.at = mix_mark
            residual(8, lambda kt: mix[:, kt, t0:], gain=lambda d, s: mod[:, 16 + d, s:s + 1], streams=streams)
            A.at = layer_mark
            rms_phase(norm_jobs(gain2, 24, streams))

            R = [A.take(3, T) for _ in streams]
            peer_mark = A.at
            qT = A.take(PEER_H, 2 * T)
            KK = A.take(PEER_H, NK)
            n0 = used[0]
            with Phase("by_act", "keys_in") as (block, by_act, keys_in):
                @block.sync
                def _(sp):
                    sp.dma_start(KK.rearrange("p a b -> p (a b)"), keys2[l]).then_inc(keys_in, 16)
                    stream(sp, 8)
                    sp.wait_ge(keys_in, 16)

                @block.tensor
                def _(pe):
                    for b in range(8):
                        if b >= 4:
                            pe.wait_ge(by_act, b - 3)
                        product(pe, n0 + b, bank[b % 4][:, t0:],
                                lambda kt: H[:, kt, t0 // T:, :].rearrange("p s t -> p (s t)"))

                @block.scalar
                def _(act):
                    for b in range(8):
                        act.wait_ge(blocks_done, n0 + b + 1)
                        act.activation(qT[:, b, t0:], bank[b % 4][:, t0:], ACT.Copy).then_inc(by_act, 1)
            used[0] += 8

            S = A.take(16, NK)
            S2 = A.take(16, NK)
            best = A.take(16, TOPK)
            bidx = A.take(16, TOPK)
            bidx_u = A.take(16, TOPK).bitcast(U32)
            cand = A.take(PEER_H, 256)
            cand2 = A.take(PEER_H, 256)
            top = A.take(PEER_H, TOPK)
            pos_u = A.take(PEER_H, TOPK).bitcast(U32)
            half_u = A.take(2, PEER_H, TOPK).bitcast(U32)
            half = A.take(2, PEER_H, TOPK)
            found = A.take(3, PEER_H * TOPK)
            zsum = A.take(2, PEER_H)
            route = tiles
            with Phase("s_ps", "a_s", "v_read", "v_diff", "a_e", "v_found", "t_ps", "a_t", "v_chain", "spilled") as (
                    block, s_ps, a_s, v_read, v_diff, a_e, v_found, t_ps, a_t, v_chain, spilled):
                @block.sync
                def _(sp):
                    stream(sp, 0)
                    if not last:
                        sp.dma_start(spill, H[:, :, 1, :]).then_inc(spilled, 16)
                        sp.wait_ge(spilled, 16)

                @block.tensor
                def _(pe):
                    def scores(n):
                        tt = route[n]
                        if n:
                            pe.wait_ge(a_s, 4 * n)
                        for h in range(PEER_H):
                            for s in range(2):
                                r = slice(64 * s, 64 * s + 64)
                                c = h % 4 * P
                                mm = pe.matmul(bank[2 * s + h // 4][:, c:c + P], qT[r, h, tt * P:(tt + 1) * P],
                                               KK[r, h, :], start=True, stop=True)
                            if h % 4 == 3:
                                mm.then_inc(s_ps, 1)

                    scores(0)
                    for n, tt in enumerate(route):
                        if n + 1 < len(route):
                            scores(n + 1)
                        pe.wait_ge(v_found, n + 1)
                        if n:
                            pe.wait_ge(a_t, n)
                        for i in range(3):
                            mm = pe.transpose(bank[4][:, i * P:(i + 1) * P], found[:, i, :], ident)
                        mm.then_inc(t_ps, 1)

                @block.scalar
                def _(act):
                    for n, tt in enumerate(route):
                        if n:
                            act.wait_ge(v_read, n)
                        for b in range(4):
                            act.wait_ge(s_ps, 2 * n + b % 2 + 1)
                            act.activation(S[:, 8 * (b % 2) + b // 2:8 * (b % 2) + 8:2, :],
                                           bank[b][:, :].rearrange("p (h n) -> p h n", h=4), ACT.Copy).then_inc(a_s, 1)
                        act.wait_ge(v_diff, n + 1)
                        act.activation(top, top, ACT.Exp).then_inc(a_e, 1)
                        act.wait_ge(t_ps, n + 1)
                        dst = R[tt // 2 if not last else 0]
                        act.activation(dst[:, :, (tt % 2) * P:(tt % 2 + 1) * P],
                                       bank[4][:, 0:384].rearrange("p (a b) -> p a b", a=3), ACT.Copy).then_inc(a_t, 1)

                @block.vector
                def _(dve):
                    link = linker(dve, v_chain)

                    def top16(n, src, scratch, val, idx):
                        for i in range(n):
                            w = dve.max(val(i)[:, 0:8], src(i))
                        link(w)
                        for i in range(n):
                            dve.max_index(idx(i)[:, 0:8], val(i)[:, 0:8], src(i))
                            w = dve.match_replace(scratch(i), val(i)[:, 0:8], src(i), -3.0e38)
                        link(w)
                        for i in range(n):
                            w = dve.max(val(i)[:, 8:16], scratch(i))
                        link(w)
                        for i in range(n):
                            w = dve.max_index(idx(i)[:, 8:16], val(i)[:, 8:16], scratch(i))
                        return w

                    for n, tt in enumerate(route):
                        dve.wait_ge(a_s, 4 * (n + 1))
                        top16(16, lambda i: S[:, i, :], lambda i: S2[:, i, :], lambda i: best[:, i, :],
                              lambda i: bidx_u[:, i, :]).then_inc(v_read, 1)
                        dve.wait_ge(v_read, n + 1)
                        dve.tensor_copy(bidx, bidx_u)
                        bh = best.rearrange("p (h s) k -> p h s k", s=2)
                        wide = [P, PEER_H, TOPK, TOPK]
                        c4 = cand.rearrange("p h (a b) -> p h a b", a=TOPK)
                        c24 = cand2.rearrange("p h (a b) -> p h a b", a=TOPK)
                        link(dve.tensor_tensor(c4, bh[:, :, 0, :].unsqueeze(3).to_broadcast(wide),
                                               bh[:, :, 1, :].unsqueeze(2).to_broadcast(wide), ALU.add))
                        link(top16(PEER_H, lambda i: cand[:, i, :], lambda i: cand2[:, i, :], lambda i: top[:, i, :],
                                   lambda i: pos_u[:, i, :]))
                        dve.tensor_scalar(half_u[:, 0, :, :], pos_u, 4, None, ALU.logical_shift_right)
                        link(dve.tensor_scalar(half_u[:, 1, :, :], pos_u, 15, None, ALU.bitwise_and))
                        link(dve.tensor_copy(half, half_u))
                        if n:
                            dve.wait_ge(t_ps, n)
                        ih = bidx.rearrange("p (h s) k -> p h s k", s=2)
                        for s in range(2):
                            link(dve.tensor_tensor(c4, half[:, s, :, :].unsqueeze(3).to_broadcast(wide),
                                                   cc("iota16").unsqueeze(1).unsqueeze(1).to_broadcast(wide), ALU.is_equal))
                            link(dve.tensor_tensor(c24, c4, ih[:, :, s, :].unsqueeze(2).to_broadcast(wide), ALU.mult))
                            link(dve.tensor_reduce(found[:, s, :].rearrange("p (h k) -> p h k", k=TOPK), c24, AX.X, ALU.add))
                        link(dve.tensor_copy(zsum[:, 1, :], top[:, :, 0]))
                        dve.tensor_tensor(top, top, zsum[:, 1, :].unsqueeze(2).to_broadcast([P, PEER_H, TOPK]),
                                          ALU.subtract).then_inc(v_diff, 1)
                        dve.wait_ge(a_e, n + 1)
                        link(dve.tensor_reduce(zsum[:, 0, :], top, AX.X, ALU.add))
                        link(dve.reciprocal(zsum[:, 0, :], zsum[:, 0, :]))
                        dve.tensor_tensor(found[:, 2, :].rearrange("p (h k) -> p h k", k=TOPK), top,
                                          zsum[:, 0, :].unsqueeze(2).to_broadcast([P, PEER_H, TOPK]),
                                          ALU.mult).then_inc(v_found, 1)

            for j, s in enumerate(streams):
                A.at = peer_mark
                G = A.take(NK, T)
                hotA = A.take(4, P)
                hotB = A.take(4, P)
                rows_, cols_, wts = (R[j][:, i, :] for i in range(3))
                with Phase("v_hot", "g_ps", "a_g", "x_hi") as (block, v_hot, g_ps, a_g, x_hi):
                    @block.sync
                    def _(sp):
                        stream(sp, 0)

                    @block.gpsimd
                    def _(pool):
                        for kt in range(KT):
                            pool.wait_ge(x_hi, kt + 1)
                            pool.tensor_tensor(H_r[:, kt, s, :], H[:, kt, s, :], H_r[:, kt, 1 - s, :].bitcast(F32),
                                               ALU.subtract)

                    @block.vector
                    def _(dve):
                        def one_hots(t, u):
                            dve.tensor_scalar(hotA[:, u, :], cc("iota"), rows_[:, bass.ds(t, 1)], wts[:, bass.ds(t, 1)],
                                              ALU.is_equal, ALU.mult)
                            dve.tensor_scalar(hotB[:, u, :], cc("iota"), cols_[:, bass.ds(t, 1)], None,
                                              ALU.is_equal).then_inc(v_hot, 1)

                        for u in range(4):
                            one_hots(u, u)
                        with dve.Fori(1, T // 4) as it:
                            for u in range(4):
                                dve.wait_ge(g_ps, it * 4 + (u - 3))
                                one_hots(it * 4 + u, u)

                    @block.tensor
                    def _(pe):
                        def products(t, b, first=False):
                            for u in range(4):
                                pe.wait_ge(v_hot, t + (u + 1))
                                if u == 0 and not first:
                                    pe.wait_ge(a_g, group(t) - 3)
                                pe.matmul(bank[b][:, u * P:(u + 1) * P], hotA[:, u, :], hotB[:, u, :], start=True,
                                          stop=True).then_inc(g_ps, 1)

                        for g in range(4):
                            group = None
                            products(4 * g, g, first=True)
                        with pe.Fori(1, T // 16) as it:
                            for g in range(4):
                                group = lambda t, g=g: it * 4 + g
                                products(it * 16 + 4 * g, g)

                    @block.scalar
                    def _(act):
                        for kt in range(KT):
                            act.activation(H_r[:, kt, 1 - s, :], H[:, kt, s, :], ACT.Copy).then_inc(x_hi, 1)
                        with act.Fori(0, T // 16) as it:
                            for g in range(4):
                                act.wait_ge(g_ps, it * 16 + (4 * g + 4))
                                act.activation(G[:, :, bass.ds(it * 16 + 4 * g, 4)].rearrange("p j t -> p t j"),
                                               bank[g][:, :].rearrange("p (t j) -> p t j", t=4), ACT.Copy).then_inc(a_g, 1)

                A.at = peer_mark + NK * T
                A.at = (A.at + 7) // 8 * 8
                parts = nc.alloc_sbuf_tensor_at(f"w_parts{l}{s}", [P, 4, T], F32R, offset=arena_at + 4 * A.at)
                W = A.take(4, T)[:, 0:2, :]
                W_lo, W_hi = parts[:, 0:2, :], parts[:, 2:4, :]
                x_hi_, x_lo_ = H_r[:, :, 1 - s, :], H_r[:, :, s, :]
                n0 = used[0]
                pairs = NK - 2
                with Phase("a_hi", "v_lo", "a_gelu", "v_prod", "v_whi", "v_w") as (
                        block, a_hi, v_lo, a_gelu, v_prod, v_whi, v_w):
                    @block.sync
                    def _(sp):
                        stream(sp, 2 * NK)

                    @block.scalar
                    def _(act):
                        def high(m, turn=0):
                            arrived(act, n0 + m, turn * 3)
                            if m >= NH:
                                act.wait_ge(blocks_done, turn * 12 + (n0 + m - NH + 1))
                            act.activation(ring_hi[:, m % NH, :], ring[:, (n0 + m) % NS, :], ACT.Copy).then_inc(a_hi, 1)

                        def gelu(c, turn=0):
                            act.wait_ge(blocks_done, turn * 12 + (n0 + max(2 * c, 1)))
                            act.activation(W[:, c % 2, :], bank[4 + c % 2][:, 0:T], ACT.Gelu).then_inc(a_gelu, 1)

                        for m in range(NH):
                            high(m)
                        gelu(0)
                        high(3)
                        high(4)
                        with act.Fori(0, pairs // 6 - 1) as turn:
                            for c in range(1, 7):
                                gelu(c, turn)
                                high(2 * c + 3, turn)
                                high(2 * c + 4, turn)
                        for c in range(NK - 7, NK):
                            gelu(c)
                            for m in (2 * c + 3, 2 * c + 4):
                                if m < 2 * NK:
                                    high(m)

                    @block.vector
                    def _(dve):
                        def low(m, turn=0):
                            dve.wait_ge(a_hi, turn * 12 + (m + 1))
                            slot = (n0 + m) % NS
                            dve.tensor_tensor(ring_lo[:, slot, :], ring[:, slot, :], ring_hi[:, m % NH, :].bitcast(F32),
                                              ALU.subtract).then_inc(v_lo, 1)

                        def weigh(c, turn=0):
                            w, g = W[:, c % 2, :], G[:, bass.ds(turn * 6 + c, 1), :].rearrange("p a t -> p (a t)")
                            dve.wait_ge(a_gelu, turn * 6 + (c + 1))
                            dve.tensor_tensor(w, w, g, ALU.mult).then_inc(v_prod, 1)
                            dve.wait_ge(v_prod, turn * 6 + (c + 1))
                            dve.tensor_copy(W_hi[:, c % 2, :], w).then_inc(v_whi, 1)
                            dve.wait_ge(v_whi, turn * 6 + (c + 1))
                            dve.tensor_tensor(W_lo[:, c % 2, :], w, W_hi[:, c % 2, :].bitcast(F32),
                                              ALU.subtract).then_inc(v_w, 1)

                        for m in range(NH):
                            low(m)
                        weigh(0)
                        low(3)
                        low(4)
                        with dve.Fori(0, pairs // 6 - 1) as turn:
                            for c in range(1, 7):
                                weigh(c, turn)
                                low(2 * c + 3, turn)
                                low(2 * c + 4, turn)
                        for c in range(NK - 7, NK):
                            weigh(c)
                            for m in (2 * c + 3, 2 * c + 4):
                                if m < 2 * NK:
                                    low(m)

                    @block.tensor
                    def _(pe):
                        def up(c, turn=0):
                            m = max(2 * c - 1, 0)
                            pe.wait_ge(v_lo, turn * 12 + (m + 1))
                            if c >= 2:
                                pe.wait_ge(a_gelu, turn * 6 + (c - 1))
                            hi, lo, o = ring_hi[:, m % NH, :], ring_lo[:, (n0 + m) % NS, :], bank[4 + c % 2][:, 0:T]
                            for kt in range(KT):
                                k = slice(kt * P, (kt + 1) * P)
                                pe.matmul(o, hi[:, k], x_hi_[:, kt, :], start=(kt == 0), stop=False)
                                pe.matmul(o, hi[:, k], x_lo_[:, kt, :], start=False, stop=False)
                                mm = pe.matmul(o, lo[:, k], x_hi_[:, kt, :], start=False, stop=(kt == KT - 1))
                            mm.then_inc(blocks_done, 1)

                        def down(c, turn=0, start=False, stop=False):
                            m = 2 * c + 2 if c < NK - 1 else 2 * NK - 1
                            pe.wait_ge(v_lo, turn * 12 + (m + 1))
                            pe.wait_ge(v_w, turn * 6 + (c + 1))
                            hi, lo = ring_hi[:, m % NH, :], ring_lo[:, (n0 + m) % NS, :]
                            halves = [(e, slice(e * 512, (e + 1) * 512)) for e in range(2)]
                            for t in range(TT):
                                w_hi, w_lo = (w[:, c % 2, t * P:(t + 1) * P] for w in (W_hi, W_lo))
                                for e, v in halves:
                                    pe.matmul(bank[2 * t + e][:, :], w_hi, hi[:, v], start=start, stop=False)
                                for e, v in halves:
                                    pe.matmul(bank[2 * t + e][:, :], w_hi, lo[:, v], start=False, stop=False)
                                for e, v in halves:
                                    mm = pe.matmul(bank[2 * t + e][:, :], w_lo, hi[:, v], start=False, stop=stop)
                            mm.then_inc(blocks_done, 1)

                        up(0)
                        up(1)
                        down(0, start=True)
                        with pe.Fori(0, pairs // 6) as turn:
                            for c in range(1, 7):
                                up(c + 1, turn)
                                down(c, turn)
                        down(NK - 1, stop=True)

                used[0] += 2 * NK
                A.at = peer_mark
                y_tok = A.take(TT, D)
                with Phase("a_y", "t_ps", "v_x", "back") as (block, a_y, t_ps, v_x, back):
                    @block.sync
                    def _(sp):
                        if s == 0:
                            sp.dma_start(H[:, :, 1, :], spill).then_inc(back, 16)
                            sp.wait_ge(back, 16)
                        stream(sp, 0)

                    @block.scalar
                    def _(act):
                        for c in range(2):
                            for t in range(TT):
                                act.activation(y_tok[:, t, c * 512:(c + 1) * 512], bank[2 * t + c][:, :],
                                               ACT.Copy).then_inc(a_y, 1)

                    @block.tensor
                    def _(pe):
                        for b in range(8):
                            pe.wait_ge(a_y, 2 * (b // 4) + 2)
                            if b >= 4:
                                pe.wait_ge(v_x, b - 3)
                            for t in range(TT):
                                mm = pe.transpose(bank[4 + b % 4][:, t * P:(t + 1) * P], y_tok[:, t, b * P:(b + 1) * P], ident)
                            mm.then_inc(t_ps, 1)

                    @block.vector
                    def _(dve):
                        for b in range(8):
                            dve.wait_ge(t_ps, b + 1)
                            dve.scalar_tensor_tensor(X[:, b, s, :], bank[4 + b % 4][:, 0:T], mod[:, 40 + b, s:s + 1],
                                                     X[:, b, s, :], ALU.mult, ALU.add).then_inc(v_x, 1)

        A.at = 0
        rms_phase([(xl, hl, column("final_g"), None)])
        with Phase("stored") as (block, stored):
            @block.sync
            def _(sp):
                sp.dma_start(out, H[:, :, 1, :]).then_inc(stored, 16)
                sp.wait_ge(stored, 16)


def blocks(w):
    g, n = w.shape[0] // D, w.shape[1] // P
    return np.ascontiguousarray(w.reshape(g, KT, P, n, P).transpose(3, 0, 2, 1, 4).reshape(n * g, P, D))


def row_blocks(w):
    n = w.shape[1] // 512
    return np.ascontiguousarray(w.reshape(4, 2, P, n, 512).transpose(3, 0, 2, 1, 4).reshape(4 * n, P, D))


def feature_columns(a):
    return a.reshape(-1, P).T


def streams_layout(ctx, x):
    return np.ascontiguousarray(np.stack([ctx, x]).reshape(2, T, KT, P).transpose(3, 2, 0, 1))


def lay_out(i):
    z = np.zeros
    sm = z((P, N_SMALL), np.float32)

    def put(name, a):
        o, n = SMALL[name]
        sm[:a.shape[0], o:o + n] = a.reshape(a.shape[0], n)

    fc = feature_columns
    put("norm_mix", fc(i["norm_mix"]))
    put("ssd_conv_w", fc(i["ssd_conv_w"]))
    put("ssd_conv_b", fc(i["ssd_conv_b"]))
    put("ssd_norm", fc(i["ssd_norm"]))
    put("ssd_d", fc(np.repeat(i["ssd_d"][0], SSD_P)))
    put("lru_conv_w", fc(i["lru_conv_w"]))
    put("lru_conv_b", fc(i["lru_conv_b"]))
    put("lru_b_a", fc(i["lru_b_a"]))
    put("lru_b_i", fc(i["lru_b_i"]))
    put("lru_lambda", fc(i["lru_lambda"]))
    put("norm_ffn", fc(i["norm_ffn"]))
    put("ffn_conv_w", fc(i["ffn_conv_w"]))
    put("ffn_conv_b", fc(i["ffn_conv_b"]))
    put("norm_final", fc(i["norm_final"]))
    put("final_g", fc(i["final_g_2"]))
    put("cond", np.stack([fc(i["c_ctx_2"]), fc(i["c_2"])], 2))
    put("dt_bias", i["ssd_dt_bias"].T)
    put("a_log", i["ssd_a_log"].T)
    w = i["w_in"][0]
    o = np.cumsum([0, D, D + 512, SSD_H, D, D, 512, 512, D, D, 3 * D])
    part = [w[:, a:b] for a, b in zip(o[:-1], o[1:])]
    dt = z((D, P), np.float32)
    dt[:, :SSD_H] = part[2]
    d = {"x": streams_layout(i["ctx_2"][0], i["x"][0])}
    d["w_in1"] = blocks(np.concatenate([dt] + [part[k] for k in (1, 4, 5, 6, 7, 0, 8, 3, 9)], 1))
    lru = [i[n][0].reshape(4, 2, P, 2, P).transpose(2, 0, 3, 1, 4).reshape(P, 2, D).transpose(1, 0, 2)
           for n in ("lru_w_a", "lru_w_i")]
    d["w_lru"] = np.ascontiguousarray(np.stack(lru, 1).reshape(4, P, D))
    d["w_br"] = np.concatenate([blocks(i["w_branch"][0, k]) for k in (2, 1, 0)])
    d["w_o1"] = blocks(i["w_o"][0])
    a, u = blocks(i["ffn_w_in"][0][:, :3 * D]), blocks(i["ffn_w_in"][0][:, 3 * D:])
    d["w_f1"] = np.ascontiguousarray(np.stack([a, u], 1).reshape(48, P, D))
    d["w_f2"] = blocks(i["ffn_w_out"][0])
    for l in range(LAYERS):
        put(f"ada_b{l}", fc(i["ada_b_2"][l]))
        put(f"norm1{l}", fc(i["norm1_g_2"][l]))
        put(f"norm2{l}", fc(i["norm2_g_2"][l]))
        put(f"conv_w{l}", fc(i["conv_w_2"][l]))
        put(f"conv_b{l}", fc(i["conv_b_2"][l]))
        put(f"ln_g{l}", fc(i["conv_ln_g_2"][l]))
        put(f"ln_b{l}", fc(i["conv_ln_b_2"][l]))
        gb = z((P, 1), np.float32)
        g = i["mlstm_gate_b_2"][l]
        gw = z((D, P), np.float32)
        mg = i["w_in_2"][l][:, 1536:1552]
        for row, k in ((0, 0), (64, 1), (32, 2), (96, 3)):
            gb[row:row + 4, 0] = g[k]
            gw[:, row:row + 4] = mg[:, 4 * k:4 * k + 4]
        put(f"gate_b{l}", gb)
        put(f"ml_norm{l}", fc(np.tile(i["mlstm_norm_g_2"][l], 2)))
        put(f"df_norm{l}", fc(i["diff_norm_g_2"][l]))
        put(f"lam{l}", np.broadcast_to(i["diff_lambda_2"][l].reshape(1, 256), (P, 256)))
        d[f"ada{l}"] = row_blocks(i["ada_w_2"][l])
        w = i["w_in_2"][l]
        order = [w[:, 256:512], w[:, 0:256], w[:, 1280:1536], w[:, 512:1280], w[:, 1552:3088]]
        d[f"w_in2_{l}"] = blocks(np.concatenate([gw] + order, 1))
        d[f"w_out2_{l}"] = blocks(i["w_out_2"][l])
        d[f"w_q2_{l}"] = blocks(i["peer_wq_2"][l])
        d[f"keys2_{l}"] = np.ascontiguousarray(i["peer_keys_2"][l].transpose(1, 3, 0, 2).reshape(P, PEER_H * NK))
        U = i["peer_u_2"][l].reshape(NK, NK, KT, P).transpose(1, 3, 2, 0).reshape(NK, P, D)
        V = i["peer_v_2"][l].reshape(NK, NK, D).transpose(1, 0, 2)
        uv = np.empty((2 * NK, P, D), np.float32)
        uv[0] = U[0]
        uv[1:-1:2] = U[1:]
        uv[2::2] = V[:-1]
        uv[-1] = V[-1]
        d[f"uv{l}"] = uv
    d["smalls"] = sm
    d.update(shape_tables())
    return d


def kernel(**inputs):
    import concourse.bacc as bacc
    from concourse.bass_utils import run_bass_kernel_spmd

    nc = bacc.Bacc("TRN2", target_bir_lowering=False, num_devices=1)
    arrays = lay_out({n: np.asarray(a) for n, a in inputs.items()})
    ap = {name: nc.dram_tensor("in_" + name, a.shape, mybir.dt.from_np(a.dtype), kind="ExternalInput").ap()
          for name, a in arrays.items()}
    out = nc.dram_tensor("out_0", (P, KT, T), F32, kind="ExternalOutput").ap()
    pair = lambda n: [ap[f"{n}{l}"] for l in range(LAYERS)]
    build(nc, ap["x"], ap["smalls"], ap["consts"], ap["mix_tables"], ap["tables"], ap["axial"], ap["w_in1"], ap["w_lru"], ap["w_br"],
          ap["w_o1"], ap["w_f1"], ap["w_f2"], pair("ada"), pair("w_in2_"), pair("w_out2_"), pair("w_q2_"),
          pair("keys2_"), pair("uv"), out)
    r = run_bass_kernel_spmd(nc, [{"in_" + n: a for n, a in arrays.items()}], core_ids=[0])
    return r.results[0]["out_0"].transpose(2, 1, 0).reshape(1, T, D)
```
